# Optimizing a Trainium2 kernel written in Bass

```python
import jax, jax.numpy as jnp
from jax import lax
import numpy as np

D_MODEL = 1024
BATCH = 1
SEQ = 256
DEPTH = 2

N_MIXERS = 2
HEAD_DIM = 64
N_Q_HEADS = D_MODEL // HEAD_DIM
N_KV_HEADS = N_Q_HEADS // 4
GQA_GROUP = N_Q_HEADS // N_KV_HEADS
WINDOW = 128
BLOCK = 128
ROT_DIM = HEAD_DIM // 4
ROPE_THETA = 500000.0
LRU_WIDTH = D_MODEL
LRU_BLOCKS = 4
LRU_BLOCK_W = LRU_WIDTH // LRU_BLOCKS
CONV_WIDTH = 4
CONV_LEFT = 2
LRU_C = 8.0
N_EXPERTS = 16
EXPERT_FF = D_MODEL
CAPACITY_FACTOR = 2
LN_EPS = 1e-5
ALPHA = (2 * DEPTH) ** 0.25
BETA = (8 * DEPTH) ** -0.25
N_ATTN_LAYERS = (DEPTH + 1) // 2
N_LRU_LAYERS = DEPTH // 2


def layer_norm(x, g, b):
    xf = x.astype(jnp.float32)
    mu = jnp.mean(xf, axis=-1, keepdims=True)
    var = jnp.mean(jnp.square(xf - mu), axis=-1, keepdims=True)
    y = (xf - mu) * lax.rsqrt(var + LN_EPS) * g.astype(jnp.float32) + b.astype(jnp.float32)
    return y.astype(x.dtype)

def partial_rotary(t, cos, sin):
    tr, tp = t[..., :ROT_DIM], t[..., ROT_DIM:]
    t1, t2 = tr[..., :ROT_DIM // 2], tr[..., ROT_DIM // 2:]
    rot = jnp.concatenate([-t2, t1], axis=-1)
    return jnp.concatenate([tr * cos + rot * sin, tp], axis=-1)

def windowed_gqa_sink(x, w_qkv, w_o, sink):
    B, S, _ = x.shape
    nb = S // BLOCK
    qkv = x @ w_qkv
    q, k, v = jnp.split(qkv, [N_Q_HEADS * HEAD_DIM, (N_Q_HEADS + N_KV_HEADS) * HEAD_DIM], axis=-1)
    q = q.reshape(B, S, N_KV_HEADS, GQA_GROUP, HEAD_DIM)
    k = k.reshape(B, S, N_KV_HEADS, HEAD_DIM)
    v = v.reshape(B, S, N_KV_HEADS, HEAD_DIM)
    pos = jnp.arange(S, dtype=jnp.float32)
    inv_freq = ROPE_THETA ** (-jnp.arange(0, ROT_DIM, 2, dtype=jnp.float32) / ROT_DIM)
    ang = pos[:, None] * inv_freq[None, :]
    ang = jnp.concatenate([ang, ang], axis=-1)
    cos, sin = jnp.cos(ang).astype(x.dtype), jnp.sin(ang).astype(x.dtype)
    q = partial_rotary(q, cos[None, :, None, None, :], sin[None, :, None, None, :])
    k = partial_rotary(k, cos[None, :, None, :], sin[None, :, None, :])

    pad = ((0, 0), (BLOCK, BLOCK), (0, 0), (0, 0))
    kb = jnp.pad(k, pad).reshape(B, nb + 2, BLOCK, N_KV_HEADS, HEAD_DIM)
    vb = jnp.pad(v, pad).reshape(B, nb + 2, BLOCK, N_KV_HEADS, HEAD_DIM)
    k_band = jnp.concatenate([kb[:, :-2], kb[:, 1:-1], kb[:, 2:]], axis=2)
    v_band = jnp.concatenate([vb[:, :-2], vb[:, 1:-1], vb[:, 2:]], axis=2)
    qb = q.reshape(B, nb, BLOCK, N_KV_HEADS, GQA_GROUP, HEAD_DIM)

    s = jnp.einsum('bnqhgd,bnkhd->bnhgqk', qb, k_band).astype(jnp.float32) * (HEAD_DIM ** -0.5)
    blk = jnp.arange(nb)
    qpos = blk[:, None] * BLOCK + jnp.arange(BLOCK)[None, :]
    kpos = (blk[:, None] - 1) * BLOCK + jnp.arange(3 * BLOCK)[None, :]
    valid = ((jnp.abs(qpos[:, :, None] - kpos[:, None, :]) <= WINDOW)
             & (kpos[:, None, :] >= 0) & (kpos[:, None, :] < S))
    s = jnp.where(valid[None, :, None, None], s, -jnp.inf)
    sink_l = sink.astype(jnp.float32).reshape(N_KV_HEADS, GQA_GROUP)[None, None, :, :, None, None]
    m = jnp.maximum(jnp.max(s, axis=-1, keepdims=True), sink_l)
    p = jnp.exp(s - m)
    denom = jnp.sum(p, axis=-1, keepdims=True) + jnp.exp(sink_l - m)
    probs = (p / denom).astype(x.dtype)
    o = jnp.einsum('bnhgqk,bnkhd->bnqhgd', probs, v_band).reshape(B, S, D_MODEL)
    return o @ w_o

def _linear_combine(left, right):
    a1, b1 = left
    a2, b2 = right
    return a1 * a2, a2 * b1 + b2

def bidir_rglru_block(x, w_in, conv_w, conv_b, w_rgate, b_rgate, w_igate, b_igate, lam, w_out):
    B, S, _ = x.shape
    gate_br, xb = jnp.split(x @ w_in, 2, axis=-1)
    xp = jnp.pad(xb, ((0, 0), (CONV_LEFT, CONV_WIDTH - 1 - CONV_LEFT), (0, 0)))
    xc = conv_b
    for j in range(CONV_WIDTH):
        xc = xc + conv_w[j] * xp[:, j:j + S]
    xr = xc.reshape(B, S, LRU_BLOCKS, LRU_BLOCK_W)
    r = jax.nn.sigmoid(jnp.einsum('bsnc,zncf->zbsnf', xr, w_rgate).reshape(2, B, S, LRU_WIDTH).astype(jnp.float32)
                       + b_rgate.astype(jnp.float32)[:, None, None, :])
    i = jax.nn.sigmoid(jnp.einsum('bsnc,zncf->zbsnf', xr, w_igate).reshape(2, B, S, LRU_WIDTH).astype(jnp.float32)
                       + b_igate.astype(jnp.float32)[:, None, None, :])
    log_a = -LRU_C * r * jax.nn.softplus(-lam.astype(jnp.float32))[:, None, None, :]
    a = jnp.exp(log_a)
    mult = jnp.sqrt(-jnp.expm1(2.0 * log_a))
    t = jnp.arange(S)
    is_start = jnp.stack([t == 0, t == S - 1])
    mult = jnp.where(is_start[:, None, :, None], 1.0, mult)
    u = mult * i * xc.astype(jnp.float32)[None]
    _, h_f = lax.associative_scan(_linear_combine, (a[0], u[0]), axis=1)
    _, h_b = lax.associative_scan(_linear_combine, (a[1], u[1]), reverse=True, axis=1)
    h = (h_f + h_b).astype(x.dtype)
    return (h * jax.nn.gelu(gate_br)) @ w_out

def expert_choice_moe(x, w_router, w_gate_up, w_down):
    B, S, _ = x.shape
    cap = CAPACITY_FACTOR * S // N_EXPERTS
    aff = jax.nn.softmax((x @ w_router).astype(jnp.float32), axis=-1)
    gates, idx = lax.top_k(jnp.swapaxes(aff, 1, 2), cap)
    bi = jnp.arange(B)[:, None, None]
    xs = x[bi, idx]
    g, u = jnp.split(jnp.einsum('becd,edf->becf', xs, w_gate_up), 2, axis=-1)
    out = jnp.einsum('becf,efd->becd', jax.nn.silu(g) * u, w_down) * gates[..., None].astype(x.dtype)
    return jnp.zeros_like(x).at[bi, idx].add(out)

def first_inputs(seed: int = 0) -> dict:
    key = jax.random.key(seed)
    ks = jax.random.split(key, 24)
    f32 = jnp.float32
    nrm = lambda k, shape, scale: jax.random.normal(k, shape, f32) * scale
    qkv_out = (N_Q_HEADS + 2 * N_KV_HEADS) * HEAD_DIM
    a8 = jax.random.uniform(ks[11], (N_LRU_LAYERS, 2, LRU_WIDTH), f32, 0.9, 0.999)
    a_base = a8 ** (1.0 / LRU_C)
    lam = jnp.log(a_base) - jnp.log1p(-a_base)
    return {
        'x': jax.random.normal(ks[0], (BATCH, SEQ, D_MODEL), f32),
        'attn_w_qkv': nrm(ks[1], (N_ATTN_LAYERS, D_MODEL, qkv_out), D_MODEL ** -0.5),
        'attn_w_o': nrm(ks[2], (N_ATTN_LAYERS, D_MODEL, D_MODEL), BETA * D_MODEL ** -0.5),
        'attn_sink': nrm(ks[3], (N_ATTN_LAYERS, N_Q_HEADS), 0.5),
        'lru_w_in': nrm(ks[4], (N_LRU_LAYERS, D_MODEL, 2 * LRU_WIDTH), D_MODEL ** -0.5),
        'lru_conv_w': nrm(ks[5], (N_LRU_LAYERS, CONV_WIDTH, LRU_WIDTH), CONV_WIDTH ** -0.5),
        'lru_conv_b': nrm(ks[6], (N_LRU_LAYERS, LRU_WIDTH), 0.02),
        'lru_w_rgate': nrm(ks[7], (N_LRU_LAYERS, 2, LRU_BLOCKS, LRU_BLOCK_W, LRU_BLOCK_W), LRU_BLOCK_W ** -0.5),
        'lru_b_rgate': nrm(ks[8], (N_LRU_LAYERS, 2, LRU_WIDTH), 0.02),
        'lru_w_igate': nrm(ks[9], (N_LRU_LAYERS, 2, LRU_BLOCKS, LRU_BLOCK_W, LRU_BLOCK_W), LRU_BLOCK_W ** -0.5),
        'lru_b_igate': nrm(ks[10], (N_LRU_LAYERS, 2, LRU_WIDTH), 0.02),
        'lru_lambda': lam,
        'lru_w_out': nrm(ks[12], (N_LRU_LAYERS, LRU_WIDTH, D_MODEL), BETA * LRU_WIDTH ** -0.5),
        'moe_w_router': nrm(ks[13], (DEPTH, D_MODEL, N_EXPERTS), D_MODEL ** -0.5),
        'moe_w_gate_up': nrm(ks[14], (DEPTH, N_EXPERTS, D_MODEL, 2 * EXPERT_FF), D_MODEL ** -0.5),
        'moe_w_down': nrm(ks[15], (DEPTH, N_EXPERTS, EXPERT_FF, D_MODEL), BETA * EXPERT_FF ** -0.5),
        'ln_mix_g': 1.0 + nrm(ks[16], (DEPTH, D_MODEL), 0.02),
        'ln_mix_b': nrm(ks[17], (DEPTH, D_MODEL), 0.02),
        'ln_ffn_g': 1.0 + nrm(ks[18], (DEPTH, D_MODEL), 0.02),
        'ln_ffn_b': nrm(ks[19], (DEPTH, D_MODEL), 0.02),
    }

def first_block(x, attn_w_qkv, attn_w_o, attn_sink, lru_w_in, lru_conv_w, lru_conv_b,
              lru_w_rgate, lru_b_rgate, lru_w_igate, lru_b_igate, lru_lambda, lru_w_out,
              moe_w_router, moe_w_gate_up, moe_w_down, ln_mix_g, ln_mix_b, ln_ffn_g, ln_ffn_b):
    for layer in range(DEPTH):
        j = layer // N_MIXERS
        if layer % N_MIXERS == 0:
            mix = windowed_gqa_sink(x, attn_w_qkv[j], attn_w_o[j], attn_sink[j])
        else:
            mix = bidir_rglru_block(x, lru_w_in[j], lru_conv_w[j], lru_conv_b[j],
                                    lru_w_rgate[j], lru_b_rgate[j], lru_w_igate[j], lru_b_igate[j],
                                    lru_lambda[j], lru_w_out[j])
        x = layer_norm(ALPHA * x + mix, ln_mix_g[layer], ln_mix_b[layer])
        ffn = expert_choice_moe(x, moe_w_router[layer], moe_w_gate_up[layer], moe_w_down[layer])
        x = layer_norm(ALPHA * x + ffn, ln_ffn_g[layer], ln_ffn_b[layer])
    return x


GRID_W = 64
CTX_LEN = 256

DEEPNORM_ALPHA = (2 * DEPTH) ** 0.25
DEEPNORM_BETA = (8 * DEPTH) ** -0.25
LN_EPS_2 = 1e-6

N_EVEN = (DEPTH + 1) // 2
N_ODD = DEPTH // 2

GLA_HEADS = 4
GLA_DK = 64
GLA_DV = 128
GLA_QK_W = GLA_HEADS * GLA_DK
GLA_V_W = GLA_HEADS * GLA_DV
GLA_GATE_RANK = 16
GLA_TAU = 16.0
GLA_CHUNK = 64

MLA_HEADS = 8
MLA_NOPE = 64
MLA_ROPE = 32
MLA_V = 64
MLA_Q_RANK = 256
MLA_KV_RANK = 128
MLA_V_W = MLA_HEADS * MLA_V
MLA_SCALE = (MLA_NOPE + MLA_ROPE) ** -0.5
ROPE_BASE = 10000.0
Q_BLOCK = 128

FNET_GROUPS = 4
FNET_GROUP_CH = 128
FNET_W = FNET_GROUPS * FNET_GROUP_CH

SGU_GROUPS = 4
SGU_GROUP_CH = 128
SGU_W = SGU_GROUPS * SGU_GROUP_CH
SGU_CHUNK = 128

EVEN_IN_SIZES = (GLA_QK_W, GLA_QK_W, GLA_V_W, 2 * GLA_GATE_RANK, GLA_V_W,
                 MLA_Q_RANK, MLA_KV_RANK, MLA_ROPE, MLA_V_W)
ODD_IN_SIZES = (FNET_W, FNET_W, SGU_W, SGU_W, SGU_W)
EVEN_OUT_IN = GLA_V_W + MLA_V_W
ODD_OUT_IN = FNET_W + SGU_W


def split_cols(z, sizes):
    idx = np.cumsum(sizes)[:-1].tolist()
    return jnp.split(z, idx, axis=-1)

def layer_norm_2(x, g=None, b=None):
    xf = x.astype(jnp.float32)
    xc = xf - jnp.mean(xf, -1, keepdims=True)
    y = xc * lax.rsqrt(jnp.mean(xc * xc, -1, keepdims=True) + LN_EPS_2)
    if g is not None:
        y = y * g.astype(jnp.float32) + b.astype(jnp.float32)
    return y.astype(x.dtype)

def rms_norm(x, g):
    xf = x.astype(jnp.float32)
    y = xf * lax.rsqrt(jnp.mean(xf * xf, -1, keepdims=True) + LN_EPS_2)
    return (y * g.astype(jnp.float32)).astype(x.dtype)

def ada_mod(cond, w, b):
    m = jnp.dot(jax.nn.silu(cond), w) + b
    return jnp.split(m, 3, axis=-1)

def modulate(x, shift, scale):
    return layer_norm_2(x) * (1 + scale[..., None, :]) + shift[..., None, :]

def axial_rope_angles(n):
    rows = n // GRID_W
    row = jnp.repeat(jnp.arange(rows, dtype=jnp.float32), GRID_W)
    col = (jnp.arange(n) % GRID_W).astype(jnp.float32)
    n_freq = MLA_ROPE // 4
    inv = ROPE_BASE ** (-jnp.arange(n_freq, dtype=jnp.float32) / n_freq)
    ang = jnp.concatenate([row[:, None] * inv, col[:, None] * inv], -1)
    return jnp.cos(ang), jnp.sin(ang)

def apply_rope(x, cos, sin):
    xf = x.astype(jnp.float32)
    x1, x2 = jnp.split(xf, 2, axis=-1)
    return jnp.concatenate([x1 * cos - x2 * sin, x1 * sin + x2 * cos], -1).astype(x.dtype)

def gla_q(q):
    B, n, _ = q.shape
    return q.astype(jnp.float32).reshape(B, n, GLA_HEADS, GLA_DK) * GLA_DK ** -0.5

def gla_kvg(k, v, lr, w2, b):
    B, n, _ = k.shape
    heads = lambda a, d: a.astype(jnp.float32).reshape(B, n, GLA_HEADS, d)
    lr_dirs = jnp.split(lr.astype(jnp.float32), 2, axis=-1)
    g = tuple(
        heads(jax.nn.log_sigmoid(jnp.einsum('bnr,re->bne', lr_dirs[d], w2[d].astype(jnp.float32))
                                 + b[d].astype(jnp.float32)) / GLA_TAU, GLA_DK)
        for d in range(2))
    return heads(k, GLA_DK), heads(v, GLA_DV), g

def gla_chunk_scan(q, k, v, g, s0):
    B, n, H, _ = q.shape
    nc = n // GLA_CHUNK
    chunk = lambda a: a.reshape(B, nc, GLA_CHUNK, H, a.shape[-1])
    q, k, v, g = chunk(q), chunk(k), chunk(v), chunk(g)
    b = jnp.cumsum(g, axis=2)
    b_mid = b[:, :, GLA_CHUNK // 2 - 1:GLA_CHUNK // 2]
    b_end = b[:, :, -1:]
    att = jnp.einsum('bcthk,bcshk->bchts', q * jnp.exp(b - b_mid), k * jnp.exp(b_mid - b))
    tri = jnp.tril(jnp.ones((GLA_CHUNK, GLA_CHUNK), dtype=bool))
    o = jnp.einsum('bchts,bcshv->bcthv', jnp.where(tri, att, 0.0), v)
    ds = jnp.einsum('bcshk,bcshv->bchkv', k * jnp.exp(b_end - b), v)
    decay = jnp.exp(b_end[:, :, 0])

    def step(s, inp):
        d, dsc = inp
        return d[..., None] * s + dsc, s

    s_last, s_start = lax.scan(step, s0, (jnp.moveaxis(decay, 1, 0), jnp.moveaxis(ds, 1, 0)))
    o = o + jnp.einsum('bcthk,cbhkv->bcthv', q * jnp.exp(b), s_start)
    return o.reshape(B, n, H, v.shape[-1]), s_last

def gla_final_state(k, v, g):
    bc = jnp.cumsum(g, axis=1)
    return jnp.einsum('bshk,bshv->bhkv', k * jnp.exp(bc[:, -1:] - bc), v)

def gla_bidir(q_l, k_l, v_l, g_l, k_c, v_c, g_c, q_c):
    B, _, H, _ = k_c.shape
    ident = lambda a: a
    rev = lambda a: a[:, ::-1]
    o_l, o_c = 0.0, 0.0
    for d, order in ((0, ident), (1, rev)):
        if q_c is None:
            s_c = gla_final_state(order(k_c), order(v_c), order(g_c[d]))
        else:
            s0 = jnp.zeros((B, H, GLA_DK, GLA_DV), jnp.float32)
            oc, s_c = gla_chunk_scan(order(q_c), order(k_c), order(v_c), order(g_c[d]), s0)
            o_c = o_c + order(oc)
        ol, _ = gla_chunk_scan(order(q_l), order(k_l), order(v_l), order(g_l[d]), s_c)
        o_l = o_l + order(ol)
    return o_l, (o_c if q_c is not None else None)

def mla_q(cq, q_norm_g, w_uq, rope):
    B, n, _ = cq.shape
    q = jnp.einsum('bnr,re->bne', rms_norm(cq, q_norm_g), w_uq).reshape(B, n, MLA_HEADS, MLA_NOPE + MLA_ROPE)
    q_nope, q_rope = q[..., :MLA_NOPE], q[..., MLA_NOPE:]
    if rope is not None:
        q_rope = apply_rope(q_rope, rope[0][:, None, :], rope[1][:, None, :])
    return q_nope, q_rope

def mla_kv(ckv, kr, kv_norm_g, w_ukv, rope):
    B, n, _ = ckv.shape
    kv = jnp.einsum('bnr,re->bne', rms_norm(ckv, kv_norm_g), w_ukv).reshape(B, n, MLA_HEADS, MLA_NOPE + MLA_V)
    if rope is not None:
        kr = apply_rope(kr, rope[0], rope[1])
    return kv[..., :MLA_NOPE], kr, kv[..., MLA_NOPE:]

def mla_attend(q_nope, q_rope, k_nope, k_rope, v):
    s = (jnp.einsum('bqhd,bkhd->bhqk', q_nope, k_nope, preferred_element_type=jnp.float32)
         + jnp.einsum('bqhr,bkr->bhqk', q_rope, k_rope, preferred_element_type=jnp.float32)) * MLA_SCALE
    p = jax.nn.softmax(s, axis=-1).astype(v.dtype)
    return jnp.einsum('bhqk,bkhd->bqhd', p, v)

def mla_latent_blocks(q_nope, q_rope, k_nope, k_rope, v):
    B, n = q_nope.shape[:2]
    nb = n // Q_BLOCK
    blocks = lambda a: jnp.moveaxis(a.reshape(B, nb, Q_BLOCK, *a.shape[2:]), 1, 0)
    o = lax.map(lambda qs: mla_attend(qs[0], qs[1], k_nope, k_rope, v), (blocks(q_nope), blocks(q_rope)))
    return jnp.moveaxis(o, 0, 1).reshape(B, n, MLA_V_W)

def even_mixer(h_lat, h_ctx, need_ctx_out, rope, w_in, gla_w2, gla_b, gla_norm_g,
               q_norm_g, w_uq, kv_norm_g, w_ukv, w_out):
    B, n, _ = h_lat.shape
    L = h_ctx.shape[1]
    proj = lambda h: split_cols(jnp.einsum('bnd,de->bne', h, w_in), EVEN_IN_SIZES)
    gq_l, gk_l, gv_l, glr_l, gg_l, cq_l, ckv_l, kr_l, mg_l = proj(h_lat)
    gq_c, gk_c, gv_c, glr_c, gg_c, cq_c, ckv_c, kr_c, mg_c = proj(h_ctx)

    k_l, v_l, g_l = gla_kvg(gk_l, gv_l, glr_l, gla_w2, gla_b)
    k_c, v_c, g_c = gla_kvg(gk_c, gv_c, glr_c, gla_w2, gla_b)
    o_gl, o_gc = gla_bidir(gla_q(gq_l), k_l, v_l, g_l, k_c, v_c, g_c,
                           gla_q(gq_c) if need_ctx_out else None)
    y_gla = rms_norm(o_gl, gla_norm_g).reshape(B, n, GLA_V_W).astype(h_lat.dtype) * jax.nn.silu(gg_l)

    kn_c, krot_c, vm_c = mla_kv(ckv_c, kr_c, kv_norm_g, w_ukv, None)
    kn_l, krot_l, vm_l = mla_kv(ckv_l, kr_l, kv_norm_g, w_ukv, rope)
    qn_l, qr_l = mla_q(cq_l, q_norm_g, w_uq, rope)
    o_ml = mla_latent_blocks(qn_l, qr_l,
                             jnp.concatenate([kn_c, kn_l], 1),
                             jnp.concatenate([krot_c, krot_l], 1),
                             jnp.concatenate([vm_c, vm_l], 1))
    y_mla = o_ml * jax.nn.silu(mg_l)
    y_lat = jnp.einsum('bne,ed->bnd', jnp.concatenate([y_gla, y_mla], -1), w_out)

    y_ctx = None
    if need_ctx_out:
        yg_c = rms_norm(o_gc, gla_norm_g).reshape(B, L, GLA_V_W).astype(h_ctx.dtype) * jax.nn.silu(gg_c)
        qn_c, qr_c = mla_q(cq_c, q_norm_g, w_uq, None)
        ym_c = mla_attend(qn_c, qr_c, kn_c, krot_c, vm_c).reshape(B, L, MLA_V_W) * jax.nn.silu(mg_c)
        y_ctx = jnp.einsum('bne,ed->bnd', jnp.concatenate([yg_c, ym_c], -1), w_out)
    return y_lat, y_ctx

def odd_mixer(h, w_in, sgu_w, sgu_b, w_out):
    B, n, _ = h.shape
    f, f_gate, u, v, s_gate = split_cols(jnp.einsum('bnd,de->bne', h, w_in), ODD_IN_SIZES)
    fg = f.astype(jnp.float32).reshape(B, n, FNET_GROUPS, FNET_GROUP_CH)
    fr = jnp.fft.fft2(fg, axes=(1, 3), norm='ortho').real.reshape(B, n, FNET_W).astype(h.dtype)
    y_f = fr * jax.nn.silu(f_gate)
    u = jax.nn.gelu(u, approximate=False)
    vg = layer_norm_2(jax.nn.gelu(v, approximate=False).reshape(B, n // SGU_CHUNK, SGU_CHUNK, SGU_GROUPS, SGU_GROUP_CH))
    sv = jnp.einsum('gts,bcsgd->bctgd', sgu_w, vg) + sgu_b.T[:, :, None]
    y_s = u * sv.reshape(B, n, SGU_W) * jax.nn.silu(s_gate)
    return jnp.einsum('bne,ed->bnd', jnp.concatenate([y_f, y_s], -1), w_out)

def second_inputs(seed: int = 0) -> dict:
    key = jax.random.key(seed)
    ks = iter(jax.random.split(key, 24))
    nrm = lambda shape, scale: jax.random.normal(next(ks), shape, jnp.float32) * scale
    D = D_MODEL
    return {
        "x": nrm((BATCH, SEQ, D), 1.0),
        "c": nrm((BATCH, D), 1.0),
        "ctx": nrm((BATCH, CTX_LEN, D), 1.0),
        "c_ctx": nrm((D,), 1.0),
        "ada_w": nrm((DEPTH, D, 3 * D), D ** -0.5),
        "ada_b": nrm((DEPTH, 3 * D), 0.02),
        "post_ln_g": 1.0 + nrm((DEPTH, D), 0.02),
        "post_ln_b": nrm((DEPTH, D), 0.02),
        "even_w_in": nrm((N_EVEN, D, sum(EVEN_IN_SIZES)), D ** -0.5),
        "gla_w2": nrm((N_EVEN, 2, GLA_GATE_RANK, GLA_QK_W), GLA_GATE_RANK ** -0.5),
        "gla_b": nrm((N_EVEN, 2, GLA_QK_W), 0.1),
        "gla_norm_g": 1.0 + nrm((N_EVEN, GLA_DV), 0.02),
        "mla_q_norm_g": 1.0 + nrm((N_EVEN, MLA_Q_RANK), 0.02),
        "mla_w_uq": nrm((N_EVEN, MLA_Q_RANK, MLA_HEADS * (MLA_NOPE + MLA_ROPE)), MLA_Q_RANK ** -0.5),
        "mla_kv_norm_g": 1.0 + nrm((N_EVEN, MLA_KV_RANK), 0.02),
        "mla_w_ukv": nrm((N_EVEN, MLA_KV_RANK, MLA_HEADS * (MLA_NOPE + MLA_V)), MLA_KV_RANK ** -0.5),
        "even_w_out": nrm((N_EVEN, EVEN_OUT_IN, D), EVEN_OUT_IN ** -0.5 * DEEPNORM_BETA),
        "odd_w_in": nrm((N_ODD, D, sum(ODD_IN_SIZES)), D ** -0.5),
        "sgu_w": nrm((N_ODD, SGU_GROUPS, SGU_CHUNK, SGU_CHUNK), SGU_CHUNK ** -0.5),
        "sgu_b": 1.0 + nrm((N_ODD, SGU_GROUPS, SGU_CHUNK), 0.1),
        "odd_w_out": nrm((N_ODD, ODD_OUT_IN, D), ODD_OUT_IN ** -0.5 * DEEPNORM_BETA),
    }

def second_block(x, c, ctx, c_ctx, ada_w, ada_b, post_ln_g, post_ln_b, even_w_in, gla_w2, gla_b, gla_norm_g,
              mla_q_norm_g, mla_w_uq, mla_kv_norm_g, mla_w_ukv, even_w_out, odd_w_in, sgu_w, sgu_b, odd_w_out):
    rope = axial_rope_angles(x.shape[1])
    for l in range(DEPTH):
        need_ctx_out = any(j % 2 == 0 for j in range(l + 1, DEPTH))
        i = l // 2
        shift, scale, gate = ada_mod(c, ada_w[l], ada_b[l])
        h_lat = modulate(x, shift, scale)
        if l % 2 == 0 or need_ctx_out:
            shift_c, scale_c, gate_c = ada_mod(c_ctx, ada_w[l], ada_b[l])
            h_ctx = modulate(ctx, shift_c, scale_c)
        if l % 2 == 0:
            y_lat, y_ctx = even_mixer(h_lat, h_ctx, need_ctx_out, rope, even_w_in[i], gla_w2[i], gla_b[i],
                                      gla_norm_g[i], mla_q_norm_g[i], mla_w_uq[i], mla_kv_norm_g[i],
                                      mla_w_ukv[i], even_w_out[i])
        else:
            y_lat = odd_mixer(h_lat, odd_w_in[i], sgu_w[i], sgu_b[i], odd_w_out[i])
            y_ctx = odd_mixer(h_ctx, odd_w_in[i], sgu_w[i], sgu_b[i], odd_w_out[i]) if need_ctx_out else None
        x = layer_norm_2(DEEPNORM_ALPHA * x + gate[:, None, :] * y_lat, post_ln_g[l], post_ln_b[l])
        if need_ctx_out:
            ctx = layer_norm_2(DEEPNORM_ALPHA * ctx + gate_c[None, :] * y_ctx, post_ln_g[l], post_ln_b[l])
    return x


def setup_inputs(seed=0):
    out = dict(first_inputs(seed))
    for name, value in second_inputs(seed + 1).items():
        if name != "x":
            out[name + "_2"] = value
    return out


def reference(
    x, attn_w_qkv, attn_w_o, attn_sink, lru_w_in, lru_conv_w, lru_conv_b, lru_w_rgate,
    lru_b_rgate, lru_w_igate, lru_b_igate, lru_lambda, lru_w_out, moe_w_router, moe_w_gate_up,
    moe_w_down, ln_mix_g, ln_mix_b, ln_ffn_g, ln_ffn_b, c_2, ctx_2, c_ctx_2, ada_w_2, ada_b_2,
    post_ln_g_2, post_ln_b_2, even_w_in_2, gla_w2_2, gla_b_2, gla_norm_g_2, mla_q_norm_g_2,
    mla_w_uq_2, mla_kv_norm_g_2, mla_w_ukv_2, even_w_out_2, odd_w_in_2, sgu_w_2, sgu_b_2,
    odd_w_out_2,
):
    x = first_block(
        x, attn_w_qkv, attn_w_o, attn_sink, lru_w_in, lru_conv_w, lru_conv_b, lru_w_rgate,
        lru_b_rgate, lru_w_igate, lru_b_igate, lru_lambda, lru_w_out, moe_w_router,
        moe_w_gate_up, moe_w_down, ln_mix_g, ln_mix_b, ln_ffn_g, ln_ffn_b,
    )
    return second_block(
        x, c_2, ctx_2, c_ctx_2, ada_w_2, ada_b_2, post_ln_g_2, post_ln_b_2, even_w_in_2,
        gla_w2_2, gla_b_2, gla_norm_g_2, mla_q_norm_g_2, mla_w_uq_2, mla_kv_norm_g_2,
        mla_w_ukv_2, even_w_out_2, odd_w_in_2, sgu_w_2, sgu_b_2, odd_w_out_2,
    )


_drawn_inputs = setup_inputs


def setup_inputs(seed=0):
    import zlib

    import numpy as np

    out = dict(_drawn_inputs(seed))
    spreads = {}
    factors = {'attn_sink': 8.0,
     'lru_b_rgate': 8.0,
     'lru_b_igate': 8.0,
     'ctx_2': 3.227,
     'ada_b_2': 4.372,
     'gla_b_2': 7.516,
     'gla_norm_g_2': 8.0,
     'mla_q_norm_g_2': 8.0,
     'mla_w_uq_2': 3.756,
     'mla_kv_norm_g_2': 8.0,
     'sgu_b_2': 4.807}
    for name, (base, spread) in spreads.items():
        noise = np.random.default_rng([zlib.crc32(name.encode()), seed]).standard_normal(out[name].shape)
        drawn = base * np.exp(spread * noise) if base else spread * noise
        out[name] = __import__('jax').numpy.asarray(drawn.astype(out[name].dtype))
    for name, factor in factors.items():
        out[name] = (out[name] * factor).astype(out[name].dtype)
    return out
```

```python
from contextlib import ExitStack

import numpy as np

import concourse.bass as bass
from concourse import mybir

F32 = mybir.dt.float32
U32 = mybir.dt.uint32
ACT = mybir.ActivationFunctionType
ALU = mybir.AluOpType
AX = mybir.AxisListType

P = 128
D = 1024
S = 256
H = S // P
T = D // P
LN_CHUNK = 512
DEPTH = 2
ALPHA = (2 * DEPTH) ** 0.25
EPS_FIRST = 1e-5
EPS_SECOND = 1e-6
UNIT = 4096
SLOTS = 6

NQ, NKV, HD = 16, 4, 64
GROUP = NQ // NKV
ROT = HD // 4
WINDOW = 128
QKV = (NQ + 2 * NKV) * HD
NE = 16
CAP = 2 * S // NE
FF = 1024
PACK = P // CAP
LB = 4
LBW = D // LB
CW = 4
LRU_C = 8.0
GH, GK, GV, GR, GCH = 4, 64, 128, 16, 64
GTAU = 16.0
NCH = S // GCH
MH, MN, MR, MV = 8, 64, 32, 64
MQ = MN + MR
MSCALE = MQ ** -0.5
QR, KVR = 256, 128
C_GQ, C_GK, C_GV, C_LR, C_GG, C_CQ, C_CKV, C_KR, C_MG = 0, 256, 512, 1024, 1056, 1568, 1824, 1952, 1984
NEG = -1e30


def constants():
    p = np.arange(P)
    token = np.arange(H)[None, :] * P + p[:, None]
    key = np.arange(S)
    out = {"k_ident": np.eye(P, dtype=np.float32)}
    far = np.abs(token[:, :, None] - key[None, None, :]) > WINDOW
    out["k_window"] = np.where(far, np.float32(NEG), np.float32(0)).astype(np.float32)
    inv = np.float32(500000.0) ** (-np.arange(0, ROT, 2, dtype=np.float32) / np.float32(ROT))
    ang = token[:, :, None].astype(np.float32) * inv.astype(np.float32)
    out["k_rope"] = np.stack([np.cos(ang), np.sin(ang)], 2).astype(np.float32)
    out["k_slot"] = np.tile(np.arange(1, CAP + 1, dtype=np.float32), (P, 1))
    t = np.arange(S)
    out["k_reset"] = np.tile(np.stack([t % GCH != 0, t % GCH != GCH - 1]).astype(np.float32), (P, 1, 1))
    s_, t_ = np.arange(P)[:, None], np.arange(P)[None, :]
    same = (s_ // GCH) == (t_ // GCH)
    out["k_tri"] = np.stack([same & (s_ <= t_), same & (s_ >= t_)], 1).astype(np.uint32)
    n_freq = MR // 4
    inv = (np.float32(10000.0) ** (-np.arange(n_freq, dtype=np.float32) / np.float32(n_freq))).astype(np.float32)
    row, col = (token // 64).astype(np.float32), (token % 64).astype(np.float32)
    ang = np.concatenate([row[:, :, None] * inv, col[:, :, None] * inv], -1)
    out["k_axial"] = np.stack([np.cos(ang), np.sin(ang)], 2).astype(np.float32)
    a = 2 * np.pi * ((token[:, :, None] * t[None, None, :]) % S) / S
    out["k_dft_n"] = (np.stack([np.cos(a), np.sin(a)], 2) / np.sqrt(S)).astype(np.float32)
    c = 2 * np.pi * ((p[:, None] * p[None, :]) % P) / P
    out["k_dft_c"] = (np.concatenate([np.cos(c), -np.sin(c)], 1) / np.sqrt(P)).astype(np.float32)
    return out


class Queue:

    def __init__(self, engine, sem):
        self.engine, self.sem, self.count, self.seen = engine, sem, 0, {}

    def need(self, *marks):
        for m in marks:
            if m is None:
                continue
            if isinstance(m, list):
                self.need(*m)
                continue
            sem, value = m
            if value > self.seen.get(id(sem), 0):
                self.engine.wait_ge(sem, value)
                self.seen[id(sem)] = value

    def mark(self, instruction):
        instruction.then_inc(self.sem, 1)
        self.count += 1
        return (self.sem, self.count)

    def last(self):
        return (self.sem, self.count) if self.count else None


class Bank:

    def __init__(self, ap):
        self.ap, self.free = ap, []


class Banks:

    def __init__(self, banks):
        self.banks, self.at = banks, 0

    def take(self):
        self.at += 1
        return self.banks[(self.at - 1) % len(self.banks)]


class Unit:

    def __init__(self, ap):
        self.ap, self.arrived, self.free = ap, None, []


class Arena:

    def __init__(self, ap, size):
        self.ap, self.size, self.at = ap, size, 0

    def take(self, *dims):
        n = int(np.prod(dims))
        assert self.at + n <= self.size, ("arena", self.at + n, self.size)
        v = self.ap[:, self.at:self.at + n]
        self.at += n
        if len(dims) == 2:
            return v.rearrange("p (a b) -> p a b", a=dims[0])
        if len(dims) == 3:
            return v.rearrange("p (a b c) -> p a b c", a=dims[0], b=dims[1])
        return v


class Program:
    MAIN, SIDE = 17104, 4912

    def __init__(self, nc, ctx, dram, out):
        self.nc, self.ctx, self.d, self.out = nc, ctx, dram, out
        sem = lambda n: ctx.enter_context(nc.semaphore(n))
        self.new_sem = sem
        self.pe = Queue(nc.tensor, sem("tensor_steps"))
        self.v = Queue(nc.vector, sem("vector_steps"))
        self.a = Queue(nc.scalar, sem("scalar_steps"))
        self.g = Queue(nc.gpsimd, sem("gpsimd_steps"))
        self.sp = Queue(nc.sync, sem("sync_steps"))
        self.banks = [Bank(ctx.enter_context(nc.psum_tensor(f"bank{i}", [P, 512], F32))[:, :]) for i in range(8)]
        ring = ctx.enter_context(nc.sbuf_tensor("weight_ring", [P, SLOTS, UNIT], F32))
        self.slots = [Unit(ring[:, i, :]) for i in range(SLOTS)]
        self.slot_sem = [sem(f"slot{i}_filled") for i in range(SLOTS)]
        self.slot_fill = [0] * SLOTS
        self.unit_at = 0
        work = ctx.enter_context(nc.sbuf_tensor("work", [P, self.MAIN + self.SIDE], F32))
        self.main = Arena(work[:, 0:self.MAIN], self.MAIN)
        self.side = Arena(work[:, self.MAIN:], self.SIDE)
        self.whole = Arena(work[:, :], self.MAIN + self.SIDE)
        self.x = self.sb("x_tokens", [P, H, D])
        self.x_ready = []
        self.flip = 0
        self.one_shot = 0

    def sb(self, name, shape, dt=F32):
        t = self.ctx.enter_context(self.nc.sbuf_tensor(name, shape, dt))
        return t[tuple(slice(None) for _ in shape)]


    def load(self, queue, pairs, name):
        s = self.new_sem(name)
        for dst, src in pairs:
            queue.engine.dma_start(dst, src).then_inc(s, 16)
        return (s, 16 * len(pairs))

    def unit(self, parts):
        i = self.unit_at % SLOTS
        self.unit_at += 1
        slot = self.slots[i]
        self.sp.need(slot.free)
        for dst, src in parts(slot.ap):
            self.nc.sync.dma_start(dst, src).then_inc(self.slot_sem[i], 16)
            self.slot_fill[i] += 16
        slot.arrived = (self.slot_sem[i], self.slot_fill[i])
        return slot

    def columns_unit(self, w, c0, c, natural=False):
        src = w.rearrange("(t p) n -> p t n", p=P) if natural else w.rearrange("(p t) n -> p t n", t=T)
        box = []

        def parts(slot):
            view = slot[:, 0:T * c].rearrange("p (t c) -> p t c", t=T)
            box.append(view)
            return [(view, src[:, :, c0:c0 + c])]

        u = self.unit(parts)
        return u, box[0]

    def either(self):
        self.flip ^= 1
        return self.flip

    def copy(self, dst, src, *marks, on_scalar=None, scale=None):
        if self.either() if on_scalar is None else on_scalar:
            self.a.need(*marks)
            if scale is None:
                return self.a.mark(self.nc.scalar.copy(dst, src))
            return self.a.mark(self.nc.scalar.activation(dst, src, ACT.Identity, scale=scale))
        self.v.need(*marks)
        if scale is None:
            return self.v.mark(self.nc.vector.tensor_copy(dst, src))
        return self.v.mark(self.nc.vector.tensor_scalar(dst, src, scale, None, ALU.mult))

    def meet(self):
        marks = [q.last() for q in (self.pe, self.v, self.a, self.g)]
        for q in (self.pe, self.v, self.a, self.g):
            q.need(*marks)

    def to_features(self, src, dst, marks, banks, evacuate=None):
        nc, out = self.nc, []
        n = dst.shape[1]
        taken = [banks.take() for _ in range(0, n, 2)]
        assert len({id(b) for b in taken}) == len(taken)
        done_of = {}
        for half in range(H):
            self.pe.need(self.ident_ready, marks[half] if len(marks) == H and isinstance(marks, list) else marks)
            for t0 in range(0, n, 2):
                bank = taken[t0 // 2]
                self.pe.need(bank.free)
                for t in range(t0, min(t0 + 2, n)):
                    o = (t - t0) * S + half * P
                    last = nc.tensor.transpose(bank.ap[:, o:o + P], src(half, t), self.ident)
                done_of[t0] = self.pe.mark(last)
        for t0 in range(0, n, 2):
            bank, done = taken[t0 // 2], done_of[t0]
            pair = min(2, n - t0)
            if evacuate is None:
                m = self.copy(dst[:, t0:t0 + pair, :].rearrange("p a b -> p (a b)"), bank.ap[:, 0:pair * S], done)
                bank.free = [m]
                out += [m] * pair
            else:
                ms = [evacuate(t, bank.ap[:, (t - t0) * S:(t - t0 + 1) * S], done) for t in range(t0, t0 + pair)]
                bank.free = ms
                out += ms
        return out

    def inverse_root(self, dst, src, scale, eps, marks):
        nc = self.nc
        self.v.need(marks)
        m = self.v.mark(nc.vector.tensor_scalar(src, src, scale, eps, ALU.mult, ALU.add))
        self.g.need(m, self.half_ready)
        n = src.shape[-1]
        return self.g.mark(nc.gpsimd.tensor_tensor(dst, src, self.minus_half[:, 0:n], ALU.pow))

    def moments(self, arena, src, marks):
        nc = self.nc
        stats = arena.take(H, 12)
        mv = arena.take(H, 2)
        out = []
        for half in range(H):
            self.v.need(marks[half])
            for c in range(2):
                m = self.v.mark(nc.vector.bn_stats(stats[:, half, 6 * c:6 * c + 6], src[:, half, c * 512:(c + 1) * 512]))
            self.v.need(m)
            out.append(self.v.mark(nc.vector.bn_aggr(mv[:, half, :], stats[:, half, :])))
        return mv, out

    def affine_rows(self, g_row, b_row, name):
        self.g.need(self.rows_free)
        return self.load(self.g, [(self.gain, g_row.partition_broadcast(P)), (self.bias, b_row.partition_broadcast(P))], name)

    def norm_space(self, arena):
        return arena.take(H, 12), arena.take(H, 2), arena.take(H), arena.take(H)

    def chunk_moments(self, space, half, c, mark):
        self.v.need(mark)
        self.moment_marks[half, c] = self.v.mark(self.nc.vector.bn_stats(
            space[0][:, half, 6 * c:6 * c + 6], self.x[:, half, c * 512:(c + 1) * 512]))

    def norm_half(self, space, half, eps, rows_ready):
        nc, v = self.nc, self.v
        stats, mv, var, rstd = space
        v.need(self.moment_marks[half, 0], self.moment_marks[half, 1])
        m = v.mark(nc.vector.bn_aggr(mv[:, half, :], stats[:, half, :]))
        v.need(m)
        e = v.mark(nc.vector.tensor_scalar(var[:, half:half + 1], mv[:, half, 1:2], eps, None, ALU.add))
        self.g.need(e, self.half_ready)
        r = self.g.mark(nc.gpsimd.tensor_tensor(rstd[:, half:half + 1], var[:, half:half + 1], self.minus_half[:, 0:1], ALU.pow))
        v.need(rows_ready)
        f = v.mark(nc.vector.scalar_tensor_tensor(self.x[:, half, :], self.x[:, half, :], mv[:, half, 0:1], self.gain,
                                                  ALU.subtract, ALU.mult))
        v.need(f, r)
        f = v.mark(nc.vector.scalar_tensor_tensor(self.x[:, half, :], self.x[:, half, :], rstd[:, half:half + 1], self.bias,
                                                  ALU.mult, ALU.add))
        self.x_ready[half] = f
        self.rows_free = [f]

    def product_and_norm(self, arena, yT, y_marks, w, banks, combine, eps, rows_ready):
        nc = self.nc
        space = self.norm_space(arena)
        units = [self.columns_unit(w, c * 512, 512, natural=True) for c in range(2)]
        for half in range(H):
            for c, (u, wv) in enumerate(units):
                bank = banks.take()
                self.pe.need(bank.free, u.arrived)
                for j in range(T):
                    self.pe.need(y_marks[j])
                    last = nc.tensor.matmul(bank.ap, yT[:, j, half * P:(half + 1) * P], wv[:, j, :],
                                            start=(j == 0), stop=(j == T - 1))
                done = self.pe.mark(last)
                u.free = [done]
                m = combine(half, c, bank.ap, done)
                bank.free = [m]
                self.chunk_moments(space, half, c, m)
            self.norm_half(space, half, eps, rows_ready)

    def residual(self, half, c, psum, done):
        self.v.need(done, self.x_ready[half])
        xs = self.x[:, half, c * 512:(c + 1) * 512]
        return self.v.mark(self.nc.vector.scalar_tensor_tensor(xs, xs, ALPHA, psum, ALU.mult, ALU.add))


    def setup(self):
        nc, d = self.nc, self.d
        self.ident = self.sb("ident", [P, P])
        self.gain = self.sb("norm_gain", [P, D])
        self.bias = self.sb("norm_bias", [P, D])
        self.rows_free, self.moment_marks = [], {}
        self.minus_half = self.sb("minus_half", [P, 8])
        self.sink = self.sb("sink", [P, NQ])
        self.rope = self.sb("rope", [P, H, 2, ROT // 2])
        self.slot_no = self.sb("slot_numbers", [P, CAP])
        self.router = self.sb("router", [P, DEPTH, T, NE])
        self.columns = self.sb("parameter_columns", [P, 96])
        self.parameter_rows = self.sb("parameter_rows", [P, P])
        self.ident_ready = self.load(self.sp, [(self.ident, d["k_ident"])], "ident_loaded")
        x_rows = d["x"].rearrange("o (h p) d -> p (o h) d", p=P)
        self.x_ready = [self.load(self.sp, [(self.x[:, half, :], x_rows[:, half, :])], f"x{half}_loaded") for half in range(H)]
        self.half_ready = self.g.mark(nc.gpsimd.memset(self.minus_half, -0.5))
        self.small_ready = self.load(self.a, [
            (self.sink, d["attn_sink"].rearrange("o h -> (o h)").partition_broadcast(P)),
            (self.rope, d["k_rope"]),
            (self.slot_no, d["k_slot"]),
            (self.router, d["moe_w_router"].rearrange("l (p t) e -> p l t e", t=T)),
        ], "small_loaded")


    def attention(self, rest):
        nc, d, A = self.nc, self.d, self.main
        banks = Banks(self.banks[0:6])
        window = A.take(H, S)
        window_ready = self.load(self.a, [(window, d["k_window"])], "window_loaded")
        rows_ready = self.affine_rows(d["ln_mix_g"][0], d["ln_mix_b"][0], "ln_mix0_rows")
        xT = A.take(T, S)
        xT_ready = self.to_features(lambda half, t: self.x[:, half, t::T], xT, self.x_ready, banks)
        qkv = A.take(H, QKV)
        qkv_ready = []
        for c in range(QKV // 512):
            u, w = self.columns_unit(d["attn_w_qkv"][0], c * 512, 512)
            for half in range(H):
                bank = banks.take()
                self.pe.need(bank.free, u.arrived)
                for t in range(T):
                    self.pe.need(xT_ready[t])
                    last = nc.tensor.matmul(bank.ap, xT[:, t, half * P:(half + 1) * P], w[:, t, :],
                                            start=(t == 0), stop=(t == T - 1))
                done = self.pe.mark(last)
                dst, src = qkv[:, half, c * 512:(c + 1) * 512], bank.ap
                if c < 2:
                    dst = dst.rearrange("p (g i d) -> p i g d", g=GROUP, i=2)
                    src = src.rearrange("p (i g d) -> p i g d", g=GROUP, i=2)
                m = self.copy(dst, src, done)
                bank.free = [m]
                qkv_ready.append(m)
            u.free = [done]
        NR = NQ + NKV
        turned = []
        tmp = [A.take(NR, ROT // 2) for _ in range(4)]
        for half in range(H):
            heads = qkv[:, half, 0:NR * HD].rearrange("p (h d) -> p h d", d=HD)
            lo, hi = heads[:, :, 0:ROT // 2], heads[:, :, ROT // 2:ROT]
            cos = self.rope[:, half, 0:1, :].to_broadcast([P, NR, ROT // 2])
            sin = self.rope[:, half, 1:2, :].to_broadcast([P, NR, ROT // 2])
            self.v.need(qkv_ready, self.small_ready, self.v.last())
            for dst, a, b in ((tmp[0], lo, cos), (tmp[1], hi, sin), (tmp[2], hi, cos), (tmp[3], lo, sin)):
                m = self.v.mark(nc.vector.tensor_tensor(dst, a, b, ALU.mult))
            self.v.need(m)
            self.v.mark(nc.vector.tensor_tensor(lo, tmp[0], tmp[1], ALU.subtract))
            turned.append(self.v.mark(nc.vector.tensor_tensor(hi, tmp[2], tmp[3], ALU.add)))
        qT = A.take(2 * GROUP, S)
        kT = A.take(2, S)
        kv = qkv[:, :, NQ * HD:(NQ + NKV) * HD].rearrange("p h (m c) -> p h m c", m=2)
        kT_ready = self.to_features(lambda half, m: kv[:, half, m, :], kT, turned, banks)
        qT_ready = self.to_features(lambda half, t: qkv[:, half, t * P:(t + 1) * P], qT, turned, banks)
        vals = qkv[:, :, (NQ + NKV) * HD:]
        oT = xT
        oT_ready = [None] * T
        DEEP = 3
        sm = [A.take(H, S) for _ in range(DEEP)]
        pT = [A.take(H, S) for _ in range(DEEP)]
        neg_max, total, at_sink, den = (A.take(NQ, H) for _ in range(4))
        sm_free, pT_free = [[] for _ in range(DEEP)], [[] for _ in range(DEEP)]
        soft, score, turned_p, out_bank = {}, {}, {}, {}

        def scores(h):
            m, i, g = h // 8, (h // GROUP) % 2, h % GROUP
            bank = banks.take()
            self.pe.need(bank.free, qT_ready[m * GROUP + g], kT_ready[m])
            for half in range(H):
                r = slice(64 * i, 64 * i + 64)
                last = nc.tensor.matmul(bank.ap[:, half * S:(half + 1) * S],
                                        qT[r, m * GROUP + g, half * P:(half + 1) * P], kT[r, m, :],
                                        start=True, stop=True)
            score[h] = (bank, self.pe.mark(last))

        def softmax(h):
            bank, done = score[h]
            s = sm[h % DEEP]
            self.v.need(done, window_ready, sm_free[h % DEEP])
            m = self.v.mark(nc.vector.scalar_tensor_tensor(s, bank.ap.rearrange("p (h k) -> p h k", h=H), HD ** -0.5,
                                                           window, ALU.mult, ALU.add))
            bank.free = [m]
            self.v.need(m)
            m = self.v.mark(nc.vector.tensor_reduce(neg_max[:, h, :], s, AX.X, ALU.max))
            self.v.need(m)
            m = self.v.mark(nc.vector.tensor_scalar(neg_max[:, h, :], neg_max[:, h, :], self.sink[:, h:h + 1], -1.0,
                                                    ALU.max, ALU.mult))
            self.a.need(m)
            for half in range(H):
                e = self.a.mark(nc.scalar.activation(s[:, half, :], s[:, half, :], ACT.Exp, bias=neg_max[:, h, half:half + 1],
                                                     accum_out=total[:, h, half:half + 1]))
            e = self.a.mark(nc.scalar.activation(at_sink[:, h, :], neg_max[:, h, :], ACT.Exp, bias=self.sink[:, h:h + 1]))
            soft[h] = e

        def normalise(h):
            s = sm[h % DEEP]
            self.v.need(soft[h])
            m = self.v.mark(nc.vector.tensor_tensor(den[:, h, :], total[:, h, :], at_sink[:, h, :], ALU.add))
            self.v.need(m)
            m = self.v.mark(nc.vector.reciprocal(den[:, h, :], den[:, h, :]))
            self.v.need(m)
            for half in range(H):
                m = self.v.mark(nc.vector.tensor_scalar(s[:, half, :], s[:, half, :], den[:, h, half:half + 1], None, ALU.mult))
            soft[h] = m

        def turn(h):
            s = sm[h % DEEP]
            bank = banks.take()
            self.pe.need(bank.free, soft[h])
            for kk in range(H):
                for half in range(H):
                    o = kk * S + half * P
                    last = nc.tensor.transpose(bank.ap[:, o:o + P], s[:, half, kk * P:(kk + 1) * P], self.ident)
            done = self.pe.mark(last)
            sm_free[h % DEEP] = [done]
            m = self.copy(pT[h % DEEP].rearrange("p a b -> p (a b)"), bank.ap, done, pT_free[h % DEEP])
            bank.free = [m]
            turned_p[h] = m

        def values(h):
            kvh = h // GROUP
            if h % 2 == 0:
                out_bank[h // 2] = banks.take()
            bank = out_bank[h // 2]
            self.pe.need(bank.free, turned_p[h])
            r = slice(64 * (h % 2), 64 * (h % 2) + 64)
            for kk in range(H):
                last = nc.tensor.matmul(bank.ap[r, 0:S], vals[:, kk, kvh * HD:(kvh + 1) * HD], pT[h % DEEP][:, kk, :],
                                        start=(kk == 0), stop=(kk == H - 1))
            done = self.pe.mark(last)
            pT_free[h % DEEP] = [done]
            if h % 2:
                m = self.copy(oT[:, h // 2, :], bank.ap[:, 0:S], done)
                bank.free = [m]
                oT_ready[h // 2] = m

        for h in range(NQ + 3):
            if h < NQ:
                scores(h)
            if 2 <= h < NQ + 2:
                normalise(h - 2)
            if 1 <= h <= NQ:
                softmax(h - 1)
            if 2 <= h < NQ + 2:
                turn(h - 2)
            if h >= 3:
                values(h - 3)
            rest()
        self.product_and_norm(A, oT, oT_ready, d["attn_w_o"][0], banks, self.residual, EPS_FIRST, rows_ready)


    def experts(self, layer, rest):
        nc, d, A = self.nc, self.d, self.main
        banks = Banks(self.banks[0:5])
        rows_ready = self.affine_rows(d["ln_ffn_g"][layer], d["ln_ffn_b"][layer], f"ln_ffn{layer}_rows")
        xT = A.take(T, S)
        xT_ready = self.to_features(lambda half, t: self.x[:, half, t::T], xT, self.x_ready, banks)
        bank = banks.take()
        self.pe.need(bank.free, xT_ready, self.small_ready)
        for half in range(H):
            for t in range(T):
                last = nc.tensor.matmul(bank.ap[:, half * NE:(half + 1) * NE], xT[:, t, half * P:(half + 1) * P],
                                        self.router[:, layer, t, :], start=(t == 0), stop=(t == T - 1))
        done = self.pe.mark(last)
        aff = A.take(H, NE)
        top, tot = A.take(H), A.take(H)
        self.v.need(done)
        m = self.v.mark(nc.vector.tensor_reduce(top, bank.ap[:, 0:H * NE].rearrange("p (h e) -> p h e", h=H), AX.X, ALU.max,
                                                negate=True))
        self.a.need(m)
        for half in range(H):
            m = self.a.mark(nc.scalar.activation(aff[:, half, :], bank.ap[:, half * NE:(half + 1) * NE], ACT.Exp,
                                                 bias=top[:, half:half + 1], accum_out=tot[:, half:half + 1]))
        bank.free = [m]
        self.v.need(m)
        m = self.v.mark(nc.vector.reciprocal(tot, tot))
        self.v.need(m)
        for half in range(H):
            m = self.v.mark(nc.vector.tensor_scalar(aff[:, half, :], aff[:, half, :], tot[:, half:half + 1], None, ALU.mult))
        aff_ready = m
        bank = banks.take()
        self.pe.need(bank.free, aff_ready)
        for half in range(H):
            last = nc.tensor.transpose(bank.ap[0:NE, half * P:(half + 1) * P], aff[:, half, :], self.ident)
        done = self.pe.mark(last)
        left, count, ones = A.take(S), A.take(S), A.take(S)
        best = A.take(8)
        one_m = self.v.mark(nc.vector.memset(ones[0:NE, :], 1.0))
        self.v.need(done)
        m = self.v.mark(nc.vector.tensor_copy(left[0:NE, :], bank.ap[0:NE, 0:S]))
        bank.free = [m]
        for _ in range(CAP // 8):
            self.v.need(m)
            m = self.v.mark(nc.vector.max(best[0:NE, :], left[0:NE, :]))
            self.v.need(m)
            m = self.v.mark(nc.vector.match_replace(left[0:NE, :], best[0:NE, :], left[0:NE, :], -1.0))
        self.v.need(m)
        m = self.v.mark(nc.vector.tensor_scalar(left[0:NE, :], left[0:NE, :], 0.0, None, ALU.is_lt))
        self.v.need(m, one_m)
        m = self.v.mark(nc.vector.tensor_tensor_scan(count[0:NE, :], ones[0:NE, :], left[0:NE, :], 0.0, ALU.mult, ALU.add))
        self.v.need(m)
        m = self.v.mark(nc.vector.tensor_tensor(count[0:NE, :], count[0:NE, :], left[0:NE, :], ALU.mult))
        bank = banks.take()
        self.pe.need(bank.free, m)
        for half in range(H):
            last = nc.tensor.transpose(bank.ap[:, half * NE:(half + 1) * NE], count[0:NE, half * P:(half + 1) * P],
                                       self.ident[0:NE, 0:NE])
        done = self.pe.mark(last)
        slot = A.take(H, NE)
        self.v.need(done)
        m = self.v.mark(nc.vector.tensor_copy(slot.rearrange("p a b -> p (a b)"), bank.ap[:, 0:H * NE]))
        bank.free = [m]
        hot, gated = A.take(H, NE * CAP), A.take(H, NE * CAP)
        self.v.need(m, self.small_ready)
        for half in range(H):
            view = hot[:, half, :].rearrange("p (e c) -> p e c", e=NE)
            m = self.v.mark(nc.vector.tensor_tensor(view, self.slot_no.unsqueeze(1).to_broadcast([P, NE, CAP]),
                                                    slot[:, half, :].unsqueeze(2).to_broadcast([P, NE, CAP]), ALU.is_equal))
        hot_ready = m
        self.v.need(m)
        for half in range(H):
            m = self.v.mark(nc.vector.tensor_tensor(
                gated[:, half, :].rearrange("p (e c) -> p e c", e=NE), hot[:, half, :].rearrange("p (e c) -> p e c", e=NE),
                aff[:, half, :].unsqueeze(2).to_broadcast([P, NE, CAP]), ALU.mult))
        gated_ready = m
        xs = A.take(T, NE * CAP)
        xs_ready = []
        for t in range(T):
            bank = banks.take()
            self.pe.need(bank.free, hot_ready)
            for half in range(H):
                last = nc.tensor.matmul(bank.ap, self.x[:, half, t::T], hot[:, half, :], start=(half == 0), stop=(half == H - 1))
            done = self.pe.mark(last)
            m = self.copy(xs[:, t, :], bank.ap, done)
            bank.free = [m]
            xs_ready.append(m)
        gathered = done
        back = A.take(NE // PACK, S)
        back_ready = self.to_features(lambda half, g: gated[:, half, g * P:(g + 1) * P], back, gated_ready, banks)
        self.v.need(gathered)
        scaled = [self.v.mark(nc.vector.tensor_scalar(self.x[:, half, :], self.x[:, half, :], ALPHA, None, ALU.mult))
                  for half in range(H)]
        sum_ready = {(half, c): scaled[half] for half in range(H) for c in range(2)}
        up_banks, turn_bank, down_bank = Banks(self.banks[0:2]), self.banks[2], self.banks[3]
        add_banks = [self.banks[4], self.banks[0]]
        space = self.norm_space(A)
        silu = [A.take(S) for _ in range(2)]
        act = [A.take(S) for _ in range(2)]
        actT = [A.take(2, P) for _ in range(2)]
        outs = [A.take(D) for _ in range(2)]
        silu_free, act_free, actT_free, outs_free = [[], []], [[], []], [[], []], [[], []]
        wgu, wd = d["moe_w_gate_up"][layer], d["moe_w_down"][layer]
        QC = D // PACK
        for e in range(NE):
            i = e % 2
            up = up_banks.take()
            self.pe.need(up.free)
            rows = wgu[e].rearrange("(p t) n -> p t n", t=T)
            for k in range(T // 2):
                u = self.unit(lambda slot: [(slot.rearrange("p (t n) -> p t n", t=2), rows[:, 2 * k:2 * k + 2, :])])
                self.pe.need(u.arrived)
                w = u.ap.rearrange("p (t a j c) -> p t a j c", t=2, a=2, j=PACK)
                for tt in range(2):
                    t = 2 * k + tt
                    self.pe.need(xs_ready[t])
                    for j in range(PACK):
                        last = nc.tensor.matmul(up.ap[CAP * j:CAP * (j + 1), :], xs[:, t, e * CAP:(e + 1) * CAP],
                                                w[:, tt, :, j, :], start=(t == 0), stop=(t == T - 1))
                done = self.pe.mark(last)
                u.free = [done]
                if k % 2:
                    rest()
            self.a.need(done, silu_free[i])
            sm = self.a.mark(nc.scalar.activation(silu[i], up.ap[:, 0:QC], ACT.Silu))
            self.v.need(sm, done, act_free[i])
            am = self.v.mark(nc.vector.tensor_tensor(act[i], silu[i], up.ap[:, QC:2 * QC], ALU.mult))
            up.free, silu_free[i] = [sm, am], [am]
            self.pe.need(am, turn_bank.free)
            for s in range(2):
                last = nc.tensor.transpose(turn_bank.ap[:, s * P:(s + 1) * P], act[i][:, s::2], self.ident)
            done = self.pe.mark(last)
            act_free[i] = [done]
            tm = self.copy(actT[i].rearrange("p a b -> p (a b)"), turn_bank.ap[:, 0:2 * P], done, actT_free[i], on_scalar=True)
            turn_bank.free = [tm]
            down_rows = wd[e].rearrange("(j c s) n -> c j (s n)", j=PACK, s=2)
            self.pe.need(tm, down_bank.free)
            for k in range(2):
                u = self.unit(lambda slot: [(slot.rearrange("p (j n) -> p j n", j=2), down_rows[:, 2 * k:2 * k + 2, :])])
                self.pe.need(u.arrived)
                w = u.ap.rearrange("p (j s q n) -> p j s q n", j=2, s=2, q=PACK)
                for jj in range(2):
                    for s in range(2):
                        j = 2 * k + jj
                        for q in range(PACK):
                            last = nc.tensor.matmul(down_bank.ap[CAP * q:CAP * (q + 1), 0:QC], actT[i][:, s, j * CAP:(j + 1) * CAP],
                                                    w[:, jj, s, q, :], start=(j == 0 and s == 0), stop=(j == 3 and s == 1))
                done = self.pe.mark(last)
                u.free = [done]
            actT_free[i] = [done]
            grp, r = e // PACK, e % PACK
            o = outs[grp % 2]
            ms = [self.copy(o[CAP * r:CAP * (r + 1), q * QC:(q + 1) * QC], down_bank.ap[CAP * q:CAP * (q + 1), 0:QC], done,
                            outs_free[grp % 2], on_scalar=q % 2) for q in range(PACK)]
            down_bank.free = ms
            if r == 0:
                outs_ready = []
            outs_ready += ms
            rest()
            if r == PACK - 1:
                for half in range(H):
                    for c in range(2):
                        add_bank = add_banks[c]
                        self.pe.need(outs_ready, add_bank.free, back_ready)
                        done = self.pe.mark(nc.tensor.matmul(add_bank.ap, back[:, grp, half * P:(half + 1) * P],
                                                             o[:, c * 512:(c + 1) * 512], start=True, stop=True))
                        xsum = self.x[:, half, c * 512:(c + 1) * 512]
                        self.v.need(done, sum_ready[half, c])
                        m = self.v.mark(nc.vector.tensor_tensor(xsum, xsum, add_bank.ap, ALU.add))
                        add_bank.free = [m]
                        sum_ready[half, c] = m
                        if e == NE - 1:
                            self.chunk_moments(space, half, c, m)
                    if e == NE - 1:
                        self.norm_half(space, half, EPS_FIRST, rows_ready)
                outs_free[grp % 2] = [done]


    def recurrent(self):
        nc, d, A = self.nc, self.d, self.main
        banks = Banks(self.banks)
        V, SC, G = self.v, self.a, self.g
        col = lambda name, i: self.columns[:, self.col[name] + i:self.col[name] + i + 1]
        rows_ready = self.affine_rows(d["ln_mix_g"][1], d["ln_mix_b"][1], "ln_mix1_rows")
        lam = self.columns[:, self.col["lam"]:self.col["lam"] + 16]
        ex, sq, acc, decay, growth = (A.take(16) for _ in range(5))
        SC.need(self.columns_ready)
        m = SC.mark(nc.scalar.activation(ex, lam, ACT.Abs))
        SC.need(m)
        m = SC.mark(nc.scalar.activation(ex, ex, ACT.Exp, scale=-1.0))
        V.need(m)
        m = V.mark(nc.vector.tensor_scalar(sq, ex, 2.0, None, ALU.add))
        V.need(m)
        m = V.mark(nc.vector.reciprocal(sq, sq))
        V.need(m)
        m = V.mark(nc.vector.tensor_tensor(ex, ex, sq, ALU.mult))
        V.need(m)
        m = V.mark(nc.vector.tensor_tensor(sq, ex, ex, ALU.mult))
        V.need(m)
        m = V.mark(nc.vector.tensor_scalar(acc, sq, 1.0 / 19, None, ALU.mult))
        for n in (17, 15, 13, 11, 9, 7, 5, 3):
            V.need(m)
            m = V.mark(nc.vector.scalar_tensor_tensor(acc, acc, 1.0 / n, sq, ALU.add, ALU.mult))
        V.need(m)
        m = V.mark(nc.vector.scalar_tensor_tensor(acc, acc, 1.0, ex, ALU.add, ALU.mult))
        m2 = V.mark(nc.vector.tensor_scalar(decay, lam, -1.0, 0.0, ALU.mult, ALU.max))
        V.need(m, m2)
        m = V.mark(nc.vector.scalar_tensor_tensor(acc, acc, 2.0, decay, ALU.mult, ALU.add))
        V.need(m)
        V.mark(nc.vector.tensor_scalar(decay, acc, -LRU_C, None, ALU.mult))
        decay_ready = V.mark(nc.vector.tensor_scalar(growth, acc, LRU_C, None, ALU.mult))
        xT_and_a = A.take(T, S)
        pad_and_a = A.take(T, S + CW - 1)
        gelu = A.take(T, S)
        xc = A.take(T, S)
        R = [A.take(T, S) for _ in range(2)]
        I = [A.take(T, S) for _ in range(2)]
        xT = xT_and_a
        xT_ready = self.to_features(lambda half, t: self.x[:, half, t::T], xT, self.x_ready, banks)
        pads = [V.mark(nc.vector.memset(pad_and_a[:, :, 0:2], 0.0)),
                V.mark(nc.vector.memset(pad_and_a[:, :, S + 2:S + 3], 0.0))]
        gelu_ready, xb_ready = [None] * T, [None] * T
        def branch(c):
            u, w = self.columns_unit(d["lru_w_in"][0], c * 512, 512)
            held = []
            for f2 in range(2):
                bank = banks.take()
                self.pe.need(bank.free, u.arrived)
                for ff in range(2):
                    f = f2 * 2 + ff
                    for t in range(T):
                        self.pe.need(xT_ready[t])
                        last = nc.tensor.matmul(bank.ap[:, ff * S:(ff + 1) * S], w[:, t, f * P:(f + 1) * P], xT[:, t, :],
                                                start=(t == 0), stop=(t == T - 1))
                held.append((bank, (c % 2) * 4 + f2 * 2, self.pe.mark(last)))
            u.free = [held[-1][2]]
            return held

        def take_gelu(held):
            for bank, f, done in held:
                SC.need(done)
                m = SC.mark(nc.scalar.activation(gelu[:, f:f + 2, :].rearrange("p a b -> p (a b)"), bank.ap, ACT.Gelu_apprx_tanh))
                gelu_ready[f] = gelu_ready[f + 1] = m
                bank.free = [m]

        for c in (2, 3):
            for bank, f, done in branch(c):
                SC.need(done)
                m = SC.mark(nc.scalar.copy(pad_and_a[:, f:f + 2, 2:S + 2], bank.ap.rearrange("p (a b) -> p a b", a=2)))
                xb_ready[f] = xb_ready[f + 1] = m
                bank.free = [m]
        take_gelu(branch(0))
        xc_ready = [None] * T
        for pair in range(0, T, 2):
            for j in range(CW):
                for f in (pair, pair + 1):
                    tap = pad_and_a[:, f, j:j + S]
                    if j == 0:
                        V.need(xb_ready[f], pads, self.columns_ready)
                        xc_ready[f] = V.mark(nc.vector.tensor_scalar(xc[:, f, :], tap, col("conv_w", f), col("conv_b", f),
                                                                     ALU.mult, ALU.add))
                    else:
                        V.need(xc_ready[f])
                        xc_ready[f] = V.mark(nc.vector.scalar_tensor_tensor(xc[:, f, :], tap, col("conv_w", 8 * j + f),
                                                                            xc[:, f, :], ALU.mult, ALU.add))
        pad_dead = xc_ready[T - 1]
        r_ready, i_ready = {}, {}
        for gate, (key, bias, dst, ready) in enumerate((("lru_w_rgate", "b_r", R, r_ready), ("lru_w_igate", "b_i", I, i_ready))):
            src = d[key][0].rearrange("z n (c p) f -> p (z n c) f", p=P)
            u = self.unit(lambda slot: [(slot.rearrange("p (b f) -> p b f", f=LBW), src)])
            w = u.ap.rearrange("p (z n c f) -> p z n c f", z=2, n=LB, c=2)
            for z in range(2):
                for n in range(LB):
                    bank = banks.take()
                    self.pe.need(bank.free, u.arrived)
                    for ff in range(2):
                        for c in range(2):
                            self.pe.need(xc_ready[2 * n + c])
                            last = nc.tensor.matmul(bank.ap[:, ff * S:(ff + 1) * S], w[:, z, n, c, ff * P:(ff + 1) * P],
                                                    xc[:, 2 * n + c, :], start=(c == 0), stop=(c == 1))
                    done = self.pe.mark(last)
                    SC.need(done)
                    for ff in range(2):
                        f = 2 * n + ff
                        m = SC.mark(nc.scalar.activation(dst[z][:, f, :], bank.ap[:, ff * S:(ff + 1) * S], ACT.Sigmoid,
                                                         bias=col(bias, z * 8 + f)))
                        ready[z, f] = m
                    bank.free = [m]
            u.free = [done]
        late = branch(1)
        xT_dead = late[-1][2]
        a_buf = [pad_and_a[:, :, 0:S], xT_and_a]
        a_dead = [pad_dead, xT_dead]
        th_ready, a_ready, u_ready = {}, {}, {}
        two = [A.take(S) for _ in range(2)]
        sq_free = [[], []]
        for z in range(2):
            for f in range(T):
                G.need(i_ready[z, f], xc_ready[f])
                u_ready[z, f] = G.mark(nc.gpsimd.tensor_tensor(I[z][:, f, :], I[z][:, f, :], xc[:, f, :], ALU.mult))
        grown = {}
        for z in range(2):
            for f in range(T):
                SC.need(decay_ready, a_dead[z], r_ready[z, f])
                a_ready[z, f] = SC.mark(nc.scalar.activation(a_buf[z][:, f, :], R[z][:, f, :], ACT.Exp,
                                                             scale=decay[:, z * 8 + f:z * 8 + f + 1]))
                SC.need(a_ready[z, f])
                th_ready[z, f] = SC.mark(nc.scalar.activation(R[z][:, f, :], R[z][:, f, :], ACT.Tanh,
                                                              scale=growth[:, z * 8 + f:z * 8 + f + 1]))
                k = f % 2
                V.need(a_ready[z, f], sq_free[k])
                m = V.mark(nc.vector.tensor_tensor(two[k], a_buf[z][:, f, :], a_buf[z][:, f, :], ALU.mult))
                V.need(m, th_ready[z, f])
                grown[z] = V.mark(nc.vector.scalar_tensor_tensor(R[z][:, f, :], two[k], 1.0, R[z][:, f, :], ALU.add, ALU.mult))
                sq_free[k] = [grown[z]]
            SC.need(grown[z])
            root = SC.mark(nc.scalar.activation(R[z], R[z], ACT.Sqrt))
            edge = 0 if z == 0 else S - 1
            back = slice(None) if z == 0 else slice(None, None, -1)
            V.need(root)
            edge_m = V.mark(nc.vector.memset(R[z][:, :, edge:edge + 1], 1.0))
            V.need(edge_m)
            if z == 1:
                take_gelu(late)
            for f in range(T):
                V.need(u_ready[z, f])
                u_ready[z, f] = V.mark(nc.vector.tensor_tensor(I[z][:, f, :], I[z][:, f, :], R[z][:, f, :], ALU.mult))
            for f in range(T):
                V.need(u_ready[z, f], a_ready[z, f])
                u_ready[z, f] = V.mark(nc.vector.tensor_tensor_scan(R[z][:, f, back], a_buf[z][:, f, back], I[z][:, f, back], 0.0,
                                                                    ALU.mult, ALU.add))
        y_ready = []
        for f in range(T):
            V.need(u_ready[0, f], u_ready[1, f])
            m = V.mark(nc.vector.tensor_tensor(R[0][:, f, :], R[0][:, f, :], R[1][:, f, :], ALU.add))
            V.need(m, gelu_ready[f])
            y_ready.append(V.mark(nc.vector.tensor_tensor(R[0][:, f, :], R[0][:, f, :], gelu[:, f, :], ALU.mult)))
        self.product_and_norm(A, R[0], y_ready, d["lru_w_out"][0], banks, self.residual, EPS_FIRST, rows_ready)


    def modulated(self, arena, src, src_ready, scale1, shift, mod_ready, dst, banks):
        nc = self.nc
        mv, m = self.moments(arena, src, src_ready)
        rstd, var = arena.take(H), arena.take(H)
        r = []
        for half in range(H):
            self.v.need(m[half])
            c = self.v.mark(nc.vector.tensor_scalar(var[:, half:half + 1], mv[:, half, 1:2], EPS_SECOND, None, ALU.add))
            self.g.need(c, self.half_ready)
            r.append(self.g.mark(nc.gpsimd.tensor_tensor(rstd[:, half:half + 1], var[:, half:half + 1],
                                                         self.minus_half[:, 0:1], ALU.pow)))
        flat = arena.take(H, D)
        flat_ready = []
        for half in range(H):
            self.v.need(r[half], m[half])
            flat_ready.append(self.v.mark(nc.vector.tensor_scalar(flat[:, half, :], src[:, half, :], mv[:, half, 0:1],
                                                                  rstd[:, half:half + 1], ALU.subtract, ALU.mult)))

        def evacuate(t, psum, done):
            if (t // 2) % 2:
                self.a.need(done, mod_ready)
                return self.a.mark(nc.scalar.activation(dst[:, t, :], psum, ACT.Identity, scale=scale1[:, t:t + 1],
                                                        bias=shift[:, t:t + 1]))
            self.v.need(done, mod_ready)
            return self.v.mark(nc.vector.tensor_scalar(dst[:, t, :], psum, scale1[:, t:t + 1], shift[:, t:t + 1],
                                                       ALU.mult, ALU.add))

        return self.to_features(lambda half, t: flat[:, half, t::T], dst, flat_ready, banks, evacuate)

    def feature_tiles(self, u, w, cols, hT, hT_ready, banks, finish, width=P):
        nc = self.nc
        for i in range(0, len(cols), 2):
            bank = banks.take()
            self.pe.need(bank.free, u.arrived)
            pair = cols[i:i + 2]
            for k, c in enumerate(pair):
                for t in range(T):
                    self.pe.need(hT_ready[t])
                    last = nc.tensor.matmul(bank.ap[0:width, k * S:(k + 1) * S], w[:, t, c:c + width], hT[:, t, :],
                                            start=(t == 0), stop=(t == T - 1))
            done = self.pe.mark(last)
            bank.free = [finish(i, bank.ap[0:width, 0:len(pair) * S], done)]
        u.free = [done]

    def token_tiles(self, u, w, c, n, hT, hT_ready, banks, finish):
        nc = self.nc
        for half in range(H):
            bank = banks.take()
            self.pe.need(bank.free, u.arrived)
            for t in range(T):
                self.pe.need(hT_ready[t])
                last = nc.tensor.matmul(bank.ap[:, 0:n], hT[:, t, half * P:(half + 1) * P], w[:, t, c:c + n],
                                        start=(t == 0), stop=(t == T - 1))
            done = self.pe.mark(last)
            bank.free = [finish(half, bank.ap[:, 0:n], done)]
        u.free = [done]

    def log_gates(self, arena, lrT, lr_ready, banks):
        nc = self.nc
        z, t = arena.take(4, S), arena.take(4, S)
        out = []
        for i in range(0, 4, 2):
            bank = banks.take()
            self.pe.need(bank.free, lr_ready, self.w2_ready)
            for k in range(2):
                last = nc.tensor.matmul(bank.ap[:, k * S:(k + 1) * S], self.w2[0:2 * GR, (i + k) * P:(i + k + 1) * P],
                                        lrT[0:2 * GR, :], start=True, stop=True)
            done = self.pe.mark(last)
            self.v.need(done)
            for k in range(2):
                b = self.col["gla_b"] + i + k
                m = self.v.mark(nc.vector.tensor_scalar(z[:, i + k, :], bank.ap[:, k * S:(k + 1) * S], self.columns[:, b:b + 1],
                                                        None, ALU.add))
            bank.free = [m]
            self.a.need(m)
            n = self.a.mark(nc.scalar.activation(t[:, i:i + 2, :], z[:, i:i + 2, :], ACT.Abs))
            self.a.need(n)
            n = self.a.mark(nc.scalar.activation(t[:, i:i + 2, :], t[:, i:i + 2, :], ACT.Exp, scale=-1.0))
            self.a.need(n)
            n = self.a.mark(nc.scalar.activation(t[:, i:i + 2, :], t[:, i:i + 2, :], ACT.Ln, bias=1.0))
            self.v.need(n)
            out.append(self.v.mark(nc.vector.scalar_tensor_tensor(z[:, i:i + 2, :], z[:, i:i + 2, :], 0.0, t[:, i:i + 2, :],
                                                                  ALU.min, ALU.subtract)))
        return z, t, out

    def rms_columns(self, arena, parts, n, marks):
        nc = self.nc
        junk = arena.take(n)
        ss, r = arena.take(len(parts)), arena.take(len(parts))
        self.a.need(marks)
        m = None
        for i, part in enumerate(parts):
            self.a.need(m)
            m = self.a.mark(nc.scalar.activation(junk, part, ACT.Square, accum_out=ss[:, i:i + 1]))
        return r, self.inverse_root(r, ss, 1.0 / n, EPS_SECOND, m)

    def side_work(self):
        nc, d, A = self.nc, self.d, self.side
        banks = Banks(self.banks[6:8])
        conds = self.sb("conditions", [P, 2, T])
        loaded = self.load(self.g, [(conds[:, 0, :], d["c_2"].rearrange("o (p t) -> p (o t)", t=T)),
                                    (conds[:, 1, :], d["c_ctx_2"].rearrange("(p t) -> p t", t=T))], "conditions_loaded")
        cT = self.sb("condition_columns", [P, T, 2])
        yield
        self.a.need(loaded)
        cond_ready = self.a.mark(nc.scalar.activation(cT.rearrange("p t c -> p c t"), conds, ACT.Silu))
        self.mod = self.sb("modulation", [P, 3, 2, T])
        self.w2 = self.sb("gate_weights", [2 * GR, 2 * GH * GK])
        z = self.v.mark(nc.vector.memset(self.w2, 0.0))
        self.g.need(z)
        self.w2_ready = self.load(self.g, [(self.w2[dd * GR:(dd + 1) * GR, dd * 256:(dd + 1) * 256], d["gla_w2_2"][0, dd])
                                           for dd in range(2)], "gate_weights_loaded")
        rows = self.parameter_rows
        at, pairs = 0, []
        self.col = {}
        for name, key in (("conv_w", "lru_conv_w"), ("conv_b", "lru_conv_b"), ("b_r", "lru_b_rgate"),
                          ("b_i", "lru_b_igate"), ("lam", "lru_lambda"), ("gla_b", "gla_b_2"),
                          ("gla_g", "gla_norm_g_2"), ("q_g", "mla_q_norm_g_2"), ("kv_g", "mla_kv_norm_g_2")):
            a = d[key]
            names = ["a", "b", "c"][:len(a.shape) - 1]
            flat = a.rearrange(f"{' '.join(names)} (n k) -> ({' '.join(names)} n) k", k=P)
            n = flat.shape[0]
            pairs.append((rows[at:at + n, :], flat))
            self.col[name] = at
            at += n
        assert at == 96
        loaded = self.load(self.g, pairs, "parameter_rows_loaded")
        yield
        self.pe.need(loaded, self.ident_ready)
        bank = banks.take()
        self.pe.need(bank.free)
        done = self.pe.mark(nc.tensor.transpose(bank.ap[:, 0:96], rows[0:96, :], self.ident[0:96, 0:96]))
        self.columns_ready = self.copy(self.columns, bank.ap[:, 0:96], done, on_scalar=False)
        bank.free = [self.columns_ready]
        start = A.at
        bias = A.take(3 * D)
        row = [A.take(512) for _ in range(2)]
        row_free = [[], []]
        bias_free = []
        stored, n_stored = [self.new_sem(f"ada_rows_{i}_stored") for i in range(2)], [0, 0]
        for layer in range(DEPTH):
            self.g.need(bias_free)
            bias_ready = self.load(self.g, [(bias[0:2, :], d["ada_b_2"][layer].partition_broadcast(2))], f"ada_bias{layer}_loaded")
            for c in range(6):
                u, w = self.columns_unit(d["ada_w_2"][layer], c * 512, 512)
                bank = banks.take()
                self.pe.need(bank.free, u.arrived, cond_ready)
                for t in range(T):
                    for j in range(PACK):
                        last = nc.tensor.matmul(bank.ap[32 * j:32 * j + 2, 0:P], cT[:, t, :], w[:, t, j * P:(j + 1) * P],
                                                start=(t == 0), stop=(t == T - 1))
                done = self.pe.mark(last)
                u.free = [done]
                self.v.need(done, bias_ready, row_free[c % 2])
                for j in range(PACK):
                    m = self.v.mark(nc.vector.tensor_tensor(row[c % 2][0:2, j * P:(j + 1) * P], bank.ap[32 * j:32 * j + 2, 0:P],
                                                            bias[0:2, c * 512 + j * P:c * 512 + (j + 1) * P], ALU.add))
                bank.free = [m]
                self.g.need(m)
                nc.gpsimd.dma_start(self.rows_dram[layer][:, c * 512:(c + 1) * 512], row[c % 2][0:2, :]).then_inc(stored[c % 2], 16)
                n_stored[c % 2] += 16
                row_free[c % 2] = [(stored[c % 2], n_stored[c % 2])]
                bias_free = [m]
                yield
            self.rows_stored = [row_free[0], row_free[1]]
            self.g.need(self.rows_stored)
            which = [(0, 0), (1, 1)] if layer == 0 else [(2, 0)]
            ms = self.load(self.g, [(self.mod[:, slot, part, :], self.rows_dram[layer][r, part * D:(part + 1) * D]
                                     .rearrange("(p t) -> p t", t=T)) for slot, r in which for part in range(2)],
                           f"modulation{layer}_loaded")
            self.v.need(ms)
            for slot, _ in which:
                m = self.v.mark(nc.vector.tensor_scalar(self.mod[:, slot, 1, :], self.mod[:, slot, 1, :], 1.0, None, ALU.add))
            if layer == 0:
                self.mod0_ready = m
            else:
                self.mod1_ready = m
            yield
        A.at = start
        ones = A.take(S)
        self.v.need(row_free)
        ones_ready = self.v.mark(nc.vector.memset(ones, 1.0))
        self.ctx_tokens = A.take(H, D)
        self.g.need(row_free, bias_free)
        mark0 = A.at
        hT = A.take(T, S)
        ctx = self.ctx_tokens
        ctx_loaded = self.load(self.g, [(ctx, d["ctx_2"].rearrange("o (h p) d -> p (o h) d", p=P))], "context_loaded")
        mv, m = self.moments(A, ctx, [ctx_loaded, ctx_loaded])
        yield
        rstd, var = A.take(H), A.take(H)
        self.v.need(m)
        c = self.v.mark(nc.vector.tensor_copy(var, mv[:, :, 1]))
        r = self.inverse_root(rstd, var, 1.0, EPS_SECOND, c)
        self.v.need(r, m)
        flat_ready = [self.v.mark(nc.vector.tensor_scalar(ctx[:, half, :], ctx[:, half, :], mv[:, half, 0:1],
                                                          rstd[:, half:half + 1], ALU.subtract, ALU.mult))
                      for half in range(H)]
        hT_ready = []
        for t0 in range(0, T, 2):
            def evacuate(t, psum, done, t0=t0):
                self.v.need(done, self.mod0_ready)
                return self.v.mark(nc.vector.tensor_scalar(hT[:, t0 + t, :], psum, self.mod[:, 1, 1, t0 + t:t0 + t + 1],
                                                           self.mod[:, 1, 0, t0 + t:t0 + t + 1], ALU.mult, ALU.add))
            hT_ready += self.to_features(lambda half, t: ctx[:, half, (t0 + t)::T], hT[:, t0:t0 + 2, :], flat_ready, banks,
                                         evacuate)
            yield
        ctx_dead = self.pe.last()
        B = Arena(self.ctx_tokens.rearrange("p h d -> p (h d)"), H * D)
        kT, vals = B.take(2, S), B.take(H, GH * GV)
        lrT = B.take(S)
        ckr = A.take(H, KVR + MR)
        w_in = d["even_w_in_2"][0]
        ready = {}

        def keep(name, dst_of):
            def finish(i, psum, done):
                dst = dst_of(i)
                if len(dst.shape) == 3:
                    psum = psum.rearrange("p (a b) -> p a b", a=dst.shape[1])
                m = self.copy(dst, psum, done, ctx_dead)
                ready.setdefault(name, []).append(m)
                return m
            return finish

        u, w = self.columns_unit(w_in, C_GK, 512)
        self.feature_tiles(u, w, [0, P], hT, hT_ready, banks, keep("k", lambda i: kT[:, i:i + 2, :]))
        yield
        self.token_tiles(u, w, 256, 256, hT, hT_ready, banks, keep("v", lambda half: vals[:, half, 0:256]))
        yield
        u, w = self.columns_unit(w_in, C_GV + 256, 256 + 2 * GR)
        self.token_tiles(u, w, 0, 256, hT, hT_ready, banks, keep("v", lambda half: vals[:, half, 256:512]))
        yield
        self.feature_tiles(u, w, [256], hT, hT_ready, banks, keep("lr", lambda i: lrT[0:2 * GR, :]), width=2 * GR)
        yield
        u, w = self.columns_unit(w_in, C_CKV, KVR + MR)
        self.token_tiles(u, w, 0, KVR + MR, hT, hT_ready, banks, keep("ckr", lambda half: ckr[:, half, :]))
        yield
        self.lat0_ready = self.latents(A, ckr, ready["ckr"], self.latT0, self.krT0, banks, False)
        yield
        hT_dead = self.pe.last()
        A.at = mark0
        for q in (self.v, self.a):
            q.need(hT_dead)
        z, t, g_ready = self.log_gates_side(A, lrT, ready["lr"], banks)
        yield
        sums = A.take(S + 1)
        wk, wkT = t[:, 2, :], t[:, 0:2, :]
        self.state0_ready = []
        wk_free = sums_free = wkT_free = []
        for dd in range(2):
            turned = []
            for i in range(2):
                self.v.need(sums_free)
                edge = S if dd == 0 else 0
                m = self.v.mark(nc.vector.memset(sums[:, edge:edge + 1], 0.0))
                self.v.need(g_ready, m, ones_ready)
                src = z[:, 2 * dd + i, :]
                if dd == 0:
                    m = self.v.mark(nc.vector.tensor_tensor_scan(sums[:, 0:S][:, ::-1], ones, src[:, ::-1], 0.0, ALU.mult, ALU.add))
                    part = sums[:, 1:S + 1]
                else:
                    m = self.v.mark(nc.vector.tensor_tensor_scan(sums[:, 1:S + 1], ones, src, 0.0, ALU.mult, ALU.add))
                    part = sums[:, 0:S]
                self.a.need(m, wk_free)
                m = self.a.mark(nc.scalar.activation(wk, part, ACT.Exp, scale=1.0 / GTAU))
                sums_free = [m]
                self.v.need(m, ready["k"])
                m = self.v.mark(nc.vector.tensor_tensor(wk, wk, kT[:, i, :], ALU.mult))
                bank = banks.take()
                self.pe.need(bank.free, m)
                for half in range(H):
                    last = nc.tensor.transpose(bank.ap[:, half * P:(half + 1) * P], wk[:, half * P:(half + 1) * P], self.ident)
                done = self.pe.mark(last)
                wk_free = [done]
                m = self.copy(wkT[:, :, i * P:(i + 1) * P], bank.ap[:, 0:S].rearrange("p (a b) -> p a b", a=H), done, wkT_free)
                bank.free = [m]
                turned.append(m)
            yield
            bank = banks.take()
            self.pe.need(bank.free, turned, ready["v"])
            for i in range(2):
                for half in range(H):
                    last = nc.tensor.matmul(bank.ap[:, i * S:(i + 1) * S], wkT[:, half, i * P:(i + 1) * P],
                                            vals[:, half, i * 256:(i + 1) * 256], start=(half == 0), stop=(half == H - 1))
            done = self.pe.mark(last)
            wkT_free = [done]
            self.v.need(done)
            for k in range(2):
                r = slice(64 * k, 64 * k + 64)
                m = self.v.mark(nc.vector.tensor_copy(
                    self.state0[r, dd, :, :],
                    bank.ap[r, :].rearrange("p (i k v) -> p i k v", i=2, k=2)[:, :, k, :]))
                self.state0_ready.append(m)
            bank.free = [m]
            yield

    def log_gates_side(self, arena, lrT, lr_ready, banks):
        return self.log_gates(arena, lrT, lr_ready, banks)

    def latents(self, arena, ckr, marks, latT, krT, banks, rotate):
        nc = self.nc
        r, r_ready = self.rms_columns(arena, [ckr[:, half, 0:KVR] for half in range(H)], KVR, marks)
        self.v.need(r_ready, marks)
        for half in range(H):
            m = self.v.mark(nc.vector.tensor_scalar(ckr[:, half, 0:KVR], ckr[:, half, 0:KVR], r[:, half:half + 1], None, ALU.mult))
        if rotate:
            m = [m, self.rotate(arena, ckr[:, :, KVR:].rearrange("p h (o r) -> p h o r", o=1), 1, marks)]
        bank = banks.take()
        self.pe.need(bank.free, m, marks)
        for half in range(H):
            nc.tensor.transpose(bank.ap[:, half * P:(half + 1) * P], ckr[:, half, 0:KVR], self.ident)
            last = nc.tensor.transpose(bank.ap[0:MR, S + half * P:S + (half + 1) * P], ckr[:, half, KVR:], self.ident)
        done = self.pe.mark(last)
        self.v.need(done, self.columns_ready)
        c = self.col["kv_g"]
        m1 = self.v.mark(nc.vector.tensor_scalar(latT, bank.ap[:, 0:S], self.columns[:, c:c + 1], None, ALU.mult))
        m2 = self.v.mark(nc.vector.tensor_copy(krT, bank.ap[0:MR, S:2 * S]))
        bank.free = [m2]
        return [m1, m2]

    def rotate(self, arena, heads, n, marks):
        nc = self.nc
        tmp = [arena.take(n, MR // 2) for _ in range(4)]
        m = None
        for half in range(H):
            a, b = heads[:, half, :, 0:MR // 2], heads[:, half, :, MR // 2:MR]
            cos = self.axial[:, half, 0:1, :].to_broadcast([P, n, MR // 2])
            sin = self.axial[:, half, 1:2, :].to_broadcast([P, n, MR // 2])
            self.v.need(marks, self.small2_ready, m)
            for dst, s, t in ((tmp[0], a, cos), (tmp[1], b, sin), (tmp[2], a, sin), (tmp[3], b, cos)):
                k = self.v.mark(nc.vector.tensor_tensor(dst, s, t, ALU.mult))
            self.v.need(k)
            self.v.mark(nc.vector.tensor_tensor(a, tmp[0], tmp[1], ALU.subtract))
            m = self.v.mark(nc.vector.tensor_tensor(b, tmp[2], tmp[3], ALU.add))
        return m

    def gate_row(self, row, layer, name):
        self.g.need(self.rows_stored)
        return self.load(self.g, [(row, self.rows_dram[layer][0, 2 * D:3 * D].partition_broadcast(P))], name)

    def gated_residual(self, tmp, row, row_ready):
        nc = self.nc
        n = [0]
        free = [[], []]

        def combine(half, c, psum, done):
            i = n[0] % 2
            n[0] += 1
            self.v.need(done, row_ready, free[i])
            m = self.v.mark(nc.vector.tensor_tensor(tmp[i], psum, row[:, c * 512:(c + 1) * 512], ALU.mult))
            xs = self.x[:, half, c * 512:(c + 1) * 512]
            self.v.need(m, self.x_ready[half])
            m = self.v.mark(nc.vector.scalar_tensor_tensor(xs, xs, ALPHA, tmp[i], ALU.mult, ALU.add))
            free[i] = [m]
            return m

        return combine

    def even(self):
        nc, d, A = self.nc, self.d, self.whole
        V, SC = self.v, self.a
        banks = Banks(self.banks)
        rows_ready = self.affine_rows(d["post_ln_g_2"][0], d["post_ln_b_2"][0], "post_ln0_rows")
        gate = A.take(D)
        tmp = [A.take(512) for _ in range(2)]
        mgT, cq, ckr = A.take(GH, S), A.take(H, QR), A.take(H, KVR + MR)
        yT = A.take(T, S)
        linear_only = A.at
        reset = A.take(2, S)
        tri = A.take(2, P).bitcast(U32)
        tables = self.load(self.g, [(reset, d["k_reset"]), (tri, d["k_tri"])], "chunk_tables_loaded")
        gate_ready = self.gate_row(gate, 0, "gate0_row")
        qT, kT, vals = A.take(2, S), A.take(2, S), A.take(H, GH * GV)
        ggT, lrT = A.take(GH, S), A.take(S)
        combine = self.gated_residual(tmp, gate, gate_ready)
        base = A.at
        hT = A.take(T, S)
        hT_ready = self.modulated(A, self.x, self.x_ready, self.mod[:, 0, 1, :], self.mod[:, 0, 0, :], self.mod0_ready, hT, banks)
        ready = {}

        def keep(name, dst_of, scale=None, func=None):
            def finish(i, psum, done):
                dst = dst_of(i)
                if len(dst.shape) == 3:
                    psum = psum.rearrange("p (a b) -> p a b", a=dst.shape[1])
                if func is not None:
                    SC.need(done)
                    m = SC.mark(nc.scalar.activation(dst, psum, func))
                else:
                    m = self.copy(dst, psum, done, scale=scale)
                ready.setdefault(name, []).append(m)
                return m
            return finish

        w_in = d["even_w_in_2"][0]
        args = (hT, hT_ready, banks)
        u, w = self.columns_unit(w_in, C_GQ, 512)
        self.feature_tiles(u, w, [0, P], *args, keep("q", lambda i: qT[:, i:i + 2, :], scale=GK ** -0.5))
        self.feature_tiles(u, w, [2 * P, 3 * P], *args, keep("k", lambda i: kT[:, i:i + 2, :]))
        u, w = self.columns_unit(w_in, C_GV, 512)
        self.token_tiles(u, w, 0, 512, *args, keep("v", lambda half: vals[:, half, :]))
        u, w = self.columns_unit(w_in, C_LR, 2 * GR + 3 * P)
        self.feature_tiles(u, w, [0], *args, keep("lr", lambda i: lrT[0:2 * GR, :]), width=2 * GR)
        self.feature_tiles(u, w, [32, 32 + P, 32 + 2 * P], *args, keep("gg", lambda i: ggT[:, i:min(i + 2, 3), :], func=ACT.Silu))
        u, w = self.columns_unit(w_in, C_GG + 3 * P, P + QR)
        self.feature_tiles(u, w, [0], *args, keep("gg", lambda i: ggT[:, 3, :], func=ACT.Silu))
        self.token_tiles(u, w, P, QR, *args, keep("cq", lambda half: cq[:, half, :]))
        u, w = self.columns_unit(w_in, C_CKV, KVR + MR + 2 * P)
        self.token_tiles(u, w, 0, KVR + MR, *args, keep("ckr", lambda half: ckr[:, half, :]))
        self.feature_tiles(u, w, [160, 160 + P], *args, keep("mg", lambda i: mgT[:, i:i + 2, :], func=ACT.Silu))
        u, w = self.columns_unit(w_in, C_MG + 2 * P, 2 * P)
        self.feature_tiles(u, w, [0, P], *args, keep("mg", lambda i: mgT[:, 2 + i:4 + i, :], func=ACT.Silu))
        self.meet()
        A.at = base
        y_ready = [None] * T
        self.linear_attention(A, banks, qT, kT, vals, lrT, ggT, reset, tri, tables, ready, yT, y_ready)
        self.meet()
        A.at = linear_only
        self.latent_attention(A, banks, cq, ckr, mgT, ready, yT, y_ready)
        self.product_and_norm(A, yT, y_ready, d["even_w_out_2"][0], banks, combine, EPS_SECOND, rows_ready)

    def linear_attention(self, A, banks, qT, kT, vals, lrT, ggT, reset, tri, tables, ready, yT, y_ready):
        nc, V, SC = self.nc, self.v, self.a
        S_ = [[A.take(2, 2 * GV) for _ in range(2)] for _ in range(2)]
        o = A.take(H, GH * GV)
        bT = A.take(4, S)
        top = A.at
        z, t, g_ready = self.log_gates(A, lrT, ready["lr"], banks)
        b_ready = []
        for dd in range(2):
            for i in range(2):
                back = slice(None) if dd == 0 else slice(None, None, -1)
                V.need(g_ready, tables)
                b_ready.append(V.mark(nc.vector.tensor_tensor_scan(bT[:, 2 * dd + i, :][:, back], reset[:, dd, :][:, back],
                                                                   z[:, 2 * dd + i, :][:, back], 0.0, ALU.mult, ALU.add)))
        V.need(b_ready)
        self.a.need(b_ready)
        A.at = top
        ke, qe, kend, qb, att, kendT = {}, {}, {}, {}, {}, {}
        e_ready = {}
        end = A.take(2, 8)
        for dd in range(2):
            ke[dd], qe[dd], kend[dd], qb[dd] = (A.take(2, S) for _ in range(4))
        for dd in range(2):
            att[dd] = A.take(4, 2 * P)
            kendT[dd] = A.take(H, S)
        for dd in range(2):
            chunks = lambda ap: ap.rearrange("p i (c t) -> p (i c) t", c=NCH)
            b = chunks(bT[:, 2 * dd:2 * dd + 2, :])
            mid = b[:, :, (GCH // 2 - 1 if dd == 0 else GCH // 2)].unsqueeze(2).to_broadcast([P, 2 * NCH, GCH])
            last_ = b[:, :, (GCH - 1 if dd == 0 else 0)]
            lastb = last_.unsqueeze(2).to_broadcast([P, 2 * NCH, GCH])
            m1 = V.mark(nc.vector.tensor_tensor(chunks(qe[dd]), b, mid, ALU.subtract))
            m2 = V.mark(nc.vector.tensor_tensor(chunks(kend[dd]), b, lastb, ALU.subtract))
            SC.need(m1, m2, b_ready)
            e1 = SC.mark(nc.scalar.activation(ke[dd], qe[dd], ACT.Exp, scale=-1.0 / GTAU))
            SC.need(e1)
            e2 = SC.mark(nc.scalar.activation(qe[dd], qe[dd], ACT.Exp, scale=1.0 / GTAU))
            e3 = SC.mark(nc.scalar.activation(kend[dd], kend[dd], ACT.Exp, scale=-1.0 / GTAU))
            e4 = SC.mark(nc.scalar.activation(qb[dd], bT[:, 2 * dd:2 * dd + 2, :], ACT.Exp, scale=1.0 / GTAU))
            e5 = SC.mark(nc.scalar.activation(end[:, dd, :], last_, ACT.Exp, scale=1.0 / GTAU))
            V.need(e1, e2, e3, e4, ready["q"], ready["k"])
            ms = [V.mark(nc.vector.tensor_tensor(buf, buf, src, ALU.mult))
                  for buf, src in ((kend[dd], kT), (ke[dd], kT), (qe[dd], qT), (qb[dd], qT))]
            e_ready[dd] = [ms[-1], e5]
        zero = [V.mark(nc.vector.memset(att[dd], 0.0)) for dd in range(2)]
        zero += [V.mark(nc.vector.memset(S_[dd][1], 0.0)) for dd in range(2)]
        V.need(self.state0_ready)
        zero0 = [V.mark(nc.vector.memset(S_[dd][0], 0.0)) for dd in range(2)]
        V.need(zero0)
        s_ready = []
        for dd in range(2):
            for k in range(2):
                r = slice(64 * k, 64 * k + 64)
                m = V.mark(nc.vector.tensor_copy(S_[dd][0][r, :, k * GV:(k + 1) * GV], self.state0[r, dd, :, :]))
            s_ready.append(m)
        att_ready, kendT_ready = {}, {}
        for dd in range(2):
            for k in range(2):
                bank = banks.take()
                self.pe.need(bank.free, e_ready[dd])
                r = slice(64 * k, 64 * k + 64)
                for i in range(2):
                    for half in range(H):
                        hs = slice(half * P, (half + 1) * P)
                        last = nc.tensor.matmul(bank.ap[:, (2 * i + half) * P:(2 * i + half + 1) * P], ke[dd][r, i, hs],
                                                qe[dd][r, i, hs], start=True, stop=True)
                done = self.pe.mark(last)
                V.need(done, zero, tables)
                for i in range(2):
                    for half in range(H):
                        h = 2 * i + k
                        c = (2 * i + half) * P
                        m = V.mark(nc.vector.copy_predicated(att[dd][:, h, half * P:(half + 1) * P], tri[:, dd, :],
                                                             bank.ap[:, c:c + P]))
                bank.free = [m]
                att_ready[dd, k] = m
            kendT_ready[dd] = []
            bank = banks.take()
            self.pe.need(bank.free)
            for half in range(H):
                for i in range(2):
                    o_ = half * S + i * P
                    last = nc.tensor.transpose(bank.ap[:, o_:o_ + P], kend[dd][:, i, half * P:(half + 1) * P], self.ident)
            done = self.pe.mark(last)
            m = self.copy(kendT[dd].rearrange("p a b -> p (a b)"), bank.ap, done)
            bank.free = [m]
            kendT_ready[dd] = m
        out = [banks.take() for _ in range(H)]
        ds_banks = Banks([b for b in self.banks if b not in out])
        started = [False, False]
        self.pe.need(out[0].free, out[1].free, ready["v"])
        for half in range(H):
            for dd in range(2):
                for h in range(GH):
                    self.pe.need(att_ready[dd, h % 2])
                    nc.tensor.matmul(out[half].ap[:, h * GV:(h + 1) * GV], att[dd][:, h, half * P:(half + 1) * P],
                                     vals[:, half, h * GV:(h + 1) * GV], start=not started[half], stop=False,
                                     skip_group_check=True)
                    started[half] = True
        s_free = [[[], []], [[], []]]
        for step in range(NCH):
            for dd in range(2):
                c = step if dd == 0 else NCH - 1 - step
                half, k = c // 2, c % 2
                rows = slice(64 * k, 64 * k + 64)
                cur, nxt = S_[dd][step % 2], S_[dd][(step + 1) % 2]
                self.pe.need(s_ready[dd])
                for i in range(2):
                    last = nc.tensor.matmul(out[half].ap[rows, i * 256:(i + 1) * 256], qb[dd][:, i, c * GCH:(c + 1) * GCH],
                                            cur[:, i, :], start=False, stop=(step == NCH - 1), skip_group_check=True)
                done = self.pe.mark(last)
                s_free[dd][step % 2] = [done]
                if step == NCH - 1:
                    last_done = done
                    continue
                bank = ds_banks.take()
                self.pe.need(bank.free, kendT_ready[dd])
                for i in range(2):
                    last = nc.tensor.matmul(bank.ap[:, i * 256:(i + 1) * 256], kendT[dd][rows, half, i * P:(i + 1) * P],
                                            vals[rows, half, i * 256:(i + 1) * 256], start=True, stop=True)
                done = self.pe.mark(last)
                V.need(done, s_free[dd][(step + 1) % 2], s_ready[dd], zero, e_ready[dd])
                for i in range(2):
                    for kk in range(2):
                        r = slice(64 * kk, 64 * kk + 64)
                        m = V.mark(nc.vector.scalar_tensor_tensor(
                            nxt[r, i, kk * GV:(kk + 1) * GV], cur[r, i, kk * GV:(kk + 1) * GV],
                            end[r, dd, i * NCH + c:i * NCH + c + 1], bank.ap[r, i * 256 + kk * GV:i * 256 + (kk + 1) * GV],
                            ALU.mult, ALU.add))
                bank.free = [m]
                s_ready[dd] = m
        o_ready = []
        for half in range(H):
            m = self.copy(o[:, half, :], out[half].ap, last_done)
            out[half].free = [m]
            o_ready.append(m)
        parts = [o[:, half, h * GV:(h + 1) * GV] for half in range(H) for h in range(GH)]
        r, r_ready = self.rms_columns(A, parts, GV, o_ready)
        V.need(r_ready, o_ready)
        n_ready = [V.mark(nc.vector.tensor_scalar(part, part, r[:, i:i + 1], None, ALU.mult)) for i, part in enumerate(parts)]
        gcol = self.columns[:, self.col["gla_g"]:self.col["gla_g"] + 1]

        def evacuate(t, psum, done):
            V.need(done, ready["gg"])
            m = V.mark(nc.vector.scalar_tensor_tensor(yT[:, t, :], psum, gcol, ggT[:, t, :], ALU.mult, ALU.mult))
            y_ready[t] = m
            return m

        self.to_features(lambda half, h: o[:, half, h * GV:(h + 1) * GV], yT[:, 0:GH, :], n_ready[-1], banks, evacuate)

    def latent_attention(self, A, banks, cq, ckr, mgT, ready, yT, y_ready):
        nc, d, V, SC = self.nc, self.d, self.v, self.a
        K = 2 * S
        KT = K // P
        KQ = QR // P
        latT, krT = A.take(K), A.take(K)[0:MR, :]
        lat_ready = self.latents(A, ckr, ready["ckr"], latT[:, S:K], krT[:, S:K], banks, True)
        V.need(self.lat0_ready)
        lat_ready += [V.mark(nc.vector.tensor_copy(latT[:, 0:S], self.latT0)),
                      V.mark(nc.vector.tensor_copy(krT[:, 0:S], self.krT0))]
        r, r_ready = self.rms_columns(A, [cq[:, half, :] for half in range(H)], QR, ready["cq"])
        V.need(r_ready)
        for half in range(H):
            m = V.mark(nc.vector.tensor_scalar(cq[:, half, :], cq[:, half, :], r[:, half:half + 1], None, ALU.mult))
        cqT = A.take(KQ, S)

        def evacuate(t, psum, done):
            V.need(done)
            c = self.col["q_g"] + t
            return V.mark(nc.vector.tensor_scalar(cqT[:, t, :], psum, self.columns[:, c:c + 1], None, ALU.mult))

        cqT_ready = self.to_features(lambda half, t: cq[:, half, t * P:(t + 1) * P], cqT, m, banks, evacuate)
        NU = KQ * MH * MQ
        u = self.unit(lambda slot: [
            (slot[:, 0:NU].rearrange("p (k n) -> p k n", k=KQ), d["mla_w_uq_2"][0].rearrange("(k p) n -> p k n", p=P)),
            (slot[:, UNIT - MH * (MN + MV):UNIT], d["mla_w_ukv_2"][0])])
        wq = u.ap[:, 0:NU].rearrange("p (k h n) -> p k h n", k=KQ, h=MH)
        wkv = u.ap[:, UNIT - MH * (MN + MV):UNIT].rearrange("p (h n) -> p h n", h=MH)
        qT, kT = A.take(MH, S), A.take(MH, K)
        vals = A.take(KT, MH * MV)
        qr = A.take(H, MH * MR)
        qr_ready = []
        for half in range(H):
            bank = banks.take()
            self.pe.need(bank.free, u.arrived, cqT_ready)
            for k in range(KQ):
                last = nc.tensor.matmul(bank.ap[:, 0:MH * MR], cqT[:, k, half * P:(half + 1) * P], wq[:, k, :, MN:MQ],
                                        start=(k == 0), stop=(k == KQ - 1))
            done = self.pe.mark(last)
            m = self.copy(qr[:, half, :], bank.ap[:, 0:MH * MR], done)
            bank.free = [m]
            qr_ready.append(m)
        rm = self.rotate(A, qr.rearrange("p h (n r) -> p h n r", n=MH), MH, qr_ready)
        q_ready, k_ready, v_ready = {h: [] for h in range(MH)}, {h: [] for h in range(MH)}, []
        for b in range(2):
            bank = banks.take()
            self.pe.need(bank.free, rm)
            for half in range(H):
                last = nc.tensor.transpose(bank.ap[:, half * P:(half + 1) * P], qr[:, half, b * P:(b + 1) * P], self.ident)
            done = self.pe.mark(last)
            ms = []
            for i in range(4):
                m = self.copy(qT[MN:MQ, 4 * b + i, :], bank.ap[MR * i:MR * (i + 1), 0:S], done)
                q_ready[4 * b + i].append(m)
                ms.append(m)
            bank.free = ms
        for h in range(MH):
            bank = banks.take()
            self.pe.need(bank.free)
            for k in range(KQ):
                last = nc.tensor.matmul(bank.ap[0:MN, 0:S], wq[:, k, h, 0:MN], cqT[:, k, :], start=(k == 0), stop=(k == KQ - 1))
            done = self.pe.mark(last)
            m = self.copy(qT[0:MN, h, :], bank.ap[0:MN, 0:S], done)
            bank.free = [m]
            q_ready[h].append(m)
            bank = banks.take()
            self.pe.need(bank.free, lat_ready)
            done = self.pe.mark(nc.tensor.matmul(bank.ap[0:MN, :], wkv[:, h, 0:MN], latT, start=True, stop=True))
            m = self.copy(kT[0:MN, h, :], bank.ap[0:MN, :], done)
            bank.free = [m]
            k_ready[h].append(m)
            k_ready[h].append(self.copy(kT[MN:MQ, h, :], krT, lat_ready))
        for kt in range(KT):
            bank = banks.take()
            self.pe.need(bank.free)
            done = self.pe.mark(nc.tensor.matmul(bank.ap, latT[:, kt * P:(kt + 1) * P], wkv[:, :, MN:MN + MV],
                                                 start=True, stop=True))
            m = self.copy(vals[:, kt, :], bank.ap, done)
            bank.free = [m]
            v_ready.append(m)
        u.free = [done]
        NB = MH * H
        DEEP = 3
        pr = [A.take(K) for _ in range(DEEP)]
        pr_free = [[] for _ in range(DEEP)]
        pT = [A.take(KT, S) for _ in range(2)]
        pT_free, pT_ready = [[], []], {}
        neg, tot = A.take(NB), A.take(NB)
        score, soft = {}, {}

        def scores(n):
            h, half = n // H, n % H
            bank = banks.take()
            self.pe.need(bank.free, q_ready[h], k_ready[h])
            done = self.pe.mark(nc.tensor.matmul(bank.ap, qT[0:MQ, h, half * P:(half + 1) * P], kT[0:MQ, h, :],
                                                 start=True, stop=True))
            V.need(done)
            m = V.mark(nc.vector.tensor_reduce(neg[:, n:n + 1], bank.ap, AX.X, ALU.max))
            V.need(m)
            m = V.mark(nc.vector.tensor_scalar(neg[:, n:n + 1], neg[:, n:n + 1], -MSCALE, None, ALU.mult))
            SC.need(m, pr_free[n % DEEP])
            m = SC.mark(nc.scalar.activation(pr[n % DEEP], bank.ap, ACT.Exp, scale=MSCALE, bias=neg[:, n:n + 1],
                                             accum_out=tot[:, n:n + 1]))
            bank.free = [m]
            soft[n] = m

        def turn(n):
            h, half = n // H, n % H
            V.need(soft[n])
            m = V.mark(nc.vector.reciprocal(tot[:, n:n + 1], tot[:, n:n + 1]))
            V.need(m)
            m = V.mark(nc.vector.tensor_scalar(pr[n % DEEP], pr[n % DEEP], tot[:, n:n + 1], None, ALU.mult))
            bank = banks.take()
            self.pe.need(bank.free, m)
            for kt in range(KT):
                last = nc.tensor.transpose(bank.ap[:, kt * P:(kt + 1) * P], pr[n % DEEP][:, kt * P:(kt + 1) * P], self.ident)
            done = self.pe.mark(last)
            pr_free[n % DEEP] = [done]
            m = self.copy(pT[h % 2][:, :, half * P:(half + 1) * P], bank.ap.rearrange("p (a b) -> p a b", a=KT), done, pT_free[h % 2])
            bank.free = [m]
            pT_ready.setdefault(h, []).append(m)

        out_bank = {}

        def values(h):
            if h % 2 == 0:
                out_bank[h // 2] = banks.take()
            bank = out_bank[h // 2]
            self.pe.need(bank.free, pT_ready[h], v_ready)
            r_ = slice(64 * (h % 2), 64 * (h % 2) + 64)
            for kt in range(KT):
                last = nc.tensor.matmul(bank.ap[r_, 0:S], vals[:, kt, h * MV:(h + 1) * MV], pT[h % 2][:, kt, :],
                                        start=(kt == 0), stop=(kt == KT - 1))
            done = self.pe.mark(last)
            pT_free[h % 2] = [done]
            if h % 2:
                V.need(done, ready["mg"])
                m = V.mark(nc.vector.tensor_tensor(yT[:, GH + h // 2, :], bank.ap[:, 0:S], mgT[:, h // 2, :], ALU.mult))
                bank.free = [m]
                y_ready[GH + h // 2] = m

        for n in range(NB + 3):
            if n < NB:
                scores(n)
            if 1 <= n <= NB:
                turn(n - 1)
            if n >= 3 and n % 2 == 1:
                values((n - 3) // 2)

    def odd(self):
        nc, d, A = self.nc, self.d, self.whole
        V, SC = self.v, self.a
        banks = Banks(self.banks)
        NG = 4
        rows_ready = self.affine_rows(d["post_ln_g_2"][1], d["post_ln_b_2"][1], "post_ln1_rows")
        dft_n = A.take(H, 2, S)
        dft_c = A.take(2 * P)
        sgu = A.take(NG, P)
        sgu_b = A.take(NG * P)
        tables = self.load(self.g, [(dft_n, d["k_dft_n"]), (dft_c, d["k_dft_c"]),
                                    (sgu, d["sgu_w_2"][0].rearrange("g t s -> t g s")),
                                    (sgu_b, d["sgu_b_2"][0].rearrange("g t -> (g t)").partition_broadcast(P))], "odd_tables_loaded")
        gate = A.take(D)
        gate_ready = self.gate_row(gate, 1, "gate1_row")
        combine = self.gated_residual([A.take(512) for _ in range(2)], gate, gate_ready)
        sguT = A.take(NG, P)
        bank = banks.take()
        self.pe.need(bank.free, tables)
        for g in range(NG):
            last = nc.tensor.transpose(bank.ap[:, g * P:(g + 1) * P], sgu[:, g, :], self.ident)
        done = self.pe.mark(last)
        sguT_ready = self.copy(sguT.rearrange("p a b -> p (a b)"), bank.ap, done)
        bank.free = [sguT_ready]
        hT = A.take(T, S)
        hT_ready = self.modulated(A, self.x, self.x_ready, self.mod[:, 2, 1, :], self.mod[:, 2, 0, :], self.mod1_ready, hT, banks)
        fT, fgT, uT, sgT = (A.take(NG, S) for _ in range(4))
        v = A.take(H, NG * P)
        ready = {}

        def keep(name, dst_of, func=None):
            def finish(i, psum, done):
                dst = dst_of(i)
                if len(dst.shape) == 3:
                    psum = psum.rearrange("p (a b) -> p a b", a=dst.shape[1])
                if func is None:
                    m = self.copy(dst, psum, done)
                else:
                    SC.need(done)
                    m = SC.mark(nc.scalar.activation(dst, psum, func))
                ready.setdefault(name, []).append(m)
                return m
            return finish

        w_in = d["odd_w_in_2"][0]
        args = (hT, hT_ready, banks)
        tiles = [0, P, 2 * P, 3 * P]
        u, w = self.columns_unit(w_in, 0, 512)
        self.feature_tiles(u, w, tiles, *args, keep("f", lambda i: fT[:, i:i + 2, :]))
        u, w = self.columns_unit(w_in, 1536, 512)
        self.token_tiles(u, w, 0, 512, *args, keep("v", lambda half: v[:, half, :], ACT.Gelu))
        u, w = self.columns_unit(w_in, 1024, 512)
        self.feature_tiles(u, w, tiles, *args, keep("u", lambda i: uT[:, i:i + 2, :], ACT.Gelu))
        u, w = self.columns_unit(w_in, 512, 512)
        self.feature_tiles(u, w, tiles, *args, keep("fg", lambda i: fgT[:, i:i + 2, :], ACT.Silu))
        u, w = self.columns_unit(w_in, 2048, 512)
        self.feature_tiles(u, w, tiles, *args, keep("sg", lambda i: sgT[:, i:i + 2, :], ACT.Silu))
        yT = A.take(T, S)
        y_ready = [None] * T
        stats, mv, rs = A.take(H * NG, 6), A.take(H * NG, 2), A.take(H * NG)
        V.need(ready["v"])
        for i in range(H * NG):
            m = V.mark(nc.vector.bn_stats(stats[:, i, :], v[:, i // NG, (i % NG) * P:(i % NG + 1) * P]))
        V.need(m)
        for i in range(H * NG):
            m = V.mark(nc.vector.bn_aggr(mv[:, i, :], stats[:, i, :]))
        V.need(m)
        var = A.take(H * NG)
        c = V.mark(nc.vector.tensor_copy(var, mv[:, :, 1]))
        r = self.inverse_root(rs, var, 1.0, EPS_SECOND, c)
        V.need(r)
        for i in range(H * NG):
            part = v[:, i // NG, (i % NG) * P:(i % NG + 1) * P]
            m = V.mark(nc.vector.tensor_scalar(part, part, mv[:, i, 0:1], rs[:, i:i + 1], ALU.subtract, ALU.mult))
        v_ready = m
        fc = A.take(H, NG * 2 * P)
        for g in range(NG):
            bank = banks.take()
            self.pe.need(bank.free, ready["f"], tables)
            for half in range(H):
                last = nc.tensor.matmul(bank.ap[:, half * 2 * P:(half + 1) * 2 * P], fT[:, g, half * P:(half + 1) * P], dft_c,
                                        start=True, stop=True)
            done = self.pe.mark(last)
            m = self.copy(fc[:, :, g * 2 * P:(g + 1) * 2 * P], bank.ap.rearrange("p (a b) -> p a b", a=H), done)
            bank.free = [m]
            bank = banks.take()
            self.pe.need(bank.free, m)
            for n in range(4):
                half, cs = n // 2, n % 2
                c0 = g * 2 * P + cs * P
                last = nc.tensor.matmul(bank.ap[:, 0:S], fc[:, half, c0:c0 + P], dft_n[:, half, cs, :], start=(n == 0), stop=(n == 3))
            done = self.pe.mark(last)
            V.need(done, ready["fg"])
            y_ready[g] = V.mark(nc.vector.tensor_tensor(yT[:, g, :], bank.ap[:, 0:S], fgT[:, g, :], ALU.mult))
            bank.free = [y_ready[g]]
        for g in range(NG):
            bank = banks.take()
            self.pe.need(bank.free, v_ready, sguT_ready)
            for half in range(H):
                last = nc.tensor.matmul(bank.ap[:, half * P:(half + 1) * P], v[:, half, g * P:(g + 1) * P], sguT[:, g, :],
                                        start=True, stop=True)
            done = self.pe.mark(last)
            y = yT[:, NG + g, :]
            V.need(done, tables)
            m = V.mark(nc.vector.tensor_tensor(y.rearrange("p (h t) -> p h t", h=H), bank.ap[:, 0:S].rearrange("p (h t) -> p h t", h=H),
                                               sgu_b[:, g * P:(g + 1) * P].unsqueeze(1).to_broadcast([P, H, P]), ALU.add))
            bank.free = [m]
            V.need(m, ready["u"])
            m = V.mark(nc.vector.tensor_tensor(y, y, uT[:, g, :], ALU.mult))
            V.need(m, ready["sg"])
            y_ready[NG + g] = V.mark(nc.vector.tensor_tensor(y, y, sgT[:, g, :], ALU.mult))
        self.product_and_norm(A, yT, y_ready, d["odd_w_out_2"][0], banks, combine, EPS_SECOND, rows_ready)

    def build(self, stop_after=None):
        nc, d = self.nc, self.d
        self.setup()
        self.latT0 = self.sb("context_latents", [P, S])
        self.krT0 = self.sb("context_rotary_keys", [MR, S])
        self.state0 = self.sb("context_states", [P, 2, 2, GV])
        self.axial = self.sb("axial", [P, H, 2, MR // 2])
        self.small2_ready = self.load(self.g, [(self.axial, d["k_axial"])], "axial_loaded")
        self.side.at = 0
        work = self.side_work()
        def rest():
            next(work, None)

        none = lambda: None
        stages = [("attention", lambda: self.attention(rest)), ("moe0", lambda: self.experts(0, rest)), ("recurrent", self.recurrent),
                  ("moe1", lambda: self.experts(1, rest)), ("even", self.even), ("odd", self.odd)]
        for name, stage in stages:
            self.main.at = self.whole.at = 0
            if name == "even":
                for _ in work:
                    pass
                self.meet()
            stage()
            self.meet()
            if stop_after == name:
                break
        stored = self.new_sem("output_stored")
        for half in range(H):
            self.sp.need(self.x_ready[half])
            nc.sync.dma_start(self.out.rearrange("o (h p) d -> p (o h) d", p=P)[:, half, :], self.x[:, half, :]).then_inc(stored, 16)
        nc.sync.wait_ge(stored, 16 * H)


def build(nc, dram, out, stop_after=None):
    with ExitStack() as ctx:
        prog = Program(nc, ctx, dram, out)
        prog.rows_dram = [nc.dram_tensor(f"ada_rows{i}", [2, 3 * D], F32, kind="Internal").ap() for i in range(DEPTH)]
        prog.build(stop_after)


_INS = ['x', 'attn_w_qkv', 'attn_w_o', 'attn_sink', 'lru_w_in', 'lru_conv_w', 'lru_conv_b', 'lru_w_rgate', 'lru_b_rgate',
        'lru_w_igate', 'lru_b_igate', 'lru_lambda', 'lru_w_out', 'moe_w_router', 'moe_w_gate_up', 'moe_w_down', 'ln_mix_g',
        'ln_mix_b', 'ln_ffn_g', 'ln_ffn_b', 'c_2', 'ctx_2', 'c_ctx_2', 'ada_w_2', 'ada_b_2', 'post_ln_g_2', 'post_ln_b_2',
        'even_w_in_2', 'gla_w2_2', 'gla_b_2', 'gla_norm_g_2', 'mla_q_norm_g_2', 'mla_w_uq_2', 'mla_kv_norm_g_2', 'mla_w_ukv_2',
        'even_w_out_2', 'odd_w_in_2', 'sgu_w_2', 'sgu_b_2', 'odd_w_out_2']


def kernel(**inputs):
    import concourse.bacc as bacc
    from concourse.bass_utils import run_bass_kernel_spmd

    nc = bacc.Bacc("TRN2", target_bir_lowering=False, num_devices=1)
    arrays, dram = {}, {}
    for name, a in [(n, np.ascontiguousarray(inputs[n])) for n in _INS] + list(constants().items()):
        arrays[f"in_{name}"] = a
        dram[name] = nc.dram_tensor(f"in_{name}", a.shape, mybir.dt.from_np(a.dtype), kind="ExternalInput").ap()
    out = nc.dram_tensor("out_x", (1, S, D), F32, kind="ExternalOutput").ap()
    build(nc, dram, out)
    result = run_bass_kernel_spmd(nc, [arrays], core_ids=[0])
    return result.results[0]["out_x"]
```

```python
from contextlib import ExitStack

import numpy as np

import concourse.bass as bass
from concourse import mybir

F32 = mybir.dt.float32
U32 = mybir.dt.uint32
F32R = mybir.dt.float32r
ACT = mybir.ActivationFunctionType
ALU = mybir.AluOpType
AX = mybir.AxisListType

P = 128
D = 1024
S = 256
H = S // P
T = D // P
DEPTH = 2
ALPHA = (2 * DEPTH) ** 0.25
EPS_FIRST = 1e-5
EPS_SECOND = 1e-6
UNIT = 4096
SLOTS = 7
TAIL_SLOTS = 3

NQ, NKV, HD = 16, 4, 64
GROUP = NQ // NKV
ROT = HD // 4
WINDOW = 128
QKV = (NQ + 2 * NKV) * HD
NE = 16
CAP = 2 * S // NE
PACK = P // CAP
LB = 4
LBW = D // LB
CW = 4
LRU_C = 8.0
GH, GK, GV, GR, GCH = 4, 64, 128, 16, 64
GTAU = 16.0
NCH = S // GCH
MH, MN, MR, MV = 8, 64, 32, 64
MQ = MN + MR
MSCALE = MQ ** -0.5
QR, KVR = 256, 128
C_GQ, C_GK, C_GV, C_LR, C_GG, C_CQ, C_CKV, C_KR, C_MG = 0, 256, 512, 1024, 1056, 1568, 1824, 1952, 1984
NEG = -1e30


def constants():
    p = np.arange(P)
    token = np.arange(H)[None, :] * P + p[:, None]
    key = np.arange(S)
    out = {"k_ident": np.eye(P, dtype=np.float32)}
    far = np.abs(token[:, :, None] - key[None, None, :]) > WINDOW
    out["k_window"] = np.where(far, np.float32(NEG), np.float32(0)).astype(np.float32)
    inv = np.float32(500000.0) ** (-np.arange(0, ROT, 2, dtype=np.float32) / np.float32(ROT))
    ang = token[:, :, None].astype(np.float32) * inv.astype(np.float32)
    out["k_rope"] = np.stack([np.cos(ang), np.sin(ang)], 2).astype(np.float32)
    out["k_slot"] = np.tile(np.arange(1, CAP + 1, dtype=np.float32), (P, 1))
    t = np.arange(S)
    out["k_reset"] = np.tile(np.stack([t % GCH != 0, t % GCH != GCH - 1]).astype(np.float32), (P, 1, 1))
    s_, t_ = np.arange(P)[:, None], np.arange(P)[None, :]
    same = (s_ // GCH) == (t_ // GCH)
    out["k_tri"] = np.stack([same & (s_ <= t_), same & (s_ >= t_)], 1).astype(np.uint32)
    n_freq = MR // 4
    inv = (np.float32(10000.0) ** (-np.arange(n_freq, dtype=np.float32) / np.float32(n_freq))).astype(np.float32)
    row, col = (token // 64).astype(np.float32), (token % 64).astype(np.float32)
    ang = np.concatenate([row[:, :, None] * inv, col[:, :, None] * inv], -1)
    out["k_axial"] = np.stack([np.cos(ang), np.sin(ang)], 2).astype(np.float32)
    a = 2 * np.pi * ((token[:, :, None] * t[None, None, :]) % S) / S
    out["k_dft_n"] = (np.stack([np.cos(a), np.sin(a)], 2) / np.sqrt(S)).astype(np.float32)
    c = 2 * np.pi * ((p[:, None] * p[None, :]) % P) / P
    out["k_dft_c"] = (np.concatenate([np.cos(c), -np.sin(c)], 1) / np.sqrt(P)).astype(np.float32)
    return out


class Queue:

    def __init__(self, engine, sem):
        self.engine, self.sem, self.count, self.seen = engine, sem, 0, {}

    def need(self, *marks):
        for m in marks:
            if m is None:
                continue
            if isinstance(m, list):
                self.need(*m)
                continue
            sem, value = m
            if value > self.seen.get(id(sem), 0):
                self.engine.wait_ge(sem, value)
                self.seen[id(sem)] = value

    def mark(self, instruction):
        instruction.then_inc(self.sem, 1)
        self.count += 1
        return (self.sem, self.count)

    def last(self):
        return (self.sem, self.count) if self.count else None


class Bank:

    def __init__(self, ap):
        self.ap, self.free = ap, []


class Banks:

    def __init__(self, banks):
        self.banks, self.at = banks, 0

    def take(self):
        self.at += 1
        return self.banks[(self.at - 1) % len(self.banks)]


class Unit:

    def __init__(self, ap, sem):
        self.ap, self.sem, self.fill, self.arrived, self.free = ap, sem, 0, None, []


class Parts:

    def __init__(self, hi, lo, ready, slots=()):
        self.hi, self.lo, self.ready, self.slots = hi, lo, ready, slots

    def at(self, *index):
        return self.hi[index], None if self.lo is None else self.lo[index]

    def read_by(self, mark):
        for s in self.slots:
            s.free = [mark]


class Arena:

    def __init__(self, ap, size):
        self.ap, self.size, self.at = ap, size, 0

    def take(self, *dims):
        n = int(np.prod(dims))
        assert self.at + n <= self.size, ("arena", self.at + n, self.size)
        v = self.ap[:, self.at:self.at + n]
        self.at += n
        if len(dims) == 2:
            return v.rearrange("p (a b) -> p a b", a=dims[0])
        if len(dims) == 3:
            return v.rearrange("p (a b c) -> p a b c", a=dims[0], b=dims[1])
        return v


class Program:
    MAIN, SIDE = 13088, 4912

    def __init__(self, nc, ctx, dram, out):
        self.nc, self.ctx, self.d, self.out = nc, ctx, dram, out
        sem = lambda n: ctx.enter_context(nc.semaphore(n))
        self.new_sem = sem
        self.pe = Queue(nc.tensor, sem("tensor_steps"))
        self.v = Queue(nc.vector, sem("vector_steps"))
        self.a = Queue(nc.scalar, sem("scalar_steps"))
        self.g = Queue(nc.gpsimd, sem("gpsimd_steps"))
        self.sp = Queue(nc.sync, sem("sync_steps"))
        self.banks = [Bank(ctx.enter_context(nc.psum_tensor(f"bank{i}", [P, 512], F32))[:, :]) for i in range(8)]
        self.twins = {}
        ring = self.with_twins("weight_ring", SLOTS, UNIT)
        self.slots = [Unit(ring[:, i * UNIT:(i + 1) * UNIT], sem(f"slot{i}_filled")) for i in range(SLOTS)]
        self.spares = None
        self.unit_at = 0
        work = self.with_twins("work", 1, self.MAIN + self.SIDE)
        self.main = Arena(work[:, 0:self.MAIN], self.MAIN)
        self.side = Arena(work[:, self.MAIN:], self.SIDE)
        self.whole = Arena(work[:, :], self.MAIN + self.SIDE)
        self.tail = Arena(ring[:, TAIL_SLOTS * UNIT:], (SLOTS - TAIL_SLOTS) * UNIT)
        self.x = self.sb("x_tokens", [P, H, D])
        self.x_ready = []
        self.flip = 0

    def with_twins(self, name, pieces, n):
        at = -(-self.nc.sbuf_base // 32) * 32
        t = self.ctx.enter_context(self.nc.sbuf_tensor(name, [P, pieces * n], F32))
        self.twins[t.name] = n, [self.nc.alloc_sbuf_tensor_at(f"{name}{i}_rounded", [P, n], F32R, offset=at + 4 * i * n)
                                 for i in range(pieces)]
        return t

    def rounded(self, x):
        n, twins = self.twins[x.tensor.name]
        dims = [list(d) for d in x.ap]
        assert dims[0] == [n * len(twins), P]
        return bass.AP(tensor=twins[x.offset // n], offset=x.offset % n, ap=[[n, P]] + dims[1:])

    def sb(self, name, shape, dt=F32):
        t = self.ctx.enter_context(self.nc.sbuf_tensor(name, shape, dt))
        return t[tuple(slice(None) for _ in shape)]


    def load(self, queue, pairs, name):
        s = self.new_sem(name)
        for dst, src in pairs:
            queue.engine.dma_start(dst, src).then_inc(s, 16)
        return (s, 16 * len(pairs))

    def next_slot(self):
        self.unit_at += 1
        return self.slots[(self.unit_at - 1) % len(self.slots)]

    def unit(self, parts):
        slot = self.next_slot()
        self.sp.need(slot.free)
        for dst, src in parts(slot.ap):
            self.nc.sync.dma_start(dst, src).then_inc(slot.sem, 16)
            slot.fill += 16
        slot.arrived = (slot.sem, slot.fill)
        return slot

    def spare(self):
        return self.spares.take() if self.spares else self.next_slot()

    def split(self, hi, x, marks, pieces, on_vector=False):
        nc, out = self.nc, []
        lo = self.rounded(x)
        n = x.shape[-1] // pieces
        for i in range(pieces):
            c = slice(i * n, (i + 1) * n)
            m = self.copy(hi[:, c], x[:, c], marks, on_scalar=not on_vector)
            self.v.need(marks, m)
            out.append(self.v.mark(nc.vector.tensor_tensor(lo[:, c], x[:, c], hi[:, c], ALU.subtract)))
        return lo, out

    def split_unit(self, u, t, c, on_vector=False):
        s = self.spare()
        (self.v if on_vector else self.a).need(s.free)
        hi = self.rounded(s.ap[:, 0:t * c])
        lo, marks = self.split(hi, u.ap[:, 0:t * c], u.arrived, t // 2, on_vector)
        shape = lambda ap: ap.rearrange("p (t c) -> p t c", t=t)
        return Parts(shape(hi), shape(lo), [marks[i // 2] for i in range(t)], [u, s])

    def product(self, out, stationary, moving, start, stop):
        (sh, sl), (mh, ml) = stationary, moving
        nc = self.nc
        if sl is None:
            return nc.tensor.matmul(out, sh, mh, start=start, stop=stop)
        nc.tensor.matmul(out, sl, mh, start=start, stop=False)
        nc.tensor.matmul(out, sh, ml, start=False, stop=False)
        return nc.tensor.matmul(out, sh, mh, start=False, stop=stop)

    def weights(self, w, *ranges, whole=False, on_vector=False):
        src = w.rearrange("(p t) n -> p t n", t=T)
        c = sum(n for _, n in ranges)

        def parts(slot):
            view, at, out = slot[:, 0:T * c].rearrange("p (t c) -> p t c", t=T), 0, []
            for c0, n in ranges:
                out.append((view[:, :, at:at + n], src[:, :, c0:c0 + n]))
                at += n
            return out

        u = self.unit(parts)
        if whole:
            return Parts(u.ap[:, 0:T * c].rearrange("p (t c) -> p t c", t=T), None, [u.arrived] * T, [u])
        return self.split_unit(u, T, c, on_vector)

    def out_weights(self, w):
        src = w.rearrange("(t p) n -> p t n", p=P)
        units = [self.unit(lambda slot: [(slot.rearrange("p (t c) -> p t c", t=T), src[:, :, c * 512:(c + 1) * 512])])
                 for c in range(2)]
        return [Parts(u.ap.rearrange("p (t c) -> p t c", t=T), None, [u.arrived] * T, [u]) for u in units]

    def columns_unit(self, w, c0, c):
        src = w.rearrange("(p t) n -> p t n", t=T)
        box = []

        def parts(slot):
            view = slot[:, 0:T * c].rearrange("p (t c) -> p t c", t=T)
            box.append(view)
            return [(view, src[:, :, c0:c0 + c])]

        u = self.unit(parts)
        return u, box[0]

    def either(self):
        self.flip ^= 1
        return self.flip

    def copy(self, dst, src, *marks, on_scalar=None, scale=None):
        if self.either() if on_scalar is None else on_scalar:
            self.a.need(*marks)
            if scale is None:
                return self.a.mark(self.nc.scalar.copy(dst, src))
            return self.a.mark(self.nc.scalar.activation(dst, src, ACT.Identity, scale=scale))
        self.v.need(*marks)
        if scale is None:
            return self.v.mark(self.nc.vector.tensor_copy(dst, src))
        return self.v.mark(self.nc.vector.tensor_scalar(dst, src, scale, None, ALU.mult))

    def meet(self):
        marks = [q.last() for q in (self.pe, self.v, self.a, self.g)]
        for q in (self.pe, self.v, self.a, self.g):
            q.need(*marks)

    def to_features(self, src, dst, marks, banks, evacuate=None, parts=None):
        nc, out = self.nc, []
        n = dst.shape[1]
        taken = [banks.take() for _ in range(0, n, 2)]
        assert len({id(b) for b in taken}) == len(taken)
        done_of = {}
        for half in range(H):
            self.pe.need(self.ident_ready, marks[half] if len(marks) == H and isinstance(marks, list) else marks)
            for t0 in range(0, n, 2):
                bank = taken[t0 // 2]
                self.pe.need(bank.free)
                for t in range(t0, min(t0 + 2, n)):
                    o = (t - t0) * S + half * P
                    last = nc.tensor.transpose(bank.ap[:, o:o + P], src(half, t), self.ident)
                done_of[t0] = self.pe.mark(last)
        for t0 in range(0, n, 2):
            bank, done = taken[t0 // 2], done_of[t0]
            pair = min(2, n - t0)
            if parts is not None:
                flat = lambda x: x[:, t0:t0 + pair, :].rearrange("p a b -> p (a b)")
                m = self.psum_parts(flat(dst), flat(parts), bank.ap[:, 0:pair * S], done)
                bank.free = [m]
                out += [m] * pair
            elif evacuate is None:
                m = self.copy(dst[:, t0:t0 + pair, :].rearrange("p a b -> p (a b)"), bank.ap[:, 0:pair * S], done)
                bank.free = [m]
                out += [m] * pair
            else:
                ms = [evacuate(t, bank.ap[:, (t - t0) * S:(t - t0 + 1) * S], done) for t in range(t0, t0 + pair)]
                bank.free = ms
                out += ms
        return out

    def inverse_root(self, dst, src, scale, eps, marks):
        nc = self.nc
        self.v.need(marks)
        m = self.v.mark(nc.vector.tensor_scalar(src, src, scale, eps, ALU.mult, ALU.add))
        self.g.need(m, self.half_ready)
        n = src.shape[-1]
        return self.g.mark(nc.gpsimd.tensor_tensor(dst, src, self.minus_half[:, 0:n], ALU.pow))

    def moments(self, arena, src, marks):
        nc = self.nc
        stats = arena.take(H, 12)
        mv = arena.take(H, 2)
        out = []
        for half in range(H):
            self.v.need(marks[half])
            for c in range(2):
                m = self.v.mark(nc.vector.bn_stats(stats[:, half, 6 * c:6 * c + 6], src[:, half, c * 512:(c + 1) * 512]))
            self.v.need(m)
            out.append(self.v.mark(nc.vector.bn_aggr(mv[:, half, :], stats[:, half, :])))
        return mv, out

    def affine_rows(self, g_row, b_row, name):
        self.a.need(self.rows_free)
        return self.load(self.a, [(self.gain, g_row.partition_broadcast(P)), (self.bias, b_row.partition_broadcast(P))], name)

    def norm_space(self, arena):
        return arena.take(H, 12), arena.take(H, 2), arena.take(H), arena.take(H)

    def chunk_moments(self, space, half, c, mark):
        self.v.need(mark)
        self.moment_marks[half, c] = self.v.mark(self.nc.vector.bn_stats(
            space[0][:, half, 6 * c:6 * c + 6], self.x[:, half, c * 512:(c + 1) * 512]))

    def norm_half(self, space, half, eps, rows_ready):
        nc, v = self.nc, self.v
        stats, mv, var, rstd = space
        v.need(self.moment_marks[half, 0], self.moment_marks[half, 1])
        m = v.mark(nc.vector.bn_aggr(mv[:, half, :], stats[:, half, :]))
        v.need(m)
        e = v.mark(nc.vector.tensor_scalar(var[:, half:half + 1], mv[:, half, 1:2], eps, None, ALU.add))
        self.g.need(e, self.half_ready)
        r = self.g.mark(nc.gpsimd.tensor_tensor(rstd[:, half:half + 1], var[:, half:half + 1], self.minus_half[:, 0:1], ALU.pow))
        v.need(rows_ready)
        f = v.mark(nc.vector.scalar_tensor_tensor(self.x[:, half, :], self.x[:, half, :], mv[:, half, 0:1], self.gain,
                                                  ALU.subtract, ALU.mult))
        v.need(f, r)
        f = v.mark(nc.vector.scalar_tensor_tensor(self.x[:, half, :], self.x[:, half, :], rstd[:, half:half + 1], self.bias,
                                                  ALU.mult, ALU.add))
        self.x_ready[half] = f
        self.rows_free = [f]

    def product_and_norm(self, arena, y, weights, banks, combine, eps, rows_ready):
        space = self.norm_space(arena)
        for half in range(H):
            for c, w in enumerate(weights):
                bank = banks.take()
                self.pe.need(bank.free)
                for j in range(T):
                    self.pe.need(y.ready[j], w.ready[j])
                    last = self.product(bank.ap, y.at(slice(None), j, slice(half * P, (half + 1) * P)),
                                        w.at(slice(None), j), start=(j == 0), stop=(j == T - 1))
                done = self.pe.mark(last)
                w.read_by(done)
                m = combine(half, c, bank.ap, done)
                bank.free = [m]
                self.chunk_moments(space, half, c, m)
            self.norm_half(space, half, eps, rows_ready)

    def split_tiles(self, hi, x, marks):
        lo, ready = self.rounded(x), []
        for t in range(0, x.shape[1], 2):
            both = slice(t, t + 2)
            self.a.need(marks[t], marks[t + 1])
            m = self.a.mark(self.nc.scalar.copy(hi[:, both, :], x[:, both, :]))
            self.v.need(marks[t], marks[t + 1], m)
            ready += [self.v.mark(self.nc.vector.tensor_tensor(lo[:, both, :], x[:, both, :], hi[:, both, :], ALU.subtract))] * 2
        return Parts(hi, lo, ready)

    def psum_parts(self, hi, lo, psum, *marks):
        self.a.need(*marks)
        m = self.a.mark(self.nc.scalar.copy(hi, psum))
        self.v.need(m, *marks)
        return self.v.mark(self.nc.vector.tensor_tensor(lo, psum, hi, ALU.subtract))

    def take_parts(self, arena, *dims):
        return self.rounded(arena.take(*dims)), self.rounded(arena.take(*dims))

    def x_features(self, arena, banks):
        hi, lo = self.take_parts(arena, T, S)
        ready = self.to_features(lambda half, t: self.x[:, half, t::T], hi, self.x_ready, banks, parts=lo)
        return Parts(hi, lo, ready)

    def residual(self, half, c, psum, done):
        self.v.need(done, self.x_ready[half])
        xs = self.x[:, half, c * 512:(c + 1) * 512]
        return self.v.mark(self.nc.vector.scalar_tensor_tensor(xs, xs, ALPHA, psum, ALU.mult, ALU.add))


    def setup(self):
        nc, d = self.nc, self.d
        self.ident = self.sb("ident", [P, P])
        self.gain = self.sb("norm_gain", [P, D])
        self.bias = self.sb("norm_bias", [P, D])
        self.rows_free, self.moment_marks = [], {}
        self.minus_half = self.sb("minus_half", [P, 8])
        self.sink = self.sb("sink", [P, NQ])
        self.rope = self.sb("rope", [P, H, 2, ROT // 2])
        self.slot_no = self.sb("slot_numbers", [P, CAP])
        self.router = self.sb("router", [P, DEPTH, T, NE])
        self.columns = self.sb("parameter_columns", [P, 96])
        self.parameter_rows = self.sb("parameter_rows", [P, P])
        self.ident_ready = self.load(self.sp, [(self.ident, d["k_ident"])], "ident_loaded")
        x_rows = d["x"].rearrange("o (h p) d -> p (o h) d", p=P)
        self.x_ready = [self.load(self.sp, [(self.x[:, half, :], x_rows[:, half, :])], f"x{half}_loaded") for half in range(H)]
        self.half_ready = self.g.mark(nc.gpsimd.memset(self.minus_half, -0.5))
        self.small_ready = self.load(self.a, [
            (self.sink, d["attn_sink"].rearrange("o h -> (o h)").partition_broadcast(P)),
            (self.rope, d["k_rope"]),
            (self.slot_no, d["k_slot"]),
            (self.router, d["moe_w_router"].rearrange("l (p t) e -> p l t e", t=T)),
        ], "small_loaded")


    def attention(self, rest):
        nc, d, A = self.nc, self.d, self.whole
        banks = Banks(self.banks[0:6])
        window = A.take(H, S)
        window_ready = self.load(self.a, [(window, d["k_window"])], "window_loaded")
        rows_ready = self.affine_rows(d["ln_mix_g"][0], d["ln_mix_b"][0], "ln_mix0_rows")
        x_room = A.ap[:, A.at:A.at + T * S].rearrange("p (t s) -> p t s", t=T)
        x = self.x_features(A, banks)
        rest()
        qkv = A.take(H, QKV)
        qkv_ready = []
        def take_qkv(c):
            def finish(half, psum, done):
                dst = qkv[:, half, c * 512:(c + 1) * 512]
                if c < 2:
                    dst = dst.rearrange("p (g i d) -> p i g d", g=GROUP, i=2)
                    psum = psum.rearrange("p (i g d) -> p i g d", g=GROUP, i=2)
                qkv_ready.append(self.copy(dst, psum, done))
                return qkv_ready[-1]
            return lambda w: self.token_tiles(w, 0, 512, x, banks, finish)
        self.projections([(d["attn_w_qkv"][0], [(c * 512, 512)], take_qkv(c)) for c in range(QKV // 512)])
        NR = NQ + NKV
        turned = []
        tmp = [A.take(NR, ROT // 2) for _ in range(4)]
        for half in range(H):
            heads = qkv[:, half, 0:NR * HD].rearrange("p (h d) -> p h d", d=HD)
            lo, hi = heads[:, :, 0:ROT // 2], heads[:, :, ROT // 2:ROT]
            cos = self.rope[:, half, 0:1, :].to_broadcast([P, NR, ROT // 2])
            sin = self.rope[:, half, 1:2, :].to_broadcast([P, NR, ROT // 2])
            self.v.need(qkv_ready, self.small_ready, self.v.last())
            for dst, a, b in ((tmp[0], lo, cos), (tmp[1], hi, sin), (tmp[2], hi, cos), (tmp[3], lo, sin)):
                m = self.v.mark(nc.vector.tensor_tensor(dst, a, b, ALU.mult))
            self.v.need(m)
            self.v.mark(nc.vector.tensor_tensor(lo, tmp[0], tmp[1], ALU.subtract))
            turned.append(self.v.mark(nc.vector.tensor_tensor(hi, tmp[2], tmp[3], ALU.add)))
        qT = A.take(2 * GROUP, S)
        kT = A.take(2, S)
        kv = qkv[:, :, NQ * HD:(NQ + NKV) * HD].rearrange("p h (m c) -> p h m c", m=2)
        kT_ready = self.to_features(lambda half, m: kv[:, half, m, :], kT, turned, banks)
        qT_ready = self.to_features(lambda half, t: qkv[:, half, t * P:(t + 1) * P], qT, turned, banks)
        vals = qkv[:, :, (NQ + NKV) * HD:]
        o = Parts(x_room, None, [None] * T)
        DEEP = 3
        sm = [A.take(H, S) for _ in range(DEEP)]
        pT = [A.take(H, S) for _ in range(2)]
        neg_max, total, at_sink, den = (A.take(NQ, H) for _ in range(4))
        sm_free, pT_free = [[] for _ in range(DEEP)], [[], []]
        soft, score, turned_p, out_bank = {}, {}, {}, {}

        def scores(h):
            m, i, g = h // 8, (h // GROUP) % 2, h % GROUP
            bank = banks.take()
            self.pe.need(bank.free, qT_ready[m * GROUP + g], kT_ready[m])
            for half in range(H):
                r = slice(64 * i, 64 * i + 64)
                last = nc.tensor.matmul(bank.ap[:, half * S:(half + 1) * S],
                                        qT[r, m * GROUP + g, half * P:(half + 1) * P], kT[r, m, :],
                                        start=True, stop=True)
            score[h] = (bank, self.pe.mark(last))

        def softmax(h):
            bank, done = score[h]
            s = sm[h % DEEP]
            self.v.need(done, window_ready, sm_free[h % DEEP])
            m = self.v.mark(nc.vector.scalar_tensor_tensor(s, bank.ap.rearrange("p (h k) -> p h k", h=H), HD ** -0.5,
                                                           window, ALU.mult, ALU.add))
            bank.free = [m]
            self.v.need(m)
            m = self.v.mark(nc.vector.tensor_reduce(neg_max[:, h, :], s, AX.X, ALU.max))
            self.v.need(m)
            m = self.v.mark(nc.vector.tensor_scalar(neg_max[:, h, :], neg_max[:, h, :], self.sink[:, h:h + 1], -1.0,
                                                    ALU.max, ALU.mult))
            self.a.need(m)
            for half in range(H):
                e = self.a.mark(nc.scalar.activation(s[:, half, :], s[:, half, :], ACT.Exp, bias=neg_max[:, h, half:half + 1],
                                                     accum_out=total[:, h, half:half + 1]))
            e = self.a.mark(nc.scalar.activation(at_sink[:, h, :], neg_max[:, h, :], ACT.Exp, bias=self.sink[:, h:h + 1]))
            soft[h] = e

        def normalise(h):
            s = sm[h % DEEP]
            self.v.need(soft[h])
            m = self.v.mark(nc.vector.tensor_tensor(den[:, h, :], total[:, h, :], at_sink[:, h, :], ALU.add))
            self.v.need(m)
            m = self.v.mark(nc.vector.reciprocal(den[:, h, :], den[:, h, :]))
            self.v.need(m)
            for half in range(H):
                m = self.v.mark(nc.vector.tensor_scalar(s[:, half, :], s[:, half, :], den[:, h, half:half + 1], None, ALU.mult))
            soft[h] = m

        def turn(h):
            s = sm[h % DEEP]
            bank = banks.take()
            self.pe.need(bank.free, soft[h])
            for kk in range(H):
                for half in range(H):
                    o = kk * S + half * P
                    last = nc.tensor.transpose(bank.ap[:, o:o + P], s[:, half, kk * P:(kk + 1) * P], self.ident)
            done = self.pe.mark(last)
            sm_free[h % DEEP] = [done]
            m = self.copy(pT[h % 2].rearrange("p a b -> p (a b)"), bank.ap, done, pT_free[h % 2])
            bank.free = [m]
            turned_p[h] = m

        def values(h):
            kvh = h // GROUP
            if h % 2 == 0:
                out_bank[h // 2] = banks.take()
            bank = out_bank[h // 2]
            self.pe.need(bank.free, turned_p[h])
            r = slice(64 * (h % 2), 64 * (h % 2) + 64)
            for kk in range(H):
                last = nc.tensor.matmul(bank.ap[r, 0:S], vals[:, kk, kvh * HD:(kvh + 1) * HD], pT[h % 2][:, kk, :],
                                        start=(kk == 0), stop=(kk == H - 1))
            done = self.pe.mark(last)
            pT_free[h % 2] = [done]
            if h % 2:
                m = self.copy(o.hi[:, h // 2, :], bank.ap[:, 0:S], done)
                bank.free = [m]
                o.ready[h // 2] = m

        for h in range(NQ + 3):
            if h < NQ:
                scores(h)
            if 2 <= h < NQ + 2:
                normalise(h - 2)
            if 1 <= h <= NQ:
                softmax(h - 1)
            if 2 <= h < NQ + 2:
                turn(h - 2)
            if h >= 3:
                values(h - 3)
            rest()
        assert A.at + 32 <= self.MAIN + self.SIDE - 3 * D
        weights = self.out_weights(d["attn_w_o"][0])
        self.product_and_norm(A, o, weights, banks, self.residual, EPS_FIRST, rows_ready)


    def experts(self, layer, rest):
        nc, d, A = self.nc, self.d, self.main
        banks = Banks(self.banks[0:5])
        rows_ready = self.affine_rows(d["ln_ffn_g"][layer], d["ln_ffn_b"][layer], f"ln_ffn{layer}_rows")
        xT = A.take(T, S)
        xT_ready = self.to_features(lambda half, t: self.x[:, half, t::T], xT, self.x_ready, banks)
        outs_room = A.take(2, D)
        x_hi = self.rounded(outs_room)
        x_lo = self.rounded(xT.rearrange("p t s -> p (t s)").rearrange("p (h d) -> p h d", h=H))
        hi_ready, lo_ready = [], []
        for half in range(H):
            self.a.need(self.x_ready[half])
            hi_ready.append(self.a.mark(nc.scalar.copy(x_hi[:, half, :], self.x[:, half, :])))
        bank = banks.take()
        self.pe.need(bank.free, xT_ready, self.small_ready)
        for half in range(H):
            for t in range(T):
                last = nc.tensor.matmul(bank.ap[:, half * NE:(half + 1) * NE], xT[:, t, half * P:(half + 1) * P],
                                        self.router[:, layer, t, :], start=(t == 0), stop=(t == T - 1))
        done = self.pe.mark(last)
        aff = A.take(H, NE)
        top, tot = A.take(H), A.take(H)
        self.v.need(done)
        m = self.v.mark(nc.vector.tensor_reduce(top, bank.ap[:, 0:H * NE].rearrange("p (h e) -> p h e", h=H), AX.X, ALU.max,
                                                negate=True))
        self.v.need(hi_ready, self.x_ready)
        low = lambda half: lo_ready.append(self.v.mark(nc.vector.tensor_tensor(x_lo[:, half, :], self.x[:, half, :], x_hi[:, half, :],
                                                                               ALU.subtract)))
        low(0)
        self.a.need(m)
        for half in range(H):
            m = self.a.mark(nc.scalar.activation(aff[:, half, :], bank.ap[:, half * NE:(half + 1) * NE], ACT.Exp,
                                                 bias=top[:, half:half + 1], accum_out=tot[:, half:half + 1]))
        bank.free = [m]
        self.v.need(m)
        m = self.v.mark(nc.vector.reciprocal(tot, tot))
        self.v.need(m)
        for half in range(H):
            m = self.v.mark(nc.vector.tensor_scalar(aff[:, half, :], aff[:, half, :], tot[:, half:half + 1], None, ALU.mult))
        aff_ready = m
        low(1)
        bank = banks.take()
        self.pe.need(bank.free, aff_ready)
        for half in range(H):
            last = nc.tensor.transpose(bank.ap[0:NE, half * P:(half + 1) * P], aff[:, half, :], self.ident)
        done = self.pe.mark(last)
        left, count, ones = A.take(S), A.take(S), A.take(S)
        best = A.take(8)
        one_m = self.v.mark(nc.vector.memset(ones[0:NE, :], 1.0))
        self.v.need(done)
        m = self.v.mark(nc.vector.tensor_copy(left[0:NE, :], bank.ap[0:NE, 0:S]))
        bank.free = [m]
        for _ in range(CAP // 8):
            self.v.need(m)
            m = self.v.mark(nc.vector.max(best[0:NE, :], left[0:NE, :]))
            self.v.need(m)
            m = self.v.mark(nc.vector.match_replace(left[0:NE, :], best[0:NE, :], left[0:NE, :], -1.0))
        self.v.need(m)
        m = self.v.mark(nc.vector.tensor_scalar(left[0:NE, :], left[0:NE, :], 0.0, None, ALU.is_lt))
        self.v.need(m, one_m)
        m = self.v.mark(nc.vector.tensor_tensor_scan(count[0:NE, :], ones[0:NE, :], left[0:NE, :], 0.0, ALU.mult, ALU.add))
        self.v.need(m)
        m = self.v.mark(nc.vector.tensor_tensor(count[0:NE, :], count[0:NE, :], left[0:NE, :], ALU.mult))
        bank = banks.take()
        self.pe.need(bank.free, m)
        for half in range(H):
            last = nc.tensor.transpose(bank.ap[:, half * NE:(half + 1) * NE], count[0:NE, half * P:(half + 1) * P],
                                       self.ident[0:NE, 0:NE])
        done = self.pe.mark(last)
        slot = A.take(H, NE)
        self.v.need(done)
        m = self.v.mark(nc.vector.tensor_copy(slot.rearrange("p a b -> p (a b)"), bank.ap[:, 0:H * NE]))
        bank.free = [m]
        hot, gated = self.rounded(A.take(H, NE * CAP)), A.take(H, NE * CAP)
        self.v.need(m, self.small_ready)
        for half in range(H):
            view = hot[:, half, :].rearrange("p (e c) -> p e c", e=NE)
            m = self.v.mark(nc.vector.tensor_tensor(view, self.slot_no.unsqueeze(1).to_broadcast([P, NE, CAP]),
                                                    slot[:, half, :].unsqueeze(2).to_broadcast([P, NE, CAP]), ALU.is_equal))
        hot_ready = m
        self.v.need(m)
        for half in range(H):
            m = self.v.mark(nc.vector.tensor_tensor(
                gated[:, half, :].rearrange("p (e c) -> p e c", e=NE), hot[:, half, :].rearrange("p (e c) -> p e c", e=NE),
                aff[:, half, :].unsqueeze(2).to_broadcast([P, NE, CAP]), ALU.mult))
        gated_ready = m
        xs = A.take(T, NE * CAP)
        xs_ready = []
        for t in range(T):
            bank = banks.take()
            self.pe.need(bank.free, hot_ready)
            self.pe.need(lo_ready)
            for half in range(H):
                nc.tensor.matmul(bank.ap, x_lo[:, half, t::T], hot[:, half, :], start=(half == 0), stop=False)
                last = nc.tensor.matmul(bank.ap, x_hi[:, half, t::T], hot[:, half, :], start=False, stop=(half == H - 1))
            done = self.pe.mark(last)
            m = self.copy(xs[:, t, :], bank.ap, done)
            bank.free = [m]
            xs_ready.append(m)
        gathered = done
        back = xT[:, 0:NE // PACK, :]
        back_ready = self.to_features(lambda half, g: gated[:, half, g * P:(g + 1) * P], back, gated_ready, banks)
        self.v.need(gathered)
        scaled = [self.v.mark(nc.vector.tensor_scalar(self.x[:, half, :], self.x[:, half, :], ALPHA, None, ALU.mult))
                  for half in range(H)]
        sum_ready = {(half, c): scaled[half] for half in range(H) for c in range(2)}
        up_banks, turn_bank, down_bank = Banks(self.banks[0:2]), self.banks[2], self.banks[3]
        add_banks = [self.banks[4], self.banks[0]]
        space = self.norm_space(A)
        silu = [A.take(S) for _ in range(2)]
        act = [A.take(S) for _ in range(2)]
        actT = [A.take(2, P) for _ in range(2)]
        outs = [outs_room[:, i, :] for i in range(2)]
        silu_free, act_free, actT_free, outs_free = [[], []], [[], []], [[], []], [[], []]
        wgu, wd = d["moe_w_gate_up"][layer], d["moe_w_down"][layer]
        QC = D // PACK
        for e in range(NE):
            i = e % 2
            up = up_banks.take()
            self.pe.need(up.free)
            rows = wgu[e].rearrange("(p t) n -> p t n", t=T)
            for k in range(T // 2):
                u = self.unit(lambda slot: [(slot.rearrange("p (t n) -> p t n", t=2), rows[:, 2 * k:2 * k + 2, :])])
                self.pe.need(u.arrived)
                w = u.ap.rearrange("p (t a j c) -> p t a j c", t=2, a=2, j=PACK)
                for tt in range(2):
                    t = 2 * k + tt
                    self.pe.need(xs_ready[t])
                    for j in range(PACK):
                        last = nc.tensor.matmul(up.ap[CAP * j:CAP * (j + 1), :], xs[:, t, e * CAP:(e + 1) * CAP],
                                                w[:, tt, :, j, :], start=(t == 0), stop=(t == T - 1))
                done = self.pe.mark(last)
                u.free = [done]
                if k % 2:
                    rest()
            self.a.need(done, silu_free[i])
            sm = self.a.mark(nc.scalar.activation(silu[i], up.ap[:, 0:QC], ACT.Silu))
            self.v.need(sm, done, act_free[i])
            am = self.v.mark(nc.vector.tensor_tensor(act[i], silu[i], up.ap[:, QC:2 * QC], ALU.mult))
            up.free, silu_free[i] = [sm, am], [am]
            self.pe.need(am, turn_bank.free)
            for s in range(2):
                last = nc.tensor.transpose(turn_bank.ap[:, s * P:(s + 1) * P], act[i][:, s::2], self.ident)
            done = self.pe.mark(last)
            act_free[i] = [done]
            tm = self.copy(actT[i].rearrange("p a b -> p (a b)"), turn_bank.ap[:, 0:2 * P], done, actT_free[i], on_scalar=True)
            turn_bank.free = [tm]
            down_rows = wd[e].rearrange("(j c s) n -> c j (s n)", j=PACK, s=2)
            self.pe.need(tm, down_bank.free)
            for k in range(2):
                u = self.unit(lambda slot: [(slot.rearrange("p (j n) -> p j n", j=2), down_rows[:, 2 * k:2 * k + 2, :])])
                self.pe.need(u.arrived)
                w = u.ap.rearrange("p (j s q n) -> p j s q n", j=2, s=2, q=PACK)
                for jj in range(2):
                    for s in range(2):
                        j = 2 * k + jj
                        for q in range(PACK):
                            last = nc.tensor.matmul(down_bank.ap[CAP * q:CAP * (q + 1), 0:QC], actT[i][:, s, j * CAP:(j + 1) * CAP],
                                                    w[:, jj, s, q, :], start=(j == 0 and s == 0), stop=(j == 3 and s == 1))
                done = self.pe.mark(last)
                u.free = [done]
            actT_free[i] = [done]
            grp, r = e // PACK, e % PACK
            o = outs[grp % 2]
            ms = [self.copy(o[CAP * r:CAP * (r + 1), q * QC:(q + 1) * QC], down_bank.ap[CAP * q:CAP * (q + 1), 0:QC], done,
                            outs_free[grp % 2], on_scalar=q % 2) for q in range(PACK)]
            down_bank.free = ms
            if r == 0:
                outs_ready = []
            outs_ready += ms
            rest()
            if r == PACK - 1:
                for half in range(H):
                    for c in range(2):
                        add_bank = add_banks[c]
                        self.pe.need(outs_ready, add_bank.free, back_ready)
                        done = self.pe.mark(nc.tensor.matmul(add_bank.ap, back[:, grp, half * P:(half + 1) * P],
                                                             o[:, c * 512:(c + 1) * 512], start=True, stop=True))
                        xsum = self.x[:, half, c * 512:(c + 1) * 512]
                        self.v.need(done, sum_ready[half, c])
                        m = self.v.mark(nc.vector.tensor_tensor(xsum, xsum, add_bank.ap, ALU.add))
                        add_bank.free = [m]
                        sum_ready[half, c] = m
                        if e == NE - 1:
                            self.chunk_moments(space, half, c, m)
                    if e == NE - 1:
                        self.norm_half(space, half, EPS_FIRST, rows_ready)
                outs_free[grp % 2] = [done]


    def recurrent(self):
        nc, d, A = self.nc, self.d, self.whole
        banks = Banks(self.banks)
        V, SC, G = self.v, self.a, self.g
        col = lambda name, i: self.columns[:, self.col[name] + i:self.col[name] + i + 1]
        rows_ready = self.affine_rows(d["ln_mix_g"][1], d["ln_mix_b"][1], "ln_mix1_rows")
        lam = self.columns[:, self.col["lam"]:self.col["lam"] + 16]
        ex, sq, acc, decay, growth = (A.take(16) for _ in range(5))
        SC.need(self.columns_ready)
        m = SC.mark(nc.scalar.activation(ex, lam, ACT.Abs))
        SC.need(m)
        m = SC.mark(nc.scalar.activation(ex, ex, ACT.Exp, scale=-1.0))
        V.need(m)
        m = V.mark(nc.vector.tensor_scalar(sq, ex, 2.0, None, ALU.add))
        V.need(m)
        m = V.mark(nc.vector.reciprocal(sq, sq))
        V.need(m)
        m = V.mark(nc.vector.tensor_tensor(ex, ex, sq, ALU.mult))
        V.need(m)
        m = V.mark(nc.vector.tensor_tensor(sq, ex, ex, ALU.mult))
        V.need(m)
        m = V.mark(nc.vector.tensor_scalar(acc, sq, 1.0 / 19, None, ALU.mult))
        for n in (17, 15, 13, 11, 9, 7, 5, 3):
            V.need(m)
            m = V.mark(nc.vector.scalar_tensor_tensor(acc, acc, 1.0 / n, sq, ALU.add, ALU.mult))
        V.need(m)
        m = V.mark(nc.vector.scalar_tensor_tensor(acc, acc, 1.0, ex, ALU.add, ALU.mult))
        m2 = V.mark(nc.vector.tensor_scalar(decay, lam, -1.0, 0.0, ALU.mult, ALU.max))
        V.need(m, m2)
        m = V.mark(nc.vector.scalar_tensor_tensor(acc, acc, 2.0, decay, ALU.mult, ALU.add))
        V.need(m)
        V.mark(nc.vector.tensor_scalar(decay, acc, -LRU_C, None, ALU.mult))
        decay_ready = V.mark(nc.vector.tensor_scalar(growth, acc, LRU_C, None, ALU.mult))
        x = self.x_features(A, banks)
        padded = A.take(T, S + CW - 1)
        gelu = A.take(T, S)
        xc = A.take(T, S)
        R = [A.take(T, S) for _ in range(2)]
        I = [A.take(T, S), padded.rearrange("p t s -> p (t s)")[:, 0:T * S].rearrange("p (t s) -> p t s", t=T)]
        pads = [V.mark(nc.vector.memset(padded[:, :, 0:2], 0.0)),
                V.mark(nc.vector.memset(padded[:, :, S + 2:S + 3], 0.0))]
        gelu_ready, xb_ready = [None] * T, [None] * T
        xc_ready = [None] * T

        def take_input(c):
            def finish(i, psum, done):
                f = c * 4 + i
                SC.need(done)
                m = SC.mark(nc.scalar.copy(padded[:, f:f + 2, 2:S + 2], psum.rearrange("p (a b) -> p a b", a=2)))
                xb_ready[f] = xb_ready[f + 1] = m
                return m
            return lambda w: self.feature_tiles(w, [f * P for f in range(4)], x, banks, finish)

        def take_gelu(c):
            def finish(i, psum, done):
                f = c * 4 + i
                SC.need(done)
                m = SC.mark(nc.scalar.activation(gelu[:, f:f + 2, :].rearrange("p a b -> p (a b)"), psum, ACT.Gelu_apprx_tanh))
                gelu_ready[f] = gelu_ready[f + 1] = m
                return m
            return lambda w: self.feature_tiles(w, [f * P for f in range(4)], x, banks, finish)

        def convolve():
            for pair in range(0, T, 2):
                for j in range(CW):
                    for f in (pair, pair + 1):
                        tap = padded[:, f, j:j + S]
                        if j == 0:
                            V.need(xb_ready[f], pads, self.columns_ready)
                            xc_ready[f] = V.mark(nc.vector.tensor_scalar(xc[:, f, :], tap, col("conv_w", f), col("conv_b", f),
                                                                         ALU.mult, ALU.add))
                        else:
                            V.need(xc_ready[f])
                            xc_ready[f] = V.mark(nc.vector.scalar_tensor_tensor(xc[:, f, :], tap, col("conv_w", 8 * j + f),
                                                                                xc[:, f, :], ALU.mult, ALU.add))

        w_in = d["lru_w_in"][0]
        xc_parts = Parts(xc, None, xc_ready)

        def branch_and_split(w):
            take_gelu(0)(w)
            convolve()
        self.projections([(w_in, [(2 * 512, 512)], take_input(0)), (w_in, [(3 * 512, 512)], take_input(1)),
                          (w_in, [(0, 512)], branch_and_split)])
        gate_weights = []
        for key in ("lru_w_rgate", "lru_w_igate"):
            src = d[key][0].rearrange("z n (c p) f -> p (z n c) f", p=P)
            u = self.unit(lambda slot: [(slot.rearrange("p (b f) -> p b f", f=LBW), src)])
            gate_weights.append(Parts(u.ap.rearrange("p (t c) -> p t c", t=2 * LB), None, [u.arrived] * 2 * LB, [u]))
        room = self.next_slot()
        SC.need(room.free)
        a_buf = [room.ap.rearrange("p (a t s) -> p a t s", a=2, t=T)[:, z] for z in range(2)]
        r_ready, i_ready = {}, {}

        def gates(z):
            for w, bias, dst, ready in zip(gate_weights, ("b_r", "b_i"), (R, I), (r_ready, i_ready)):
                for n in range(LB):
                    bank = banks.take()
                    self.pe.need(bank.free, w.ready[z * LB + n])
                    for ff in range(2):
                        for c in range(2):
                            self.pe.need(xc_parts.ready[2 * n + c])
                            at = c * LBW + ff * P
                            last = self.product(bank.ap[:, ff * S:(ff + 1) * S], w.at(slice(None), z * LB + n, slice(at, at + P)),
                                                xc_parts.at(slice(None), 2 * n + c), start=(c == 0), stop=(c == 1))
                    done = self.pe.mark(last)
                    SC.need(done)
                    for ff in range(2):
                        f = 2 * n + ff
                        m = SC.mark(nc.scalar.activation(dst[z][:, f, :], bank.ap[:, ff * S:(ff + 1) * S], ACT.Sigmoid,
                                                         bias=col(bias, z * 8 + f)))
                        ready[z, f] = m
                    bank.free = [m]
                w.read_by(done)
            xc_parts.read_by(done)

        a_ready, u_ready, grown = {}, {}, {}
        two = [A.take(2, S) for _ in range(2)]
        sq_free = [[], []]

        def decays(z):
            for f in range(T):
                G.need(i_ready[z, f], xc_ready[f])
                u_ready[z, f] = G.mark(nc.gpsimd.tensor_tensor(I[z][:, f, :], I[z][:, f, :], xc[:, f, :], ALU.mult))
            for f in range(0, T, 2):
                both = slice(f, f + 2)
                for g in (f, f + 1):
                    SC.need(decay_ready, r_ready[z, g])
                    a_ready[z, g] = SC.mark(nc.scalar.activation(a_buf[z][:, g, :], R[z][:, g, :], ACT.Exp,
                                                                 scale=decay[:, z * 8 + g:z * 8 + g + 1]))
                for g in (f, f + 1):
                    SC.need(a_ready[z, g])
                    tanh = SC.mark(nc.scalar.activation(R[z][:, g, :], R[z][:, g, :], ACT.Tanh,
                                                        scale=growth[:, z * 8 + g:z * 8 + g + 1]))
                k = f // 2 % 2
                V.need(a_ready[z, f + 1], sq_free[k])
                m = V.mark(nc.vector.tensor_tensor(two[k], a_buf[z][:, both, :], a_buf[z][:, both, :], ALU.mult))
                V.need(m, tanh)
                grown[z] = V.mark(nc.vector.scalar_tensor_tensor(R[z][:, both, :], two[k], 1.0, R[z][:, both, :], ALU.add, ALU.mult))
                sq_free[k] = [grown[z]]

        def scans(z):
            SC.need(grown[z])
            root = SC.mark(nc.scalar.activation(R[z], R[z], ACT.Sqrt))
            edge = 0 if z == 0 else S - 1
            back = slice(None) if z == 0 else slice(None, None, -1)
            V.need(root)
            edge_m = V.mark(nc.vector.memset(R[z][:, :, edge:edge + 1], 1.0))
            V.need(edge_m)
            for f in range(T):
                V.need(u_ready[z, f])
                u_ready[z, f] = V.mark(nc.vector.tensor_tensor(I[z][:, f, :], I[z][:, f, :], R[z][:, f, :], ALU.mult))
            for f in range(T):
                V.need(u_ready[z, f], a_ready[z, f])
                u_ready[z, f] = V.mark(nc.vector.tensor_tensor_scan(R[z][:, f, back], a_buf[z][:, f, back], I[z][:, f, back], 0.0,
                                                                    ALU.mult, ALU.add))

        gates(0)
        decays(0)
        gates(1)
        late = self.weights(w_in, (512, 512), on_vector=True)
        scans(0)
        take_gelu(1)(late)
        decays(1)
        weights = self.out_weights(d["lru_w_out"][0])
        scans(1)
        room.free = [u_ready[1, f] for f in range(T)]
        y_ready = []
        for f in range(T):
            V.need(u_ready[0, f], u_ready[1, f])
            m = V.mark(nc.vector.tensor_tensor(R[0][:, f, :], R[0][:, f, :], R[1][:, f, :], ALU.add))
            V.need(m, gelu_ready[f])
            y_ready.append(V.mark(nc.vector.tensor_tensor(R[0][:, f, :], R[0][:, f, :], gelu[:, f, :], ALU.mult)))
        y = Parts(R[0], None, y_ready)
        self.product_and_norm(A, y, weights, banks, self.residual, EPS_FIRST, rows_ready)


    def modulated(self, arena, src, src_ready, scale1, shift, mod_ready, hi, dst, banks):
        nc = self.nc
        start = arena.at
        mv, m = self.moments(arena, src, src_ready)
        rstd, var = arena.take(H), arena.take(H)
        r = []
        for half in range(H):
            self.v.need(m[half])
            c = self.v.mark(nc.vector.tensor_scalar(var[:, half:half + 1], mv[:, half, 1:2], EPS_SECOND, None, ALU.add))
            self.g.need(c, self.half_ready)
            r.append(self.g.mark(nc.gpsimd.tensor_tensor(rstd[:, half:half + 1], var[:, half:half + 1],
                                                         self.minus_half[:, 0:1], ALU.pow)))
        flat = arena.take(H, D)
        flat_ready = []
        for half in range(H):
            self.v.need(r[half], m[half])
            flat_ready.append(self.v.mark(nc.vector.tensor_scalar(flat[:, half, :], src[:, half, :], mv[:, half, 0:1],
                                                                  rstd[:, half:half + 1], ALU.subtract, ALU.mult)))

        def evacuate(t, psum, done):
            if (t // 2) % 2:
                self.a.need(done, mod_ready)
                return self.a.mark(nc.scalar.activation(dst[:, t, :], psum, ACT.Identity, scale=scale1[:, t:t + 1],
                                                        bias=shift[:, t:t + 1]))
            self.v.need(done, mod_ready)
            return self.v.mark(nc.vector.tensor_scalar(dst[:, t, :], psum, scale1[:, t:t + 1], shift[:, t:t + 1],
                                                       ALU.mult, ALU.add))

        ready = self.to_features(lambda half, t: flat[:, half, t::T], dst, flat_ready, banks, evacuate)
        arena.at = start
        for q in (self.v, self.a):
            q.need(self.pe.last())
        return self.split_tiles(hi, dst, ready)

    def feature_tiles(self, w, cols, h, banks, finish, width=P):
        for i in range(0, len(cols), 2):
            bank = banks.take()
            self.pe.need(bank.free)
            pair = cols[i:i + 2]
            for k, c in enumerate(pair):
                for t in range(T):
                    self.pe.need(w.ready[t], h.ready[t])
                    last = self.product(bank.ap[0:width, k * S:(k + 1) * S], w.at(slice(None), t, slice(c, c + width)),
                                        h.at(slice(None), t), start=(t == 0), stop=(t == T - 1))
            done = self.pe.mark(last)
            bank.free = [finish(i, bank.ap[0:width, 0:len(pair) * S], done)]
        w.read_by(done)

    def token_tiles(self, w, c, n, h, banks, finish):
        for half in range(H):
            bank = banks.take()
            self.pe.need(bank.free)
            for t in range(T):
                self.pe.need(w.ready[t], h.ready[t])
                last = self.product(bank.ap[:, 0:n], h.at(slice(None), t, slice(half * P, (half + 1) * P)),
                                    w.at(slice(None), t, slice(c, c + n)), start=(t == 0), stop=(t == T - 1))
            done = self.pe.mark(last)
            bank.free = [finish(half, bank.ap[:, 0:n], done)]
        w.read_by(done)

    def projections(self, steps):
        nxt = self.weights(steps[0][0], *steps[0][1])
        for i, (_, _, run) in enumerate(steps):
            w = nxt
            if i + 1 < len(steps):
                nxt = self.weights(steps[i + 1][0], *steps[i + 1][1])
            run(w)

    def log_gates(self, arena, lrT, lr_ready, banks):
        nc = self.nc
        z, t = arena.take(4, S), arena.take(4, S)
        out = []
        for i in range(0, 4, 2):
            bank = banks.take()
            self.pe.need(bank.free, lr_ready, self.w2_ready)
            for k in range(2):
                last = nc.tensor.matmul(bank.ap[:, k * S:(k + 1) * S], self.w2[0:2 * GR, (i + k) * P:(i + k + 1) * P],
                                        lrT[0:2 * GR, :], start=True, stop=True)
            done = self.pe.mark(last)
            self.v.need(done)
            for k in range(2):
                b = self.col["gla_b"] + i + k
                m = self.v.mark(nc.vector.tensor_scalar(z[:, i + k, :], bank.ap[:, k * S:(k + 1) * S], self.columns[:, b:b + 1],
                                                        None, ALU.add))
            bank.free = [m]
            self.a.need(m)
            n = self.a.mark(nc.scalar.activation(t[:, i:i + 2, :], z[:, i:i + 2, :], ACT.Abs))
            self.a.need(n)
            n = self.a.mark(nc.scalar.activation(t[:, i:i + 2, :], t[:, i:i + 2, :], ACT.Exp, scale=-1.0))
            self.a.need(n)
            n = self.a.mark(nc.scalar.activation(t[:, i:i + 2, :], t[:, i:i + 2, :], ACT.Ln, bias=1.0))
            self.v.need(n)
            out.append(self.v.mark(nc.vector.scalar_tensor_tensor(z[:, i:i + 2, :], z[:, i:i + 2, :], 0.0, t[:, i:i + 2, :],
                                                                  ALU.min, ALU.subtract)))
        return z, t, out

    def rms_columns(self, arena, parts, n, marks):
        nc = self.nc
        junk = arena.take(n)
        ss, r = arena.take(len(parts)), arena.take(len(parts))
        self.a.need(marks)
        m = None
        for i, part in enumerate(parts):
            self.a.need(m)
            m = self.a.mark(nc.scalar.activation(junk, part, ACT.Square, accum_out=ss[:, i:i + 1]))
        return r, self.inverse_root(r, ss, 1.0 / n, EPS_SECOND, m)

    def side_work(self):
        nc, d, A = self.nc, self.d, self.side
        banks = Banks(self.banks[6:8])
        conds = self.sb("conditions", [P, 2, T])
        loaded = self.load(self.g, [(conds[:, 0, :], d["c_2"].rearrange("o (p t) -> p (o t)", t=T)),
                                    (conds[:, 1, :], d["c_ctx_2"].rearrange("(p t) -> p t", t=T))], "conditions_loaded")
        cT = self.sb("condition_columns", [P, T, 2])
        self.mod = self.sb("modulation", [P, 3, 2, T])
        self.w2 = self.sb("gate_weights", [2 * GR, 2 * GH * GK])
        z = self.v.mark(nc.vector.memset(self.w2, 0.0))
        self.g.need(z)
        self.w2_ready = self.load(self.g, [(self.w2[dd * GR:(dd + 1) * GR, dd * 256:(dd + 1) * 256], d["gla_w2_2"][0, dd])
                                           for dd in range(2)], "gate_weights_loaded")
        rows = self.parameter_rows
        at, pairs = 0, []
        self.col = {}
        for name, key in (("conv_w", "lru_conv_w"), ("conv_b", "lru_conv_b"), ("b_r", "lru_b_rgate"),
                          ("b_i", "lru_b_igate"), ("lam", "lru_lambda"), ("gla_b", "gla_b_2"),
                          ("gla_g", "gla_norm_g_2"), ("q_g", "mla_q_norm_g_2"), ("kv_g", "mla_kv_norm_g_2")):
            a = d[key]
            names = ["a", "b", "c"][:len(a.shape) - 1]
            flat = a.rearrange(f"{' '.join(names)} (n k) -> ({' '.join(names)} n) k", k=P)
            n = flat.shape[0]
            pairs.append((rows[at:at + n, :], flat))
            self.col[name] = at
            at += n
        assert at == 96
        rows_loaded = self.load(self.g, pairs, "parameter_rows_loaded")
        bias_ready = [self.load(self.g, [(self.ada_room[layer], d["ada_b_2"][layer].partition_broadcast(2))],
                                f"ada_bias{layer}_loaded") for layer in range(DEPTH)]
        yield
        self.a.need(loaded)
        cond_ready = self.a.mark(nc.scalar.activation(cT.rearrange("p t c -> p c t"), conds, ACT.Silu))
        self.pe.need(rows_loaded, self.ident_ready)
        bank = banks.take()
        self.pe.need(bank.free)
        done = self.pe.mark(nc.tensor.transpose(bank.ap[:, 0:96], rows[0:96, :], self.ident[0:96, 0:96]))
        self.columns_ready = self.copy(self.columns, bank.ap[:, 0:96], done, on_scalar=False)
        bank.free = [self.columns_ready]
        start = A.at
        rows = self.ada_room
        row_done = []
        for layer in range(DEPTH):
            for c in range(6):
                u, w = self.columns_unit(d["ada_w_2"][layer], c * 512, 512)
                bank = banks.take()
                self.pe.need(bank.free, u.arrived, cond_ready)
                for t in range(T):
                    for j in range(PACK):
                        last = nc.tensor.matmul(bank.ap[32 * j:32 * j + 2, 0:P], cT[:, t, :], w[:, t, j * P:(j + 1) * P],
                                                start=(t == 0), stop=(t == T - 1))
                done = self.pe.mark(last)
                u.free = [done]
                self.v.need(done, bias_ready[layer])
                for j in range(PACK):
                    part = rows[layer][:, c * 512 + j * P:c * 512 + (j + 1) * P]
                    m = self.v.mark(nc.vector.tensor_tensor(part, bank.ap[32 * j:32 * j + 2, 0:P], part, ALU.add))
                bank.free = [m]
                yield
            row_done.append(m)
        self.g.need(row_done)
        stored = self.new_sem("ada_rows_stored")
        for layer in range(DEPTH):
            nc.gpsimd.dma_start(self.rows_dram[layer], rows[layer]).then_inc(stored, 16)
        self.rows_stored = (stored, 16 * DEPTH)
        while self.in_attention:
            yield
        self.g.need(self.rows_stored)
        ms = self.load(self.g, [(self.mod[:, slot, part, :], self.rows_dram[layer][r, part * D:(part + 1) * D]
                                 .rearrange("(p t) -> p t", t=T)) for slot, layer, r in ((0, 0, 0), (1, 0, 1), (2, 1, 0))
                                for part in range(2)], "modulation_loaded")
        for _ in range(6):
            yield
        self.v.need(ms)
        for slot in range(3):
            m = self.v.mark(nc.vector.tensor_scalar(self.mod[:, slot, 1, :], self.mod[:, slot, 1, :], 1.0, None, ALU.add))
        self.mod_ready = m
        yield
        A.at = start
        ones = A.take(S)
        self.v.need(self.rows_stored)
        ones_ready = self.v.mark(nc.vector.memset(ones, 1.0))
        self.ctx_tokens = A.take(H, D)
        mark0 = A.at
        hT = A.take(T, S)
        ctx = self.ctx_tokens
        ctx_loaded = self.load(self.g, [(ctx, d["ctx_2"].rearrange("o (h p) d -> p (o h) d", p=P))], "context_loaded")
        for _ in range(6):
            yield
        mv, m = self.moments(A, ctx, [ctx_loaded, ctx_loaded])
        yield
        rstd, var = A.take(H), A.take(H)
        self.v.need(m)
        c = self.v.mark(nc.vector.tensor_copy(var, mv[:, :, 1]))
        r = self.inverse_root(rstd, var, 1.0, EPS_SECOND, c)
        self.v.need(r, m)
        flat_ready = [self.v.mark(nc.vector.tensor_scalar(ctx[:, half, :], ctx[:, half, :], mv[:, half, 0:1],
                                                          rstd[:, half:half + 1], ALU.subtract, ALU.mult))
                      for half in range(H)]
        hT_ready = []
        for t0 in range(0, T, 2):
            def evacuate(t, psum, done, t0=t0):
                self.v.need(done, self.mod_ready)
                return self.v.mark(nc.vector.tensor_scalar(hT[:, t0 + t, :], psum, self.mod[:, 1, 1, t0 + t:t0 + t + 1],
                                                           self.mod[:, 1, 0, t0 + t:t0 + t + 1], ALU.mult, ALU.add))
            hT_ready += self.to_features(lambda half, t: ctx[:, half, (t0 + t)::T], hT[:, t0:t0 + 2, :], flat_ready, banks,
                                         evacuate)
            yield
        ctx_dead = self.pe.last()
        B = Arena(self.ctx_tokens.rearrange("p h d -> p (h d)"), H * D)
        kT, vals = B.take(2, S), B.take(H, GH * GV)
        lrT = B.take(S)
        ckr = A.take(H, KVR + MR)
        w_in = d["even_w_in_2"][0]
        ready = {}

        def keep(name, dst_of):
            def finish(i, psum, done):
                dst = dst_of(i)
                if len(dst.shape) == 3:
                    psum = psum.rearrange("p (a b) -> p a b", a=dst.shape[1])
                m = self.copy(dst, psum, done, ctx_dead)
                ready.setdefault(name, []).append(m)
                return m
            return finish

        h = Parts(hT, None, hT_ready)
        w = self.weights(w_in, (C_GK, 512), whole=True)
        self.feature_tiles(w, [0, P], h, banks, keep("k", lambda i: kT[:, i:i + 2, :]))
        yield
        self.token_tiles(w, 256, 256, h, banks, keep("v", lambda half: vals[:, half, 0:256]))
        yield
        w = self.weights(w_in, (C_GV + 256, 256 + 2 * GR), whole=True)
        self.token_tiles(w, 0, 256, h, banks, keep("v", lambda half: vals[:, half, 256:512]))
        yield
        self.feature_tiles(w, [256], h, banks, keep("lr", lambda i: lrT[0:2 * GR, :]), width=2 * GR)
        yield
        w = self.weights(w_in, (C_CKV, KVR + MR), whole=True)
        self.token_tiles(w, 0, KVR + MR, h, banks, keep("ckr", lambda half: ckr[:, half, :]))
        yield
        scaled = self.scaled_latents(A, ckr, ready["ckr"], False)
        yield
        self.lat0_ready = self.turned_latents(ckr, scaled, ready["ckr"], self.latT0, self.krT0, banks)
        yield
        hT_dead = self.pe.last()
        A.at = mark0
        for q in (self.v, self.a):
            q.need(hT_dead)
        z, t, g_ready = self.log_gates(A, lrT, ready["lr"], banks)
        yield
        sums = A.take(S + 1)
        wk, wkT = t[:, 2, :], t[:, 0:2, :]
        self.state0_ready = []
        wk_free = sums_free = wkT_free = []
        for dd in range(2):
            turned = []
            for i in range(2):
                self.v.need(sums_free)
                edge = S if dd == 0 else 0
                m = self.v.mark(nc.vector.memset(sums[:, edge:edge + 1], 0.0))
                self.v.need(g_ready, m, ones_ready)
                src = z[:, 2 * dd + i, :]
                if dd == 0:
                    m = self.v.mark(nc.vector.tensor_tensor_scan(sums[:, 0:S][:, ::-1], ones, src[:, ::-1], 0.0, ALU.mult, ALU.add))
                    part = sums[:, 1:S + 1]
                else:
                    m = self.v.mark(nc.vector.tensor_tensor_scan(sums[:, 1:S + 1], ones, src, 0.0, ALU.mult, ALU.add))
                    part = sums[:, 0:S]
                self.a.need(m, wk_free)
                m = self.a.mark(nc.scalar.activation(wk, part, ACT.Exp, scale=1.0 / GTAU))
                sums_free = [m]
                self.v.need(m, ready["k"])
                m = self.v.mark(nc.vector.tensor_tensor(wk, wk, kT[:, i, :], ALU.mult))
                bank = banks.take()
                self.pe.need(bank.free, m)
                for half in range(H):
                    last = nc.tensor.transpose(bank.ap[:, half * P:(half + 1) * P], wk[:, half * P:(half + 1) * P], self.ident)
                done = self.pe.mark(last)
                wk_free = [done]
                m = self.copy(wkT[:, :, i * P:(i + 1) * P], bank.ap[:, 0:S].rearrange("p (a b) -> p a b", a=H), done, wkT_free)
                bank.free = [m]
                turned.append(m)
            yield
            bank = banks.take()
            self.pe.need(bank.free, turned, ready["v"])
            for i in range(2):
                for half in range(H):
                    last = nc.tensor.matmul(bank.ap[:, i * S:(i + 1) * S], wkT[:, half, i * P:(i + 1) * P],
                                            vals[:, half, i * 256:(i + 1) * 256], start=(half == 0), stop=(half == H - 1))
            done = self.pe.mark(last)
            wkT_free = [done]
            self.v.need(done)
            for k in range(2):
                r = slice(64 * k, 64 * k + 64)
                m = self.v.mark(nc.vector.tensor_copy(
                    self.state0[r, dd, :, :],
                    bank.ap[r, :].rearrange("p (i k v) -> p i k v", i=2, k=2)[:, :, k, :]))
                self.state0_ready.append(m)
            bank.free = [m]
            yield

    def scaled_latents(self, arena, ckr, marks, rotate):
        nc = self.nc
        r, r_ready = self.rms_columns(arena, [ckr[:, half, 0:KVR] for half in range(H)], KVR, marks)
        self.v.need(r_ready, marks)
        for half in range(H):
            m = self.v.mark(nc.vector.tensor_scalar(ckr[:, half, 0:KVR], ckr[:, half, 0:KVR], r[:, half:half + 1], None, ALU.mult))
        if rotate:
            m = [m, self.rotate(arena, ckr[:, :, KVR:].rearrange("p h (o r) -> p h o r", o=1), 1, marks)]
        return m

    def turned_latents(self, ckr, m, marks, latT, krT, banks):
        nc = self.nc
        bank = banks.take()
        self.pe.need(bank.free, m, marks)
        for half in range(H):
            nc.tensor.transpose(bank.ap[:, half * P:(half + 1) * P], ckr[:, half, 0:KVR], self.ident)
            last = nc.tensor.transpose(bank.ap[0:MR, S + half * P:S + (half + 1) * P], ckr[:, half, KVR:], self.ident)
        done = self.pe.mark(last)
        self.v.need(done, self.columns_ready)
        c = self.col["kv_g"]
        m1 = self.v.mark(nc.vector.tensor_scalar(latT, bank.ap[:, 0:S], self.columns[:, c:c + 1], None, ALU.mult))
        m2 = self.v.mark(nc.vector.tensor_copy(krT, bank.ap[0:MR, S:2 * S]))
        bank.free = [m2]
        return [m1, m2]

    def rotate(self, arena, heads, n, marks):
        nc = self.nc
        tmp = [arena.take(n, MR // 2) for _ in range(4)]
        m = None
        for half in range(H):
            a, b = heads[:, half, :, 0:MR // 2], heads[:, half, :, MR // 2:MR]
            cos = self.axial[:, half, 0:1, :].to_broadcast([P, n, MR // 2])
            sin = self.axial[:, half, 1:2, :].to_broadcast([P, n, MR // 2])
            self.v.need(marks, self.small2_ready, m)
            for dst, s, t in ((tmp[0], a, cos), (tmp[1], b, sin), (tmp[2], a, sin), (tmp[3], b, cos)):
                k = self.v.mark(nc.vector.tensor_tensor(dst, s, t, ALU.mult))
            self.v.need(k)
            self.v.mark(nc.vector.tensor_tensor(a, tmp[0], tmp[1], ALU.subtract))
            m = self.v.mark(nc.vector.tensor_tensor(b, tmp[2], tmp[3], ALU.add))
        return m

    def gate_row(self, row, layer, name):
        self.a.need(self.rows_stored)
        return self.load(self.a, [(row, self.rows_dram[layer][0, 2 * D:3 * D].partition_broadcast(P))], name)

    def gated_residual(self, tmp, row, row_ready):
        nc = self.nc
        n = [0]
        free = [[], []]

        def combine(half, c, psum, done):
            i = n[0] % 2
            n[0] += 1
            self.v.need(done, row_ready, free[i])
            m = self.v.mark(nc.vector.tensor_tensor(tmp[i], psum, row[:, c * 512:(c + 1) * 512], ALU.mult))
            xs = self.x[:, half, c * 512:(c + 1) * 512]
            self.v.need(m, self.x_ready[half])
            m = self.v.mark(nc.vector.scalar_tensor_tensor(xs, xs, ALPHA, tmp[i], ALU.mult, ALU.add))
            free[i] = [m]
            return m

        return combine

    def whole_ring(self):
        at = self.unit_at % len(self.slots)
        for s in self.lent_slots:
            s.free = [q.last() for q in (self.pe, self.v, self.a, self.g)]
        self.slots, self.unit_at = self.slots[at:] + self.lent_slots + self.slots[:at], 0

    def even(self):
        nc, d, A = self.nc, self.d, self.whole
        V, SC = self.v, self.a
        banks = Banks(self.banks)
        rows_ready = self.affine_rows(d["post_ln_g_2"][0], d["post_ln_b_2"][0], "post_ln0_rows")
        cq, ckr = self.tail.take(H, QR), self.tail.take(H, KVR + MR)
        yT, mgT = A.take(T, S), A.take(GH, S)
        reset = A.take(2, S)
        tri = A.take(2, P).bitcast(U32)
        tables = self.load(self.a, [(reset, d["k_reset"]), (tri, d["k_tri"])], "chunk_tables_loaded")
        qT, kT, vals = A.take(2, S), A.take(2, S), A.take(H, GH * GV)
        ggT, lrT = A.take(GH, S), A.take(S)
        h_room = A.take(2, T * S)
        tiles = lambda i: h_room[:, i, :].rearrange("p (t s) -> p t s", t=T)
        h = self.modulated(A, self.x, self.x_ready, self.mod[:, 0, 1, :], self.mod[:, 0, 0, :], self.mod_ready,
                           self.rounded(tiles(0)), tiles(1), banks)
        ready = {}

        def keep(name, dst_of, scale=None, func=None):
            def finish(i, psum, done):
                dst = dst_of(i)
                if len(dst.shape) == 3:
                    psum = psum.rearrange("p (a b) -> p a b", a=dst.shape[1])
                if func is not None:
                    SC.need(done)
                    m = SC.mark(nc.scalar.activation(dst, psum, func))
                else:
                    m = self.copy(dst, psum, done, scale=scale)
                ready.setdefault(name, []).append(m)
                return m
            return finish

        w_in = d["even_w_in_2"][0]
        y_ready = [None] * T
        self.projecting = True
        linear = self.linear_attention(A, h_room, qT, kT, vals, lrT, ggT, reset, tri, tables, ready, yT, y_ready)
        latent = self.latent_attention(self.tail, cq, ckr, mgT, ready, yT, y_ready)
        both = lambda: (next(linear), next(latent))
        args = (h, banks)
        n_lr = 2 * GR

        def narrow(w):
            self.feature_tiles(w, [0], *args, keep("lr", lambda i: lrT[0:n_lr, :]), width=n_lr)
            self.token_tiles(w, n_lr, QR, *args, keep("cq", lambda half: cq[:, half, :]))
            self.token_tiles(w, n_lr + QR, KVR + MR, *args, keep("ckr", lambda half: ckr[:, half, :]))
            both()

        def queries_keys(w):
            self.feature_tiles(w, [0, P], *args, keep("q", lambda i: qT[:, i:i + 2, :], scale=GK ** -0.5))
            both()
            self.feature_tiles(w, [2 * P, 3 * P], *args, keep("k", lambda i: kT[:, i:i + 2, :]))
            both()

        def values(w):
            self.token_tiles(w, 0, 512, *args, keep("v", lambda half: vals[:, half, :]))
            both()

        def gates(name, dst):
            def run(w):
                for i in (0, 2):
                    self.feature_tiles(w, [i * P, (i + 1) * P], *args, keep(name, lambda _: dst[:, i:i + 2, :], func=ACT.Silu))
                    both()
            return run

        self.spares = Banks(self.spare_slots)
        self.projections([(w_in, [(C_LR, n_lr), (C_CQ, QR + KVR + MR)], narrow), (w_in, [(C_GQ, 512)], queries_keys),
                          (w_in, [(C_GV, 512)], values), (w_in, [(C_GG, 512)], gates("gg", ggT)),
                          (w_in, [(C_MG, 512)], gates("mg", mgT))])
        self.spares = None
        self.projecting = False
        self.meet()
        running = [linear, latent]
        gate = vals.rearrange("p h n -> p (h n)")
        while running:
            for one in list(running):
                if next(one, self) is self:
                    running = [o for o in running if o is not one]
                    if one is linear:
                        SC.need(self.pe.last(), self.v.last())
                        gate_ready = self.gate_row(gate, 0, "gate0_row")
                        self.v.need(self.pe.last())
        weights = self.out_weights(d["even_w_out_2"][0])
        combine = self.gated_residual([qT.rearrange("p a b -> p (a b)"), kT.rearrange("p a b -> p (a b)")], gate, gate_ready)
        self.whole_ring()
        y = Parts(yT, None, y_ready)
        self.product_and_norm(A, y, weights, banks, combine, EPS_SECOND, rows_ready)

    def linear_attention(self, A, h_room, qT, kT, vals, lrT, ggT, reset, tri, tables, ready, yT, y_ready):
        nc, V, SC = self.nc, self.v, self.a
        own = self.banks[0:4]
        banks = Banks(own)
        bT = A.take(4, S)
        top = A.at
        z, t, g_ready = self.log_gates(A, lrT, ready["lr"], banks)
        yield
        b_ready = []
        for dd in range(2):
            for i in range(2):
                back = slice(None) if dd == 0 else slice(None, None, -1)
                V.need(g_ready, tables)
                b_ready.append(V.mark(nc.vector.tensor_tensor_scan(bT[:, 2 * dd + i, :][:, back], reset[:, dd, :][:, back],
                                                                   z[:, 2 * dd + i, :][:, back], 0.0, ALU.mult, ALU.add)))
        yield
        A.at = top
        V.need(b_ready)
        self.a.need(b_ready)
        ke, qe, kend, qb, att, kendT = {}, {}, {}, {}, {}, {}
        e_ready = {}
        end = A.take(2, 8)
        for dd in range(2):
            ke[dd], qe[dd], kend[dd], qb[dd] = (A.take(2, S) for _ in range(4))
        for dd in range(2):
            chunks = lambda ap: ap.rearrange("p i (c t) -> p (i c) t", c=NCH)
            b = chunks(bT[:, 2 * dd:2 * dd + 2, :])
            mid = b[:, :, (GCH // 2 - 1 if dd == 0 else GCH // 2)].unsqueeze(2).to_broadcast([P, 2 * NCH, GCH])
            last_ = b[:, :, (GCH - 1 if dd == 0 else 0)]
            lastb = last_.unsqueeze(2).to_broadcast([P, 2 * NCH, GCH])
            m1 = V.mark(nc.vector.tensor_tensor(chunks(qe[dd]), b, mid, ALU.subtract))
            m2 = V.mark(nc.vector.tensor_tensor(chunks(kend[dd]), b, lastb, ALU.subtract))
            SC.need(m1, m2, b_ready)
            e1 = SC.mark(nc.scalar.activation(ke[dd], qe[dd], ACT.Exp, scale=-1.0 / GTAU))
            SC.need(e1)
            e2 = SC.mark(nc.scalar.activation(qe[dd], qe[dd], ACT.Exp, scale=1.0 / GTAU))
            e3 = SC.mark(nc.scalar.activation(kend[dd], kend[dd], ACT.Exp, scale=-1.0 / GTAU))
            e4 = SC.mark(nc.scalar.activation(qb[dd], bT[:, 2 * dd:2 * dd + 2, :], ACT.Exp, scale=1.0 / GTAU))
            e5 = SC.mark(nc.scalar.activation(end[:, dd, :], last_, ACT.Exp, scale=1.0 / GTAU))
            V.need(e1, e2, e3, e4, ready["q"], ready["k"])
            ms = [V.mark(nc.vector.tensor_tensor(buf, buf, src, ALU.mult))
                  for buf, src in ((kend[dd], kT), (ke[dd], kT), (qe[dd], qT), (qb[dd], qT))]
            e_ready[dd] = [ms[-1], e5]
            yield
        while self.projecting:
            yield
        over = Arena(h_room.rearrange("p a b -> p (a b)"), 2 * T * S)
        S_ = [[over.take(2, 2 * GV) for _ in range(2)] for _ in range(2)]
        for dd in range(2):
            att[dd] = over.take(4, 2 * P)
            kendT[dd] = kend[dd]
        zero = [V.mark(nc.vector.memset(att[dd], 0.0)) for dd in range(2)]
        zero += [V.mark(nc.vector.memset(S_[dd][1], 0.0)) for dd in range(2)]
        V.need(self.state0_ready)
        zero0 = [V.mark(nc.vector.memset(S_[dd][0], 0.0)) for dd in range(2)]
        V.need(zero0)
        s_ready = []
        for dd in range(2):
            for k in range(2):
                r = slice(64 * k, 64 * k + 64)
                m = V.mark(nc.vector.tensor_copy(S_[dd][0][r, :, k * GV:(k + 1) * GV], self.state0[r, dd, :, :]))
            s_ready.append(m)
        att_ready, kendT_ready = {}, {}
        for dd in range(2):
            for k in range(2):
                bank = banks.take()
                self.pe.need(bank.free, e_ready[dd])
                r = slice(64 * k, 64 * k + 64)
                for i in range(2):
                    for half in range(H):
                        hs = slice(half * P, (half + 1) * P)
                        last = nc.tensor.matmul(bank.ap[:, (2 * i + half) * P:(2 * i + half + 1) * P], ke[dd][r, i, hs],
                                                qe[dd][r, i, hs], start=True, stop=True)
                done = self.pe.mark(last)
                V.need(done, zero, tables)
                for i in range(2):
                    for half in range(H):
                        h = 2 * i + k
                        c = (2 * i + half) * P
                        m = V.mark(nc.vector.copy_predicated(att[dd][:, h, half * P:(half + 1) * P], tri[:, dd, :],
                                                             bank.ap[:, c:c + P]))
                bank.free = [m]
                att_ready[dd, k] = m
                yield
            kendT_ready[dd] = []
            bank = banks.take()
            self.pe.need(bank.free)
            for half in range(H):
                for i in range(2):
                    o_ = half * S + i * P
                    last = nc.tensor.transpose(bank.ap[:, o_:o_ + P], kend[dd][:, i, half * P:(half + 1) * P], self.ident)
            done = self.pe.mark(last)
            m = self.copy(kendT[dd].rearrange("p a b -> p (a b)"), bank.ap, done)
            bank.free = [m]
            kendT_ready[dd] = m
            yield
        out = [banks.take() for _ in range(H)]
        ds_banks = Banks([b for b in own if b not in out])
        started = [False, False]
        self.pe.need(out[0].free, out[1].free, ready["v"])
        for half in range(H):
            for dd in range(2):
                for h in range(GH):
                    self.pe.need(att_ready[dd, h % 2])
                    nc.tensor.matmul(out[half].ap[:, h * GV:(h + 1) * GV], att[dd][:, h, half * P:(half + 1) * P],
                                     vals[:, half, h * GV:(h + 1) * GV], start=not started[half], stop=False,
                                     skip_group_check=True)
                    started[half] = True
            yield
        s_free = [[[], []], [[], []]]
        for step in range(NCH):
            for dd in range(2):
                c = step if dd == 0 else NCH - 1 - step
                half, k = c // 2, c % 2
                rows = slice(64 * k, 64 * k + 64)
                cur, nxt = S_[dd][step % 2], S_[dd][(step + 1) % 2]
                self.pe.need(s_ready[dd])
                for i in range(2):
                    last = nc.tensor.matmul(out[half].ap[rows, i * 256:(i + 1) * 256], qb[dd][:, i, c * GCH:(c + 1) * GCH],
                                            cur[:, i, :], start=False, stop=(step == NCH - 1), skip_group_check=True)
                done = self.pe.mark(last)
                s_free[dd][step % 2] = [done]
                if step == NCH - 1:
                    last_done = done
                    continue
                bank = ds_banks.take()
                self.pe.need(bank.free, kendT_ready[dd])
                for i in range(2):
                    last = nc.tensor.matmul(bank.ap[:, i * 256:(i + 1) * 256], kendT[dd][rows, half, i * P:(i + 1) * P],
                                            vals[rows, half, i * 256:(i + 1) * 256], start=True, stop=True)
                done = self.pe.mark(last)
                V.need(done, s_free[dd][(step + 1) % 2], s_ready[dd], zero, e_ready[dd])
                for i in range(2):
                    for kk in range(2):
                        r = slice(64 * kk, 64 * kk + 64)
                        m = V.mark(nc.vector.scalar_tensor_tensor(
                            nxt[r, i, kk * GV:(kk + 1) * GV], cur[r, i, kk * GV:(kk + 1) * GV],
                            end[r, dd, i * NCH + c:i * NCH + c + 1], bank.ap[r, i * 256 + kk * GV:i * 256 + (kk + 1) * GV],
                            ALU.mult, ALU.add))
                bank.free = [m]
                s_ready[dd] = m
                yield
        yield
        o = A.take(H, GH * GV)
        o_ready = []
        for half in range(H):
            m = self.copy(o[:, half, :], out[half].ap, last_done)
            out[half].free = [m]
            o_ready.append(m)
        parts = [o[:, half, h * GV:(h + 1) * GV] for half in range(H) for h in range(GH)]
        r, r_ready = self.rms_columns(A, parts, GV, o_ready)
        V.need(r_ready, o_ready)
        n_ready = [V.mark(nc.vector.tensor_scalar(part, part, r[:, i:i + 1], None, ALU.mult)) for i, part in enumerate(parts)]
        for _ in range(3):
            yield
        gcol = self.columns[:, self.col["gla_g"]:self.col["gla_g"] + 1]

        def evacuate(t, psum, done):
            V.need(done, ready["gg"])
            m = V.mark(nc.vector.scalar_tensor_tensor(yT[:, t, :], psum, gcol, ggT[:, t, :], ALU.mult, ALU.mult))
            y_ready[t] = m
            return m

        self.to_features(lambda half, h: o[:, half, h * GV:(h + 1) * GV], yT[:, 0:GH, :], n_ready[-1], banks, evacuate)

    def latent_attention(self, A, cq, ckr, mgT, ready, yT, y_ready):
        nc, d, V, SC = self.nc, self.d, self.v, self.a
        banks = Banks(self.banks[4:8])
        K = 2 * S
        KT = K // P
        KQ = QR // P
        latT, krT = A.take(K), A.take(K)[0:MR, :]
        scaled = self.scaled_latents(A, ckr, ready["ckr"], True)
        r, r_ready = self.rms_columns(A, [cq[:, half, :] for half in range(H)], QR, ready["cq"])
        V.need(r_ready)
        for half in range(H):
            m = V.mark(nc.vector.tensor_scalar(cq[:, half, :], cq[:, half, :], r[:, half:half + 1], None, ALU.mult))
        yield
        lat_ready = self.turned_latents(ckr, scaled, ready["ckr"], latT[:, S:K], krT[:, S:K], banks)
        V.need(self.lat0_ready)
        lat_ready += [V.mark(nc.vector.tensor_copy(latT[:, 0:S], self.latT0)),
                      V.mark(nc.vector.tensor_copy(krT[:, 0:S], self.krT0))]
        cqT = A.take(KQ, S)

        def evacuate(t, psum, done):
            V.need(done)
            c = self.col["q_g"] + t
            return V.mark(nc.vector.tensor_scalar(cqT[:, t, :], psum, self.columns[:, c:c + 1], None, ALU.mult))

        yield
        cqT_ready = self.to_features(lambda half, t: cq[:, half, t * P:(t + 1) * P], cqT, m, banks, evacuate)
        yield
        NU = KQ * MH * MQ
        u = self.unit(lambda slot: [
            (slot[:, 0:NU].rearrange("p (k n) -> p k n", k=KQ), d["mla_w_uq_2"][0].rearrange("(k p) n -> p k n", p=P)),
            (slot[:, UNIT - MH * (MN + MV):UNIT], d["mla_w_ukv_2"][0])])
        wq = u.ap[:, 0:NU].rearrange("p (k h n) -> p k h n", k=KQ, h=MH)
        wkv = u.ap[:, UNIT - MH * (MN + MV):UNIT].rearrange("p (h n) -> p h n", h=MH)
        qT = A.take(MH, S)
        qr = A.take(H, MH * MR)
        qr_ready = []
        for half in range(H):
            bank = banks.take()
            self.pe.need(bank.free, u.arrived, cqT_ready)
            for k in range(KQ):
                last = nc.tensor.matmul(bank.ap[:, 0:MH * MR], cqT[:, k, half * P:(half + 1) * P], wq[:, k, :, MN:MQ],
                                        start=(k == 0), stop=(k == KQ - 1))
            done = self.pe.mark(last)
            m = self.copy(qr[:, half, :], bank.ap[:, 0:MH * MR], done)
            bank.free = [m]
            qr_ready.append(m)
        yield
        rm = self.rotate(A, qr.rearrange("p h (n r) -> p h n r", n=MH), MH, qr_ready)
        yield
        q_ready, k_ready, v_ready = {h: [] for h in range(MH)}, {h: [] for h in range(MH)}, []
        for b in range(2):
            bank = banks.take()
            self.pe.need(bank.free, rm)
            for half in range(H):
                last = nc.tensor.transpose(bank.ap[:, half * P:(half + 1) * P], qr[:, half, b * P:(b + 1) * P], self.ident)
            done = self.pe.mark(last)
            ms = []
            for i in range(4):
                m = self.copy(qT[MN:MQ, 4 * b + i, :], bank.ap[MR * i:MR * (i + 1), 0:S], done)
                q_ready[4 * b + i].append(m)
                ms.append(m)
            bank.free = ms
            yield
        assert A.at <= (SLOTS - TAIL_SLOTS - 2) * UNIT
        while self.projecting:
            yield
        kT = A.take(MH, K)
        vals = A.take(KT, MH * MV)
        for h in range(MH):
            bank = banks.take()
            self.pe.need(bank.free)
            for k in range(KQ):
                last = nc.tensor.matmul(bank.ap[0:MN, 0:S], wq[:, k, h, 0:MN], cqT[:, k, :], start=(k == 0), stop=(k == KQ - 1))
            done = self.pe.mark(last)
            m = self.copy(qT[0:MN, h, :], bank.ap[0:MN, 0:S], done)
            bank.free = [m]
            q_ready[h].append(m)
            bank = banks.take()
            self.pe.need(bank.free, lat_ready)
            done = self.pe.mark(nc.tensor.matmul(bank.ap[0:MN, :], wkv[:, h, 0:MN], latT, start=True, stop=True))
            m = self.copy(kT[0:MN, h, :], bank.ap[0:MN, :], done)
            bank.free = [m]
            k_ready[h].append(m)
            k_ready[h].append(self.copy(kT[MN:MQ, h, :], krT, lat_ready))
            yield
        for kt in range(KT):
            bank = banks.take()
            self.pe.need(bank.free)
            done = self.pe.mark(nc.tensor.matmul(bank.ap, latT[:, kt * P:(kt + 1) * P], wkv[:, :, MN:MN + MV],
                                                 start=True, stop=True))
            m = self.copy(vals[:, kt, :], bank.ap, done)
            bank.free = [m]
            v_ready.append(m)
        u.free = [done]
        yield
        outs_free = banks.banks[3].free
        banks = Banks(banks.banks[0:3])
        NB = MH * H
        DEEP = 3
        pr = [A.take(K) for _ in range(DEEP)]
        pr_free = [[] for _ in range(DEEP)]
        pT = [A.take(KT, S) for _ in range(2)]
        pT_free, pT_ready = [[], []], {}
        neg, tot = A.take(NB), A.take(NB)
        score, soft = {}, {}

        def scores(n):
            h, half = n // H, n % H
            bank = banks.take()
            self.pe.need(bank.free, q_ready[h], k_ready[h])
            done = self.pe.mark(nc.tensor.matmul(bank.ap, qT[0:MQ, h, half * P:(half + 1) * P], kT[0:MQ, h, :],
                                                 start=True, stop=True))
            score[n] = (bank, done)

        def softmax(n):
            bank, done = score[n]
            V.need(done)
            m = V.mark(nc.vector.tensor_reduce(neg[:, n:n + 1], bank.ap, AX.X, ALU.max))
            V.need(m)
            m = V.mark(nc.vector.tensor_scalar(neg[:, n:n + 1], neg[:, n:n + 1], -MSCALE, None, ALU.mult))
            SC.need(m, pr_free[n % DEEP])
            m = SC.mark(nc.scalar.activation(pr[n % DEEP], bank.ap, ACT.Exp, scale=MSCALE, bias=neg[:, n:n + 1],
                                             accum_out=tot[:, n:n + 1]))
            bank.free = [m]
            soft[n] = m

        def normalise(n):
            V.need(soft[n])
            m = V.mark(nc.vector.reciprocal(tot[:, n:n + 1], tot[:, n:n + 1]))
            V.need(m)
            soft[n] = V.mark(nc.vector.tensor_scalar(pr[n % DEEP], pr[n % DEEP], tot[:, n:n + 1], None, ALU.mult))

        def turn(n):
            h, half = n // H, n % H
            bank = banks.take()
            self.pe.need(bank.free, soft[n])
            for kt in range(KT):
                last = nc.tensor.transpose(bank.ap[:, kt * P:(kt + 1) * P], pr[n % DEEP][:, kt * P:(kt + 1) * P], self.ident)
            done = self.pe.mark(last)
            pr_free[n % DEEP] = [done]
            m = self.copy(pT[h % 2][:, :, half * P:(half + 1) * P], bank.ap.rearrange("p (a b) -> p a b", a=KT), done,
                          pT_free[h % 2], on_scalar=True)
            bank.free = [m]
            pT_ready.setdefault(h, []).append(m)

        outs = [Bank(self.banks[7].ap[:, i * S:(i + 1) * S]) for i in range(2)]
        for o in outs:
            o.free = outs_free

        def values(h):
            bank = outs[h // 2 % 2]
            self.pe.need(bank.free, pT_ready[h], v_ready)
            r_ = slice(64 * (h % 2), 64 * (h % 2) + 64)
            for kt in range(KT):
                last = nc.tensor.matmul(bank.ap[r_, :], vals[:, kt, h * MV:(h + 1) * MV], pT[h % 2][:, kt, :],
                                        start=(kt == 0), stop=(kt == KT - 1))
            done = self.pe.mark(last)
            pT_free[h % 2] = [done]
            if h % 2:
                V.need(done, ready["mg"])
                m = V.mark(nc.vector.tensor_tensor(yT[:, GH + h // 2, :], bank.ap, mgT[:, h // 2, :], ALU.mult))
                bank.free = [m]
                y_ready[GH + h // 2] = m

        for n in range(NB + 4):
            if n < NB:
                scores(n)
            if 2 <= n < NB + 2:
                normalise(n - 2)
            if n < NB:
                softmax(n)
            if 2 <= n < NB + 2:
                turn(n - 2)
            if n >= 4 and n % 2 == 0:
                values((n - 4) // 2)
            yield

    def odd(self):
        nc, d, A = self.nc, self.d, self.whole
        V, SC = self.v, self.a
        banks = Banks(self.banks)
        NG = 4
        rows_ready = self.affine_rows(d["post_ln_g_2"][1], d["post_ln_b_2"][1], "post_ln1_rows")
        dft_n = A.take(H, 2, S)
        dft_c = A.take(2 * P)
        sgu = A.take(NG, P)
        sgu_b = A.take(NG * P)
        tables = self.load(self.a, [(dft_n, d["k_dft_n"]), (dft_c, d["k_dft_c"]),
                                    (sgu, d["sgu_w_2"][0].rearrange("g t s -> t g s")),
                                    (sgu_b, d["sgu_b_2"][0].rearrange("g t -> (g t)").partition_broadcast(P))], "odd_tables_loaded")
        gate = A.take(D)
        gate_ready = self.gate_row(gate, 1, "gate1_row")
        combine = self.gated_residual([A.take(512) for _ in range(2)], gate, gate_ready)
        sguT = A.take(NG, P)
        hi, dst = self.rounded(A.take(T, S)), A.take(T, S)
        h = self.modulated(A, self.x, self.x_ready, self.mod[:, 2, 1, :], self.mod[:, 2, 0, :], self.mod_ready, hi, dst, banks)
        fT, fgT, uT, sgT = (A.take(NG, S) for _ in range(4))
        v = A.take(H, NG * P)
        ready = {}

        def keep(name, dst_of, func=None):
            def finish(i, psum, done):
                dst = dst_of(i)
                if len(dst.shape) == 3:
                    psum = psum.rearrange("p (a b) -> p a b", a=dst.shape[1])
                if func is None:
                    m = self.copy(dst, psum, done)
                else:
                    SC.need(done)
                    m = SC.mark(nc.scalar.activation(dst, psum, func))
                ready.setdefault(name, []).append(m)
                return m
            return finish

        w_in = d["odd_w_in_2"][0]
        args = (h, banks)
        tiles = [0, P, 2 * P, 3 * P]
        self.projections([
            (w_in, [(0, 512)], lambda w: self.feature_tiles(w, tiles, *args, keep("f", lambda i: fT[:, i:i + 2, :]))),
            (w_in, [(1536, 512)], lambda w: self.token_tiles(w, 0, 512, *args, keep("v", lambda half: v[:, half, :], ACT.Gelu))),
            (w_in, [(1024, 512)], lambda w: self.feature_tiles(w, tiles, *args, keep("u", lambda i: uT[:, i:i + 2, :], ACT.Gelu))),
            (w_in, [(512, 512)], lambda w: self.feature_tiles(w, tiles, *args, keep("fg", lambda i: fgT[:, i:i + 2, :], ACT.Silu))),
            (w_in, [(2048, 512)], lambda w: self.feature_tiles(w, tiles, *args, keep("sg", lambda i: sgT[:, i:i + 2, :], ACT.Silu))),
        ])
        bank = banks.take()
        self.pe.need(bank.free, tables)
        for g in range(NG):
            last = nc.tensor.transpose(bank.ap[:, g * P:(g + 1) * P], sgu[:, g, :], self.ident)
        done = self.pe.mark(last)
        sguT_ready = self.copy(sguT.rearrange("p a b -> p (a b)"), bank.ap, done)
        bank.free = [sguT_ready]
        weights = self.out_weights(d["odd_w_out_2"][0])
        yT = A.take(T, S)
        y_ready = [None] * T
        stats, mv, rs = A.take(H * NG, 6), A.take(H * NG, 2), A.take(H * NG)
        V.need(ready["v"])
        for i in range(H * NG):
            m = V.mark(nc.vector.bn_stats(stats[:, i, :], v[:, i // NG, (i % NG) * P:(i % NG + 1) * P]))
        V.need(m)
        for i in range(H * NG):
            m = V.mark(nc.vector.bn_aggr(mv[:, i, :], stats[:, i, :]))
        V.need(m)
        var = A.take(H * NG)
        c = V.mark(nc.vector.tensor_copy(var, mv[:, :, 1]))
        r = self.inverse_root(rs, var, 1.0, EPS_SECOND, c)
        V.need(r)
        for i in range(H * NG):
            part = v[:, i // NG, (i % NG) * P:(i % NG + 1) * P]
            m = V.mark(nc.vector.tensor_scalar(part, part, mv[:, i, 0:1], rs[:, i:i + 1], ALU.subtract, ALU.mult))
        v_ready = m
        fc = dst.rearrange("p t s -> p (t s)").rearrange("p (h n) -> p h n", h=H)
        for g in range(NG):
            bank = banks.take()
            self.pe.need(bank.free, ready["f"], tables)
            for half in range(H):
                last = nc.tensor.matmul(bank.ap[:, half * 2 * P:(half + 1) * 2 * P], fT[:, g, half * P:(half + 1) * P], dft_c,
                                        start=True, stop=True)
            done = self.pe.mark(last)
            m = self.copy(fc[:, :, g * 2 * P:(g + 1) * 2 * P], bank.ap.rearrange("p (a b) -> p a b", a=H), done)
            bank.free = [m]
            bank = banks.take()
            self.pe.need(bank.free, m)
            for n in range(4):
                half, cs = n // 2, n % 2
                c0 = g * 2 * P + cs * P
                last = nc.tensor.matmul(bank.ap[:, 0:S], fc[:, half, c0:c0 + P], dft_n[:, half, cs, :], start=(n == 0), stop=(n == 3))
            done = self.pe.mark(last)
            V.need(done, ready["fg"])
            y_ready[g] = V.mark(nc.vector.tensor_tensor(yT[:, g, :], bank.ap[:, 0:S], fgT[:, g, :], ALU.mult))
            bank.free = [y_ready[g]]
        for g in range(NG):
            bank = banks.take()
            self.pe.need(bank.free, v_ready, sguT_ready)
            for half in range(H):
                last = nc.tensor.matmul(bank.ap[:, half * P:(half + 1) * P], v[:, half, g * P:(g + 1) * P], sguT[:, g, :],
                                        start=True, stop=True)
            done = self.pe.mark(last)
            y = yT[:, NG + g, :]
            V.need(done, tables)
            m = V.mark(nc.vector.tensor_tensor(y.rearrange("p (h t) -> p h t", h=H), bank.ap[:, 0:S].rearrange("p (h t) -> p h t", h=H),
                                               sgu_b[:, g * P:(g + 1) * P].unsqueeze(1).to_broadcast([P, H, P]), ALU.add))
            bank.free = [m]
            V.need(m, ready["u"])
            m = V.mark(nc.vector.tensor_tensor(y, y, uT[:, g, :], ALU.mult))
            V.need(m, ready["sg"])
            y_ready[NG + g] = V.mark(nc.vector.tensor_tensor(y, y, sgT[:, g, :], ALU.mult))
        y = Parts(yT, None, y_ready)
        self.product_and_norm(A, y, weights, banks, combine, EPS_SECOND, rows_ready)

    def build(self):
        nc, d = self.nc, self.d
        self.setup()
        self.latT0 = self.sb("context_latents", [P, S])
        self.krT0 = self.sb("context_rotary_keys", [MR, S])
        self.state0 = self.sb("context_states", [P, 2, 2, GV])
        self.axial = self.sb("axial", [P, H, 2, MR // 2])
        self.small2_ready = self.load(self.g, [(self.axial, d["k_axial"])], "axial_loaded")
        work = self.side_work()

        def rest():
            next(work, None)

        room = self.MAIN + self.SIDE - 3 * D
        self.ada_room = [self.whole.ap[32 * i:32 * i + 2, room:] for i in range(DEPTH)]
        stages = [("attention", lambda: self.attention(rest)), ("moe0", lambda: self.experts(0, rest)), ("recurrent", self.recurrent),
                  ("moe1", lambda: self.experts(1, rest)), ("even", self.even), ("odd", self.odd)]
        for name, stage in stages:
            self.main.at = self.whole.at = self.tail.at = 0
            self.in_attention = name == "attention"
            if name == "moe0":
                for q in (self.pe, self.v, self.a, self.g):
                    q.need(self.rows_stored)
            if name == "recurrent":
                for _ in work:
                    pass
                self.meet()
            if name == "even":
                self.slots, self.lent_slots = self.slots[0:TAIL_SLOTS], self.slots[TAIL_SLOTS:]
                self.spare_slots = self.lent_slots[-2:]
            stage()
            self.meet()
        stored = self.new_sem("output_stored")
        for half in range(H):
            self.sp.need(self.x_ready[half])
            nc.sync.dma_start(self.out.rearrange("o (h p) d -> p (o h) d", p=P)[:, half, :], self.x[:, half, :]).then_inc(stored, 16)
        nc.sync.wait_ge(stored, 16 * H)


def build(nc, dram, out):
    with ExitStack() as ctx:
        prog = Program(nc, ctx, dram, out)
        prog.rows_dram = [nc.dram_tensor(f"ada_rows{i}", [2, 3 * D], F32, kind="Internal").ap() for i in range(DEPTH)]
        prog.build()


_INS = ['x', 'attn_w_qkv', 'attn_w_o', 'attn_sink', 'lru_w_in', 'lru_conv_w', 'lru_conv_b', 'lru_w_rgate', 'lru_b_rgate',
        'lru_w_igate', 'lru_b_igate', 'lru_lambda', 'lru_w_out', 'moe_w_router', 'moe_w_gate_up', 'moe_w_down', 'ln_mix_g',
        'ln_mix_b', 'ln_ffn_g', 'ln_ffn_b', 'c_2', 'ctx_2', 'c_ctx_2', 'ada_w_2', 'ada_b_2', 'post_ln_g_2', 'post_ln_b_2',
        'even_w_in_2', 'gla_w2_2', 'gla_b_2', 'gla_norm_g_2', 'mla_q_norm_g_2', 'mla_w_uq_2', 'mla_kv_norm_g_2', 'mla_w_ukv_2',
        'even_w_out_2', 'odd_w_in_2', 'sgu_w_2', 'sgu_b_2', 'odd_w_out_2']


def kernel(**inputs):
    import concourse.bacc as bacc
    from concourse.bass_utils import run_bass_kernel_spmd

    nc = bacc.Bacc("TRN2", target_bir_lowering=False, num_devices=1)
    arrays, dram = {}, {}
    for name, a in [(n, np.ascontiguousarray(inputs[n])) for n in _INS] + list(constants().items()):
        arrays[f"in_{name}"] = a
        dram[name] = nc.dram_tensor(f"in_{name}", a.shape, mybir.dt.from_np(a.dtype), kind="ExternalInput").ap()
    out = nc.dram_tensor("out_x", (1, S, D), F32, kind="ExternalOutput").ap()
    build(nc, dram, out)
    result = run_bass_kernel_spmd(nc, [arrays], core_ids=[0])
    return result.results[0]["out_x"]
```
